# Optimizing a Trainium2 kernel written in Bass

```python
import math
import jax, jax.numpy as jnp
from jax import lax
import numpy as np

D_MODEL = 1024
BATCH = 1
SEQ = 512
DEPTH = 1
DEC_BATCH = 8
DEC_SEQ = 1
PAST_LEN = 2048
PAGE_SIZE = 128

RET_HEADS = 4
RET_DK = 128
RET_DV = 128
RET_WIDTH = RET_HEADS * RET_DV
RET_CHUNK = 128
ROPE_BASE = 10000.0
DIFF_HEADS = 4
DIFF_DH = 64
DIFF_DV = 2 * DIFF_DH
DIFF_WIDTH = DIFF_HEADS * DIFF_DV
DIFF_SCALE = DIFF_DH ** -0.5
Q_BLOCK = 128
MIX_WIDTH = RET_WIDTH + DIFF_WIDTH
IN_SIZES = (RET_HEADS * RET_DK, RET_HEADS * RET_DK, RET_WIDTH, RET_WIDTH,
            DIFF_HEADS * 2 * DIFF_DH, DIFF_HEADS * 2 * DIFF_DH, DIFF_WIDTH)
IN_WIDTH = sum(IN_SIZES)
IN_SPLITS = tuple(int(v) for v in np.cumsum(IN_SIZES)[:-1])
N_BUCKETS = 32
MAX_DISTANCE = 128
MEM_LEN = 256
MEM_HEADS = 4
MEM_DH = D_MODEL // MEM_HEADS
PEER_HEADS = 8
N_KEYS = 128
N_EXPERTS = N_KEYS * N_KEYS
PEER_TOPK = 16
PEER_DQ = 256
PEER_DHALF = PEER_DQ // 2
PEER_BLOCK = 128
PEER_V_SCALE = 0.2

EPS = 1e-6
NEG_INF = -1e30

kernel_name = "hybrid_retention_diffattn_peer_step"

def rms_norm(x, g):
    xf = x.astype(jnp.float32)
    y = xf * lax.rsqrt(jnp.mean(xf * xf, axis=-1, keepdims=True) + EPS)
    return (y * g.astype(jnp.float32)).astype(x.dtype)

def head_norm(x):
    return x * lax.rsqrt(jnp.mean(x * x, axis=-1, keepdims=True) + EPS)

def rotary(x, pos):
    half = x.shape[-1] // 2
    inv = 1.0 / (ROPE_BASE ** (jnp.arange(half, dtype=jnp.float32) / half))
    ang = pos.astype(jnp.float32)[:, None] * inv[None, :]
    cos = jnp.cos(ang)[:, None, :]
    sin = jnp.sin(ang)[:, None, :]
    x1, x2 = x[..., :half], x[..., half:]
    return jnp.concatenate([x1 * cos - x2 * sin, x1 * sin + x2 * cos], axis=-1)

def t5_bias(rel, table):
    n = jnp.maximum(rel, 0)
    max_exact = N_BUCKETS // 2
    nf = jnp.maximum(n, 1).astype(jnp.float32)
    large = max_exact + (jnp.log(nf / max_exact) / math.log(MAX_DISTANCE / max_exact)
                         * (N_BUCKETS - max_exact)).astype(jnp.int32)
    large = jnp.minimum(large, N_BUCKETS - 1)
    bucket = jnp.where(n < max_exact, n, large)
    return jnp.moveaxis(table[bucket].astype(jnp.float32), -1, 0)

def token_mix_inputs(x, g_mix, w_in, pos):
    B, T, _ = x.shape
    xn = rms_norm(x, g_mix)
    proj = (xn @ w_in).astype(jnp.float32)
    rq, rk, rv, rg, dq, dk, dv = jnp.split(proj, IN_SPLITS, axis=-1)
    rq = rotary(rq.reshape(B, T, RET_HEADS, RET_DK), pos) * (RET_DK ** -0.5)
    rk = rotary(rk.reshape(B, T, RET_HEADS, RET_DK), pos)
    rv = rv.reshape(B, T, RET_HEADS, RET_DV)
    dq = dq.reshape(B, T, DIFF_HEADS, 2, DIFF_DH)
    dk = dk.reshape(B, T, DIFF_HEADS, 2, DIFF_DH)
    dv = dv.reshape(B, T, DIFF_HEADS, DIFF_DV)
    return rq, rk, rv, rg, dq, dk, dv

def retention_chunk(state, q, k, v, log_gamma):
    L = q.shape[1]
    n = jnp.arange(L, dtype=jnp.float32)
    diff = n[:, None] - n[None, :]
    decay = jnp.where(diff[None] >= 0,
                      jnp.exp(jnp.maximum(diff, 0.0)[None] * log_gamma[:, None, None]), 0.0)
    scores = jnp.einsum('bnhd,bmhd->bhnm', q, k) * decay[None]
    inner = jnp.einsum('bhnm,bmhe->bnhe', scores, v)
    q_decay = jnp.exp((n + 1.0)[:, None] * log_gamma[None, :])
    cross = jnp.einsum('bnhd,bhde->bnhe', q, state) * q_decay[None, :, :, None]
    k_decay = jnp.exp((L - 1.0 - n)[None, :] * log_gamma[:, None])
    new_state = (jnp.exp(L * log_gamma)[None, :, None, None] * state
                 + jnp.einsum('bmhd,hm,bmhe->bhde', k, k_decay, v))
    return inner + cross, new_state

def retention_prompt(rq, rk, rv, log_gamma):
    B, S = rq.shape[:2]
    nc = S // RET_CHUNK

    def to_chunks(t):
        return jnp.moveaxis(t.reshape(B, nc, RET_CHUNK, *t.shape[2:]), 1, 0)

    s0 = jnp.zeros((B, RET_HEADS, RET_DK, RET_DV), jnp.float32)

    def step(state, qkv):
        o, state = retention_chunk(state, qkv[0], qkv[1], qkv[2], log_gamma)
        return state, o

    s_fin, o = lax.scan(step, s0, (to_chunks(rq), to_chunks(rk), to_chunks(rv)))
    return jnp.moveaxis(o, 0, 1).reshape(B, S, RET_HEADS, RET_DV), s_fin

def diff_lambda(lq1, lk1, lq2, lk2, lam_init):
    f = jnp.float32
    return (jnp.exp(jnp.sum(lq1.astype(f) * lk1.astype(f)))
            - jnp.exp(jnp.sum(lq2.astype(f) * lk2.astype(f))) + lam_init)

def diff_weights(s, lam):
    p = jax.nn.softmax(s.astype(jnp.float32), axis=-1)
    return p[:, :, 0] - lam * p[:, :, 1]

def diff_attn_prompt(dq, dk, dv, lam, rel_bias):
    B, S = dq.shape[:2]
    nb = S // Q_BLOCK
    qb = jnp.moveaxis(dq.reshape(B, nb, Q_BLOCK, DIFF_HEADS, 2, DIFF_DH), 1, 0)
    kpos = jnp.arange(S)

    def block(args):
        i, q = args
        qpos = i * Q_BLOCK + jnp.arange(Q_BLOCK)
        rel = qpos[:, None] - kpos[None, :]
        s = jnp.einsum('bqhcd,bkhcd->bhcqk', q, dk) * DIFF_SCALE + t5_bias(rel, rel_bias)[:, None]
        s = jnp.where(rel >= 0, s, NEG_INF)
        w = diff_weights(s, lam)
        return jnp.einsum('bhqk,bkhe->bqhe', w, dv)

    o = lax.map(block, (jnp.arange(nb), qb))
    return jnp.moveaxis(o, 0, 1).reshape(B, S, DIFF_HEADS, DIFF_DV)

def diff_attn_sample(dq, dk, dv, k_past, v_past, lam, rel_bias):
    T = dq.shape[1]
    P = k_past.shape[1]
    qpos = P + jnp.arange(T)
    rel_past = qpos[:, None] - jnp.arange(P)[None, :]
    rel_new = qpos[:, None] - qpos[None, :]
    s_past = jnp.einsum('bqhcd,bkhcd->bhcqk', dq, k_past) * DIFF_SCALE + t5_bias(rel_past, rel_bias)[:, None]
    s_new = jnp.einsum('bqhcd,bkhcd->bhcqk', dq, dk) * DIFF_SCALE + t5_bias(rel_new, rel_bias)[:, None]
    s_new = jnp.where(rel_new >= 0, s_new, NEG_INF)
    w = diff_weights(jnp.concatenate([s_past, s_new], axis=-1), lam)
    return (jnp.einsum('bhqk,bkhe->bqhe', w[..., :P], v_past)
            + jnp.einsum('bhqk,bkhe->bqhe', w[..., P:], dv))

def mix_output(ro, rg, do, lam_init, w_out):
    B, T = ro.shape[:2]
    ret = head_norm(ro).reshape(B, T, RET_WIDTH) * jax.nn.silu(rg)
    dif = head_norm(do).reshape(B, T, DIFF_WIDTH) * (1.0 - lam_init)
    return jnp.concatenate([ret, dif], axis=-1).astype(w_out.dtype) @ w_out

def mem_kv(mem, g_mem, w_mk, w_mv):
    B, M, _ = mem.shape
    mn = rms_norm(mem, g_mem)
    return ((mn @ w_mk).reshape(B, M, MEM_HEADS, MEM_DH),
            (mn @ w_mv).reshape(B, M, MEM_HEADS, MEM_DH))

def cross_attend(x, g_cross, w_mq, w_mo, mk, mv):
    B, T, D = x.shape
    q = (rms_norm(x, g_cross) @ w_mq).reshape(B, T, MEM_HEADS, MEM_DH)
    s = jnp.einsum('bqhd,bkhd->bhqk', q, mk).astype(jnp.float32) * (MEM_DH ** -0.5)
    p = jax.nn.softmax(s, axis=-1)
    o = jnp.einsum('bhqk,bkhd->bqhd', p, mv.astype(jnp.float32)).reshape(B, T, D)
    return o.astype(w_mo.dtype) @ w_mo

def peer_rows(xb, w_pq, sub_keys, peer_u, peer_v):
    n = xb.shape[0]
    q = (xb @ w_pq).astype(jnp.float32).reshape(n, PEER_HEADS, 2, PEER_DHALF)
    s = jnp.einsum('nhcd,hckd->nhck', q, sub_keys.astype(jnp.float32))
    top_s, top_i = lax.top_k(s, PEER_TOPK)
    cand_s = (top_s[:, :, 0, :, None] + top_s[:, :, 1, None, :]).reshape(n, PEER_HEADS, PEER_TOPK * PEER_TOPK)
    cand_i = (top_i[:, :, 0, :, None] * N_KEYS + top_i[:, :, 1, None, :]).reshape(n, PEER_HEADS, PEER_TOPK * PEER_TOPK)
    best_s, best_pos = lax.top_k(cand_s, PEER_TOPK)
    idx = jnp.take_along_axis(cand_i, best_pos, axis=-1)
    g = jax.nn.softmax(best_s, axis=-1)
    u = peer_u[idx]
    a = jax.nn.gelu(jnp.einsum('nd,nhkd->nhk', xb, u).astype(jnp.float32), approximate=False)
    v = peer_v[idx]
    return jnp.einsum('nhk,nhkd->nd', g * a, v.astype(jnp.float32)).astype(xb.dtype)

def peer_ffn(xn, w_pq, sub_keys, peer_u, peer_v):
    B, T, D = xn.shape
    n = B * T
    flat = xn.reshape(n, D)
    if n % PEER_BLOCK == 0 and n > PEER_BLOCK:
        out = lax.map(lambda xb: peer_rows(xb, w_pq, sub_keys, peer_u, peer_v),
                      flat.reshape(n // PEER_BLOCK, PEER_BLOCK, D)).reshape(n, D)
    else:
        out = peer_rows(flat, w_pq, sub_keys, peer_u, peer_v)
    return out.reshape(B, T, D)

def setup_inputs(seed: int = 0) -> dict:
    key = jax.random.key(seed)
    ks = jax.random.split(key, 32)
    f32 = jnp.float32
    n_pages = PAST_LEN // PAGE_SIZE
    n_used = DEC_BATCH * n_pages
    p_total = n_used + n_used // 4

    def nrm(k, shape, scale):
        return jax.random.normal(k, shape, f32) * scale

    def gain(k, shape):
        return 1.0 + 0.05 * jax.random.normal(k, shape, f32)

    page_table = jax.random.permutation(ks[5], p_total)[:n_used].reshape(DEC_BATCH, n_pages).astype(jnp.int32)
    return {
        "x_prompt": nrm(ks[0], (BATCH, SEQ, D_MODEL), 1.0),
        "x_sample": nrm(ks[1], (DEC_BATCH, DEC_SEQ, D_MODEL), 1.0),
        "mem_prompt": nrm(ks[2], (BATCH, MEM_LEN, D_MODEL), 1.0),
        "cache_diff_k": nrm(ks[3], (DEPTH, p_total, PAGE_SIZE, DIFF_HEADS, 2, DIFF_DH), 1.0),
        "cache_diff_v": nrm(ks[4], (DEPTH, p_total, PAGE_SIZE, DIFF_HEADS, DIFF_DV), 1.0),
        "page_table": page_table,
        "state_ret": nrm(ks[6], (DEPTH, DEC_BATCH, RET_HEADS, RET_DK, RET_DV), 1.0),
        "cache_mem_k": nrm(ks[7], (DEPTH, DEC_BATCH, MEM_LEN, MEM_HEADS, MEM_DH), 1.0),
        "cache_mem_v": nrm(ks[8], (DEPTH, DEC_BATCH, MEM_LEN, MEM_HEADS, MEM_DH), 1.0),
        "g_mix": gain(ks[9], (DEPTH, D_MODEL)),
        "w_in": nrm(ks[10], (DEPTH, D_MODEL, IN_WIDTH), D_MODEL ** -0.5),
        "w_out": nrm(ks[11], (DEPTH, MIX_WIDTH, D_MODEL), MIX_WIDTH ** -0.5),
        "lam_q1": nrm(ks[12], (DEPTH, DIFF_DH), 0.1),
        "lam_k1": nrm(ks[13], (DEPTH, DIFF_DH), 0.1),
        "lam_q2": nrm(ks[14], (DEPTH, DIFF_DH), 0.1),
        "lam_k2": nrm(ks[15], (DEPTH, DIFF_DH), 0.1),
        "rel_bias": nrm(ks[16], (N_BUCKETS, DIFF_HEADS), 0.5),
        "g_cross": gain(ks[17], (DEPTH, D_MODEL)),
        "g_mem": gain(ks[18], (DEPTH, D_MODEL)),
        "w_mq": nrm(ks[19], (DEPTH, D_MODEL, D_MODEL), D_MODEL ** -0.5),
        "w_mk": nrm(ks[20], (DEPTH, D_MODEL, D_MODEL), D_MODEL ** -0.5),
        "w_mv": nrm(ks[21], (DEPTH, D_MODEL, D_MODEL), D_MODEL ** -0.5),
        "w_mo": nrm(ks[22], (DEPTH, D_MODEL, D_MODEL), D_MODEL ** -0.5),
        "g_ffn": gain(ks[23], (DEPTH, D_MODEL)),
        "w_pq": nrm(ks[24], (DEPTH, D_MODEL, PEER_HEADS * PEER_DQ), D_MODEL ** -0.5),
        "sub_keys": nrm(ks[25], (DEPTH, PEER_HEADS, 2, N_KEYS, PEER_DHALF), PEER_DHALF ** -0.5),
        "peer_u": nrm(ks[26], (DEPTH, N_EXPERTS, D_MODEL), D_MODEL ** -0.5),
        "peer_v": nrm(ks[27], (DEPTH, N_EXPERTS, D_MODEL), PEER_V_SCALE),
        "g_final": gain(ks[28], (D_MODEL,)),
    }

def reference(x_prompt, x_sample, mem_prompt, cache_diff_k, cache_diff_v, page_table, state_ret,
              cache_mem_k, cache_mem_v, g_mix, w_in, w_out, lam_q1, lam_k1, lam_q2, lam_k2, rel_bias,
              g_cross, g_mem, w_mq, w_mk, w_mv, w_mo, g_ffn, w_pq, sub_keys, peer_u, peer_v, g_final):
    n_pages = page_table.shape[1]
    past = n_pages * PAGE_SIZE
    db, t_s = x_sample.shape[:2]
    log_gamma = jnp.log(1.0 - 2.0 ** (-5.0 - jnp.arange(RET_HEADS, dtype=jnp.float32)))
    pos_p = jnp.arange(x_prompt.shape[1])
    pos_s = past + jnp.arange(t_s)

    hp, hs = x_prompt, x_sample
    k_p_list, v_p_list, ret_p_list, mk_p_list, mv_p_list = [], [], [], [], []
    k_s_list, v_s_list, ret_s_list = [], [], []
    for l in range(DEPTH):
        lam_init = 0.8 - 0.6 * math.exp(-0.3 * l)
        lam = diff_lambda(lam_q1[l], lam_k1[l], lam_q2[l], lam_k2[l], lam_init)

        rq, rk, rv, rg, dq, dk, dv = token_mix_inputs(hp, g_mix[l], w_in[l], pos_p)
        ro, ret_state_p = retention_prompt(rq, rk, rv, log_gamma)
        do = diff_attn_prompt(dq, dk, dv, lam, rel_bias)
        hp = hp + mix_output(ro, rg, do, lam_init, w_out[l]).astype(hp.dtype)
        mk, mv = mem_kv(mem_prompt, g_mem[l], w_mk[l], w_mv[l])
        hp = hp + cross_attend(hp, g_cross[l], w_mq[l], w_mo[l], mk, mv).astype(hp.dtype)
        hp = hp + peer_ffn(rms_norm(hp, g_ffn[l]), w_pq[l], sub_keys[l], peer_u[l], peer_v[l]).astype(hp.dtype)
        k_p_list.append(dk.astype(cache_diff_k.dtype))
        v_p_list.append(dv.astype(cache_diff_v.dtype))
        ret_p_list.append(ret_state_p.astype(state_ret.dtype))
        mk_p_list.append(mk.astype(cache_mem_k.dtype))
        mv_p_list.append(mv.astype(cache_mem_v.dtype))

        rq, rk, rv, rg, dq, dk, dv = token_mix_inputs(hs, g_mix[l], w_in[l], pos_s)
        ro_s, ret_state_s = retention_chunk(state_ret[l].astype(jnp.float32), rq, rk, rv, log_gamma)
        k_past = cache_diff_k[l][page_table].reshape(db, past, DIFF_HEADS, 2, DIFF_DH)
        v_past = cache_diff_v[l][page_table].reshape(db, past, DIFF_HEADS, DIFF_DV)
        do_s = diff_attn_sample(dq, dk, dv, k_past, v_past, lam, rel_bias)
        hs = hs + mix_output(ro_s, rg, do_s, lam_init, w_out[l]).astype(hs.dtype)
        hs = hs + cross_attend(hs, g_cross[l], w_mq[l], w_mo[l], cache_mem_k[l], cache_mem_v[l]).astype(hs.dtype)
        hs = hs + peer_ffn(rms_norm(hs, g_ffn[l]), w_pq[l], sub_keys[l], peer_u[l], peer_v[l]).astype(hs.dtype)
        k_s_list.append(dk.astype(cache_diff_k.dtype))
        v_s_list.append(dv.astype(cache_diff_v.dtype))
        ret_s_list.append(ret_state_s.astype(state_ret.dtype))

    y_prompt = rms_norm(hp, g_final)
    y_sample = rms_norm(hs, g_final)
    new_diff_k_prompt = jnp.stack(k_p_list)
    new_diff_v_prompt = jnp.stack(v_p_list)
    state_ret_prompt = jnp.stack(ret_p_list)
    mem_k_prompt = jnp.stack(mk_p_list)
    mem_v_prompt = jnp.stack(mv_p_list)
    new_diff_k_sample = jnp.stack(k_s_list)
    new_diff_v_sample = jnp.stack(v_s_list)
    state_ret_sample = jnp.stack(ret_s_list)
    return (y_prompt, y_sample, new_diff_k_prompt, new_diff_v_prompt, state_ret_prompt,
            mem_k_prompt, mem_v_prompt, new_diff_k_sample, new_diff_v_sample, state_ret_sample)


_drawn_inputs = setup_inputs


def setup_inputs(seed=0):
    import zlib

    import numpy as np

    out = dict(_drawn_inputs(seed))
    spreads = {}
    factors = {'lam_q2': 7.093, 'g_cross': 6.534, 'g_ffn': 2.892}
    for name, (base, spread) in spreads.items():
        noise = np.random.default_rng([zlib.crc32(name.encode()), seed]).standard_normal(out[name].shape)
        drawn = base * np.exp(spread * noise) if base else spread * noise
        out[name] = __import__('jax').numpy.asarray(drawn.astype(out[name].dtype))
    for name, factor in factors.items():
        out[name] = (out[name] * factor).astype(out[name].dtype)
    return out
```

```python
from contextlib import ExitStack
import math

import numpy as np
import concourse.bass as bass
from concourse import mybir

F32 = mybir.dt.float32
U32 = mybir.dt.uint32
I32 = mybir.dt.int32
ALU = mybir.AluOpType
ACT = mybir.ActivationFunctionType
AX = mybir.AxisListType

P = 128
D = 1024
KD = D // P
SEQ = 512
NBLK = SEQ // P
DB = 8
NB = NBLK + 1
SMP = NBLK
ROWS = [P] * NBLK + [DB]
TOK = SEQ + DB
MEM = 256
NMEM = MEM // P
H = 4
HC = 2 * H
DH = 64
MDH = D // H
PAGES = 16
PAGE = 128
PAST = PAGES * PAGE
PPG = 4
GRP = PAGES // PPG
TPR = PAGE // 32
NBUCKET = 32
EPS = 1e-6
NEG = -1e30
LAM_INIT = 0.8 - 0.6 * math.exp(-0.0)
SCALE = DH ** -0.5
MSCALE = MDH ** -0.5
PH = 8
NSUB = 2 * PH
NK = 128
TOPK = 16
NSEL = PH * TOPK
NEXP = NK * NK
CHUNK = 8

TL = 640
PIECES = [("ident", 128), ("ones", 128), ("zeros", 128), ("rot", NB * 256), ("decayT", H * P), ("qdec", H * P),
          ("kdec", H), ("gL", H), ("gam", H), ("sel", DB * P), ("mask8", DB * DB), ("hmask", 512),
          ("hmask4", D), ("line", TL), ("past", 6 * P), ("even", 1), ("odd", 1), ("dmask", DB * DB),
          ("part32", 1), ("iota16", TOPK)]
CO = {}
_o = 0
for _n, _w in PIECES:
    CO[_n] = (_o, _w)
    _o += _w
CW = _o


def shape_constants():
    c = np.zeros((P, CW), np.float32)

    def put(name, value, rows=P):
        o, w = CO[name]
        c[:rows, o:o + w] = np.asarray(value, np.float32).reshape(-1, w)

    p = np.arange(P)
    put("ident", np.eye(P))
    put("ones", np.ones((P, P)))
    half = P // 2
    inv = (np.float32(1.0) / (np.float32(10000.0) ** (np.arange(half, dtype=np.float32) / np.float32(half)))).astype(np.float32)
    rot = np.zeros((P, NB, 4, half), np.float32)
    for b in range(NB):
        pos = np.float32(PAST) * np.ones(P, np.float32) if b == SMP else (b * P + p).astype(np.float32)
        ang = (pos[:, None] * inv[None, :]).astype(np.float32).astype(np.float64)
        rot[:, b, 0] = np.cos(ang) * P ** -0.5
        rot[:, b, 1] = np.sin(ang) * P ** -0.5
        rot[:, b, 2] = np.cos(ang)
        rot[:, b, 3] = np.sin(ang)
    put("rot", rot)
    lg = np.log(1.0 - 2.0 ** (-5.0 - np.arange(H)))
    dif = p[None, :] - p[:, None]
    dec = np.where(dif[:, None, :] >= 0, np.exp(np.maximum(dif, 0)[:, None, :] * lg[None, :, None]), 0.0)
    put("decayT", dec)
    put("qdec", np.broadcast_to(np.exp((p[None, :] + 1.0) * lg[:, None])[None], (P, H, P)))
    put("kdec", np.exp((P - 1.0 - p)[:, None] * lg[None, :]))
    put("gL", np.broadcast_to(np.exp(P * lg)[None], (P, H)))
    put("gam", np.broadcast_to(np.exp(lg)[None], (P, H)))
    sel = np.zeros((DB, DB, P))
    for b in range(DB):
        sel[b, b] = 1.0
    put("sel", sel, DB)
    put("mask8", np.broadcast_to(np.eye(DB)[None], (P, DB, DB)))
    dm = np.zeros((DB, DB, DB))
    for b in range(DB):
        dm[b, b] = 1.0
    put("dmask", dm, DB)
    hc = np.arange(HC)
    put("hmask", hc[:, None] // 2 == np.arange(512)[None, :] // P, HC)
    put("hmask4", np.arange(H)[:, None] == np.arange(D)[None, :] // MDH, H)

    def bucket(n):
        n = np.maximum(n, 0)
        me = NBUCKET // 2
        nf = np.maximum(n, 1).astype(np.float32)
        large = me + (np.log(nf / np.float32(me)) / np.float32(math.log(128 / me)) * np.float32(NBUCKET - me)).astype(np.int32)
        return np.where(n < me, n, np.minimum(large, NBUCKET - 1))

    rel = SEQ - 1 - np.arange(TL)
    line = np.zeros((NBUCKET + 1, TL))
    for m in range(TL):
        line[bucket(rel[m:m + 1])[0] if rel[m] >= 0 else NBUCKET, m] = 1.0
    put("line", line, NBUCKET + 1)
    past = np.zeros((NBUCKET, 6, P))
    for j in range(TPR):
        pos = ((GRP - 1) * PPG + p // 32) * PAGE + (p % 32) * TPR + j
        past[bucket(PAST - pos), j, p] = 1.0
    past[NBUCKET - 1, 4] = 1.0
    past[0, 5] = 1.0
    put("past", past, NBUCKET)
    put("even", hc % 2 == 0, HC)
    put("odd", hc % 2 == 1, HC)
    put("part32", p % 32)
    put("iota16", np.broadcast_to(np.arange(TOPK)[None], (P, TOPK)))
    return c


LAYOUT = [("const", 6912), ("misc", 1024), ("dvs", 512), ("xt", 8 * 776), ("w", 2 * 4096), ("r1", 5120), ("r2", 7680),
          ("r3", 2560), ("ring", 3 * 2048), ("s", 1104), ("toe", 2048), ("g", 1024), ("t", 4096)]
BASE = {}
_o = 0
for _n, _w in LAYOUT:
    BASE[_n] = _o
    _o += _w
SBW = _o
RING = 3
PSUM_TURN, PSUM_JOB = 0, 4

WTILES = ([("w_mk", 512 * i, "mem") for i in range(2)] + [("w_mv", 512 * i, "mem") for i in range(2)]
          + [("w_in", 512 * c, k) for c, k in ((4, "dq"), (5, "dk"), (6, "dv"), (0, "rq"), (1, "rk"), (2, "rv"), (3, "rg"))]
          + [("w_out", 512 * i, "mix") for i in range(2)] + [("w_mq", 512 * i, "mq") for i in range(2)]
          + [("w_mo", 512 * i, "mo") for i in range(2)] + [("w_pq", 512 * i, "pq") for i in range(4)])
JOBS = [(t, u) for t, (_, _, k) in enumerate(WTILES) if k != "pq" for u in range(NMEM if k == "mem" else NB)]
PQ0 = len(WTILES) - 4
BY_DVE = ("rq", "rk", "mix", "mo")


def job_kind(j):
    return WTILES[JOBS[j][0]][2]


def first_job(kind):
    return next(j for j in range(len(JOBS)) if job_kind(j) == kind)


def taken_by(j):
    dve = job_kind(j) in BY_DVE
    return dve, sum((job_kind(i) in BY_DVE) == dve for i in range(j + 1))


TILES = ([("k", b, g) for b in range(DB) for g in range(GRP)] + [("st", b, 0) for b in range(DB)]
         + [("v", b, g) for b in range(DB) for g in range(GRP)] + [("mk", b, 0) for b in range(DB)]
         + [("mv", b, 0) for b in range(DB)])
TILE_BY_DVE = ("k", "mk")


def tile_no(kind, b, g=0):
    return TILES.index((kind, b, g))


def tile_used(n):
    dve = TILES[n][0] in TILE_BY_DVE
    return dve, sum((TILES[i][0] in TILE_BY_DVE) == dve for i in range(n + 1))


SEMS = """const_loaded small_loaded mem_loaded x_loaded gains_loaded w_loaded0 w_loaded1 tile_in0 tile_in1 tile_in2
        tile_used_dve tile_used_pe ss_cleared sumsq_done inv_done rstd_done xn_ready turned xt_done job_ready
        job_taken_dve job_taken_act vstep astep mem_stored0 mem_stored1 mem_stored2 mem_stored3 new_kv_stored
        lam_sums lam_exp lam_ready line_cols line_ps line_row line_stored toe_loaded past_ps past_ready kvidx_ready
        rows_turned rowsT_done scores_ready sc_biased nmax_ready exp_done w_ready wmat_turned wT_ready av_done
        dif_taken srow_saved qb_ready s_scored colmax_ready colmax_turned maxdiag_ready maxbc_ready sarg_ready
        sexp_done esum_ready z_ready coef_ready pv_done om_ready dif_row_ready rqd_ready ret_scores ret_sc_ready
        ret_out ret_state ret_rows rqm_ready kexp_ready outer_ready ns_ready ns_stored0 ns_stored1 ns_stored2
        state_stored hsq_ready hrstd_done mix_ready x_again done_stored final_ready mkr_loaded mkr_turned mkT_done
        mv_loaded cs_ready cmax_ready cexp_done ce_turned ceT_ready co_ready co_taken cqb_ready cs_scored
        ccolmax_ready ccolmax_turned cmaxdiag_ready cmaxbc_ready csexp_done cesum_ready cz_ready ccoef_ready
        cpv_done com_ready crow_ready sk_loaded sk_turned skT_done rqp_ready rqp_taken rs_ready rs_taken sel_ready
        sidx_turned xb_ready gelu_done weight_ready diag_ready y_ready u_in0 u_in1 u_in2 u_in3 u_in4 u_in5 u_in6
        u_in7 v_in0 v_in1 v_in2 v_in3 v_in4 v_in5 v_in6 v_in7 u_used v_used idx_copied smp_w""".split()


def build(nc, x_prompt, x_sample, mem_prompt, cache_diff_k, cache_diff_v, page_table, state_ret, cache_mem_k,
          cache_mem_v, g_mix, w_in, w_out, lam_q1, lam_k1, lam_q2, lam_k2, rel_bias, g_cross, g_mem, w_mq, w_mk,
          w_mv, w_mo, g_ffn, w_pq, sub_keys, peer_u, peer_v, g_final, consts, line_dram,
          y_prompt, y_sample, new_k_p, new_v_p, state_p, mk_p, mv_p, new_k_s, new_v_s, state_s):
    weights = {"w_mk": w_mk, "w_mv": w_mv, "w_in": w_in, "w_out": w_out, "w_mq": w_mq, "w_mo": w_mo, "w_pq": w_pq}
    with ExitStack() as ctx:
        A = ctx.enter_context(nc.sbuf_tensor("arena", [P, SBW], F32))
        PS = ctx.enter_context(nc.psum_tensor("ps", [P, 8, 512], F32))
        s = {n: ctx.enter_context(nc.semaphore(n)) for n in SEMS}

        def at(region, off, n):
            return A[:, BASE[region] + off:BASE[region] + off + n]

        def const(name):
            return at("const", CO[name][0], CO[name][1])

        small_used = [0]

        def small(n):
            small_used[0] += n
            assert small_used[0] <= 1024
            return at("misc", small_used[0] - n, n)

        ident, ones, zeros = const("ident"), const("ones"), const("zeros")
        rot = const("rot").rearrange("p (b t d) -> p b t d", b=NB, t=4)
        sel = const("sel").rearrange("p (b m) -> p b m", b=DB)
        mask8 = const("mask8").rearrange("p (b j) -> p b j", b=DB)
        dmask = const("dmask").rearrange("p (b j) -> p b j", b=DB)

        XT = at("xt", 0, 8 * 776).rearrange("p (k t) -> p k t", k=KD)
        W = [at("w", 4096 * i, 4096).rearrange("p (k n) -> p k n", k=KD) for i in range(2)]
        G = at("g", 0, 1024)
        GM = at("t", 0, 1024)
        XN = [at("t", 2048 + 1024 * i, 1024) for i in range(2)]
        X0 = at("r1", 0, 7 * 1024).rearrange("p (u d) -> p u d", u=7)
        DQT = at("r1", 0, H * TOK).rearrange("p (h t) -> p h t", h=H)
        DKT = at("r1", 2560, H * TOK).rearrange("p (h t) -> p h t", h=H)
        HR = at("r1", 0, NB * D).rearrange("p (b d) -> p b d", b=NB)
        DV = at("r2", 0, 2560).rearrange("p (b d) -> p b d", b=NB)
        RK = at("r2", 2560, 2560).rearrange("p (b d) -> p b d", b=NB)
        RG = at("r2", 5120, 2560).rearrange("p (b d) -> p b d", b=NB)
        QR = at("r2", 0, NB * D).rearrange("p (b d) -> p b d", b=NB)
        DIF = at("r3", 0, 2560).rearrange("p (b d) -> p b d", b=NB)
        MSTAGE = [at("r3", 512 * i, 512) for i in range(4)]
        SLOT = [at("ring", 2048 * i, 2048) for i in range(RING)]
        S = at("s", 0, 1024)
        TOE = at("toe", 0, 2048).rearrange("p (h c) -> p h c", h=H)
        DVS = at("dvs", 0, 512)
        SRQ, SRK = at("g", 0, 512), at("g", 512, 512)
        SC = [at("t", 1024 * i, 1024).rearrange("p (c n) -> p c n", c=2) for i in range(2)]
        WM = [at("t", 2048 + 512 * i, 512) for i in range(2)]
        WT = [at("t", 3072 + 512 * i, 512) for i in range(2)]
        RQD, RKD = at("t", 0, 512), at("t", 512, 512)
        RSC = at("t", 1024, 512)
        STATE = at("t", 1536, 512)
        ROT_A, ROT_B = at("t", 2048, 512), at("t", 2560, 512)
        KEXP = [at("t", 2048 + 512 * i, 512) for i in range(2)]
        RQM = at("t", 3072, H * DB * DB).rearrange("p (h b j) -> p h b j", h=H, b=DB)
        OM = [at("t", 3072 + 512 * i, 512) for i in range(2)]
        SQ = [at("t", 2048 * i, 2048) for i in range(2)]

        ss = [small(8) for _ in range(4)]
        rstd = [small(8) for _ in range(4)]
        lamv = small(256)
        lsum, lexp, nlam = small(2), small(2), small(1)
        tab = small(H)
        pt_f, kv_idx = small(32), small(32)
        nmx, zsum = small(4), small(4)
        bias_s = small(24).rearrange("p (j h) -> p j h", j=6)
        sself, sself_e = small(HC), small(DB * HC).rearrange("p (b c) -> p b c", b=DB)
        sself_m = small(DB * HC).rearrange("p (b c) -> p b c", b=DB)
        colmax, mcol = small(64), small(1)
        esum = small(DB * HC).rearrange("p (b c) -> p b c", b=DB)
        rz, coef = small(DB), small(1)
        cl = small(DB * DB).rearrange("p (b j) -> p b j", b=DB)
        hss = small(NB * 8).rearrange("p (b h) -> p b h", b=NB)
        mdiag = small(64)
        TABB = at("t", 1024, 512).rearrange("p (h m) -> p h m", h=H)
        PTAB = at("t", 1536, DB * PAGES)
        LROW = at("ring", 0, H * TL).rearrange("p (h c) -> p h c", h=H)
        BFULL = at("t", 1536, 128).rearrange("p (x c) -> p x c", x=16)

        k_rows = cache_diff_k.rearrange("l g (r t) h c d -> (l g r) (t h c d)", t=TPR)
        v_rows = cache_diff_v.rearrange("l g (r t) h d -> (l g r) (t h d)", t=TPR)
        mk_rows = cache_mem_k.rearrange("l b (p t) h d -> (l b) p (t h d)", t=NMEM)
        mv_rows = cache_mem_v.rearrange("l b (p t) h d -> (l b) p (t h d)", t=NMEM)
        mem_out = {"w_mk": mk_p.rearrange("l b (u p) h d -> (l b u) p (h d)", p=P),
                   "w_mv": mv_p.rearrange("l b (u p) h d -> (l b u) p (h d)", p=P)}
        kp_out = new_k_p.rearrange("l b (u p) h c d -> (l b u) p (h c d)", p=P)
        vp_out = new_v_p.rearrange("l b (u p) h d -> (l b u) p (h d)", p=P)
        ks_out = new_k_s.rearrange("l b t h c d -> (l b t) (h c d)")
        vs_out = new_v_s.rearrange("l b t h d -> (l b t) (h d)")
        xp = x_prompt.rearrange("b (u p) d -> (b u) p d", p=P)
        yp = y_prompt.rearrange("b (u p) d -> (b u) p d", p=P)
        line_rows = line_dram[0:H * P * TL].rearrange("(h p c) -> p h c", h=H, p=P)

        TURN = 7
        N_MIX, N_CROSS, N_Q, N_O, N_FFN, N_END = (TURN + NB * i for i in range(6))

        def turn_banks(n):
            return PS[:, 2 * (n % 2):2 * (n % 2) + 2, :].rearrange("p a c -> p (a c)")

        def w_arrived(eng, t):
            eng.wait_ge((s["w_loaded0"], s["w_loaded1"])[t % 2], 16 * (t // 2 + 1))

        tile_in = (s["tile_in0"], s["tile_in1"], s["tile_in2"])
        mem_stored = (s["mem_stored0"], s["mem_stored1"], s["mem_stored2"], s["mem_stored3"])
        ns_stored = (s["ns_stored0"], s["ns_stored1"], s["ns_stored2"])

        def tile_arrived(eng, n):
            eng.wait_ge(tile_in[n % RING], 16 * (n // RING + 1))

        NSTORES = 2 * NB

        MKR = at("t", 0, 2048).rearrange("p (m d) -> p m d", m=NMEM)
        MKT = at("toe", 0, 2048).rearrange("p (k m) -> p k m", k=KD)
        MV = at("r3", 0, 2048).rearrange("p (m d) -> p m d", m=NMEM)
        CE = [at("t", 1024 * i, 1024).rearrange("p (h m) -> p h m", h=H) for i in range(2)]
        CET = [at("t", 2048 + 1024 * i, 1024) for i in range(2)]
        COM = [at("t", 1024 * i, 1024) for i in range(2)]
        CS = at("s", 0, DB * NMEM * H)
        CS4 = CS.rearrange("p (b j h) -> p b j h", b=DB, j=NMEM)
        cneg, csum = small(2 * H), small(2 * H)
        ccol, cesum = at("s", 128, DB * H), at("s", 160, DB * H)
        cmd = at("s", 192, DB * H)
        cmx = at("s", 224, 1)
        crz = at("s", 232, DB)
        ccl = at("s", 240, DB * DB).rearrange("p (b j) -> p b j", b=DB)
        SKR = at("t", 0, 2048).rearrange("p (x d) -> p x d", x=NSUB)
        SKT = at("toe", 0, 2048).rearrange("p (x k) -> p x k", x=NSUB)
        QPT = [at("t", 2048 + TOK * i, TOK) for i in range(2)]
        WORK = at("t", 3200, NB * NK).rearrange("p (b k) -> p b k", b=NB)
        TV = at("ring", 0, NB * NSUB * TOPK).rearrange("p (b x k) -> p b x k", b=NB, x=NSUB)
        TI = at("ring", 1280, NB * NSUB * TOPK).rearrange("p (b x k) -> p b x k", b=NB, x=NSUB)
        CAND = at("w", 0, 2048)
        CAND2 = at("w", 2048, 2048)
        HOT = at("w", 4096, 2048)
        BV, BI = at("w", 6144, NSEL), at("w", 6272, NSEL)
        TIF = at("w", 6400, NSUB * TOPK)
        AF, CF = at("w", 6656, NSEL), at("w", 6784, NSEL)
        AU, CU = at("w", 6912, NSEL), at("w", 7040, NSEL)
        GA, GC = at("w", 7168, NSEL), at("w", 7296, NSEL)
        bsum = at("w", 7424, PH)
        IDX = at("r3", 0, NB * NSEL).rearrange("p (b k) -> p b k", b=NB)
        GATE = at("r3", 640, NB * NSEL).rearrange("p (b k) -> p b k", b=NB)
        SIDXF, SIDX, SGATE = at("r3", 1280, DB), at("r3", 1288, DB), at("r3", 1296, DB)
        sdot, sgl = at("r3", 1304, DB), at("r3", 1312, DB)
        SWM = at("r3", 1320, DB * DB).rearrange("p (b j) -> p b j", b=DB)
        dots, gl, WCH = at("r3", 1384, CHUNK), at("r3", 1392, CHUNK), at("r3", 1400, CHUNK)
        sidx_row = at("r3", 1408, NSEL)
        ICH = [at("r3", 1536 + CHUNK * i, CHUNK) for i in range(2)]
        USLOT = [at("xt", 1024 * i, 1024) for i in range(CHUNK)]
        VSLOT = [at("ring", 1024 * i, 1024) for i in range(CHUNK)]
        DIAG = [at("t", 128 * i, 128) for i in range(CHUNK)]
        uv_in = ((s["u_in0"], s["u_in1"], s["u_in2"], s["u_in3"], s["u_in4"], s["u_in5"], s["u_in6"], s["u_in7"]),
                 (s["v_in0"], s["v_in1"], s["v_in2"], s["v_in3"], s["v_in4"], s["v_in5"], s["v_in6"], s["v_in7"]))
        NCH = NSEL // CHUNK

        block = ctx.enter_context(nc.Block())

        @block.sync
        def _(sp):
            sp.dma_start(at("const", 0, CW), consts).then_inc(s["const_loaded"], 16)
            m = mem_prompt.rearrange("b (u p) d -> p (b u) d", p=P)
            sp.dma_start(X0[:, 0:NMEM, :], m).then_inc(s["mem_loaded"], 16)
            sp.dma_start(GM, g_mem[0].partition_broadcast(P)).then_inc(s["mem_loaded"], 16)
            sp.dma_start(X0[:, NMEM:NMEM + NBLK, :], x_prompt.rearrange("b (u p) d -> p (b u) d", p=P)).then_inc(s["x_loaded"], 16)
            sp.dma_start(X0[0:DB, NMEM + SMP, :], x_sample.rearrange("b t d -> (b t) d")).then_inc(s["x_loaded"], 16)
            sp.dma_start(G, g_mix[0].partition_broadcast(P)).then_inc(s["gains_loaded"], 16)
            for i, v in enumerate((lam_q1, lam_k1, lam_q2, lam_k2)):
                sp.dma_start(lamv[:, 64 * i:64 * i + 64], v[0].partition_broadcast(P)).then_inc(s["small_loaded"], 16)
            sp.dma_start(tab[0:NBUCKET, :], rel_bias).then_inc(s["small_loaded"], 16)
            sp.dma_start(PTAB.bitcast(I32), page_table.rearrange("b g -> (b g)").partition_broadcast(P)
                         ).then_inc(s["small_loaded"], 16)
            for t, (name, c0, kind) in enumerate(WTILES):
                if t == 13:
                    sp.wait_ge(s["hsq_ready"], 1)
                    sp.wait_ge(s["state_stored"], 16)
                    sp.dma_start(HR[:, 0:NBLK, :], x_prompt.rearrange("b (u p) d -> p (b u) d", p=P)).then_inc(s["x_again"], 16)
                    sp.dma_start(HR[0:DB, SMP, :], x_sample.rearrange("b t d -> (b t) d")).then_inc(s["x_again"], 16)
                    sp.dma_start(G, g_cross[0].partition_broadcast(P)).then_inc(s["gains_loaded"], 16)
                    for i in range(4):
                        sp.wait_ge(mem_stored[i], 32)
                    sp.dma_start(MKR, mk_p.rearrange("l b (u p) h d -> p (l b u) (h d)", p=P)).then_inc(s["mkr_loaded"], 16)
                    sp.wait_ge(s["turned"], N_CROSS)
                    sp.dma_start(MV, mv_p.rearrange("l b (u p) h d -> p (l b u) (h d)", p=P)).then_inc(s["mv_loaded"], 16)
                if t == 15:
                    sp.wait_ge(s["xn_ready"], TURN + NB)
                    sp.dma_start(G, g_ffn[0].partition_broadcast(P)).then_inc(s["gains_loaded"], 16)
                if t == 18:
                    sp.wait_ge(s["crow_ready"], DB + 1)
                    sp.dma_start(SKR, sub_keys[0].rearrange("h c k d -> k (h c) d")).then_inc(s["sk_loaded"], 16)
                if t >= 2:
                    last_job = max(j for j in range(len(JOBS)) if JOBS[j][0] <= t - 2) if t - 2 < PQ0 else 0
                    if t - 2 < PQ0:
                        sp.wait_ge(s["job_ready"], last_job + 1)
                    else:
                        sp.wait_ge(s["rqp_ready"], 4 * (t - 1 - PQ0))
                w = weights[name][0].rearrange("(k p) n -> p k n", p=P)
                sp.dma_start(W[t % 2], w[:, :, c0:c0 + 512]).then_inc((s["w_loaded0"], s["w_loaded1"])[t % 2], 16)

            sp.wait_ge(s["xn_ready"], TURN + 2 * NB)
            sp.dma_start(G, g_final.partition_broadcast(P)).then_inc(s["gains_loaded"], 16)
            for b in range(NB):
                sp.wait_ge(s["final_ready"], b + 1)
                if b == SMP:
                    sp.dma_start(y_sample.rearrange("b t d -> (b t) d"), QR[0:DB, b, :]).then_inc(s["done_stored"], 16)
                else:
                    sp.dma_start(yp[b], QR[:, b, :]).then_inc(s["done_stored"], 16)
            sp.wait_ge(s["done_stored"], 16 * NB)

        @block.gpsimd
        def _(pool):
            pool.wait_ge(s["kvidx_ready"], 1)
            for n, (kind, b, g) in enumerate(TILES):
                if n >= RING:
                    dve, c = tile_used(n - RING)
                    if TILES[n - RING][0] == "mv":
                        pool.wait_ge(s["cpv_done"], TILES[n - RING][1] + 1)
                    else:
                        pool.wait_ge(s["tile_used_dve"] if dve else s["tile_used_pe"], c)
                    if TILES[n - RING][0] == "st":
                        prior = [m for m in range(n - RING + 1) if TILES[m][0] == "st" and m % RING == n % RING]
                        pool.wait_ge(ns_stored[n % RING], 16 * len(prior))
                else:
                    pool.wait_ge(s["line_stored"], 16)
                if kind in ("k", "v"):
                    pool.indirect_dma_start(SLOT[n % RING], None, k_rows if kind == "k" else v_rows,
                                            bass.IndirectOffsetOnAxis(kv_idx[:, b * GRP + g:b * GRP + g + 1].bitcast(U32), 0)
                                            ).then_inc(tile_in[n % RING], 16)
                elif kind == "st":
                    pool.dma_start(SLOT[n % RING][:, 0:512].rearrange("p (h e) -> p h e", h=H),
                                   state_ret[0, b].rearrange("h d e -> d h e")).then_inc(tile_in[n % RING], 16)
                else:
                    pool.dma_start(SLOT[n % RING], (mk_rows if kind == "mk" else mv_rows)[b]).then_inc(tile_in[n % RING], 16)

            def gather(slot, which, idx):
                pool.indirect_dma_start((USLOT, VSLOT)[which][slot], None, (peer_u, peer_v)[which][0],
                                        bass.IndirectOffsetOnAxis(idx.bitcast(U32), 0)).then_inc(uv_in[which][slot], 16)

            pool.wait_ge(s["sel_ready"], NB + 1)
            pool.wait_ge(s["skT_done"], 4)
            for which in range(2):
                for b in range(DB):
                    gather(b, which, SIDX[:, b:b + 1])
            for blk in range(NBLK):
                with pool.Fori(0, NCH // 2) as c2:
                    for half in range(2):
                        pool.tensor_copy(ICH[half].bitcast(U32), IDX[:, blk, bass.ds(c2 * (2 * CHUNK) + half * CHUNK, CHUNK)].bitcast(U32)
                                         ).then_inc(s["idx_copied"], 1)
                        pool.wait_ge(s["idx_copied"], c2 * 2 + (NCH * blk + half + 1))
                        for which, used in ((0, s["u_used"]), (1, s["v_used"])):
                            for k in range(CHUNK):
                                pool.wait_ge(used, c2 * (2 * CHUNK) + (CHUNK * (NCH * blk + half) + k + 1))
                                pool.nop(nofuse=True)
                                gather(k, which, ICH[half][:, k:k + 1])

        @block.scalar
        def _(act):
            steps = [0]

            def link(ins):
                steps[0] += 1
                ins.then_inc(s["astep"], 1)
                act.wait_ge(s["astep"], steps[0])

            def sumsq(stage, rows_of, junk):
                if stage == 0:
                    act.wait_ge(s["ss_cleared"], 1)
                last = None
                for u, (r, src) in enumerate(rows_of):
                    last = act.activation(junk[0:r, :], src, ACT.Square, accum_out=ss[stage][0:r, u:u + 1])
                    if u < len(rows_of) - 1:
                        link(last)
                last.then_inc(s["sumsq_done"], 1)
                act.wait_ge(s["inv_done"], stage + 1)
                act.activation(rstd[stage], rstd[stage], ACT.Sqrt).then_inc(s["rstd_done"], 1)

            def xt_copy(n, b0):
                r = P if n < 6 or (n - TURN) % NB != SMP else DB
                if n == 6:
                    r = DB
                act.wait_ge(s["turned"], n + 1)
                act.copy(XT[:, :, P * b0:P * b0 + r],
                         turn_banks(n).rearrange("p (k t) -> p k t", k=KD)[:, :, 0:r]).then_inc(s["xt_done"], 1)

            def job_rows(j):
                return P if job_kind(j) == "mem" else ROWS[JOBS[j][1]]

            def take(j, dst):
                act.wait_ge(s["job_ready"], j + 1)
                kind = job_kind(j)
                act.activation(dst, PS[0:job_rows(j), PSUM_JOB + j % 2, :], ACT.Silu if kind == "rg" else ACT.Copy
                               ).then_inc(s["job_taken_act"], 1)

            for h in range(H):
                act.wait_ge(s["line_ps"], h + 1)
                act.copy(LROW[:, h, 0:512], PS[:, 6, :]).then_inc(s["line_cols"], 1)
                act.copy(LROW[:, h, 512:TL], PS[:, 7, 0:TL - 512]).then_inc(s["line_row"], 1)
            act.wait_ge(s["line_row"], H)
            act.wait_ge(s["line_cols"], H)
            act.dma_start(line_rows, LROW).then_inc(s["line_stored"], 16)
            act.wait_ge(s["line_stored"], 16)
            for h in range(H):
                o = h * P * TL + P - 1
                act.dma_start(TOE[:, h, :], line_dram[o:o + P * (TL - 1)].rearrange("(p c) -> p c", p=P)[:, 0:512]
                              ).then_inc(s["toe_loaded"], 16)
            act.wait_ge(s["lam_sums"], 1)
            act.activation(lexp, lsum, ACT.Exp).then_inc(s["lam_exp"], 1)
            act.wait_ge(s["mem_loaded"], 32)
            act.wait_ge(s["x_loaded"], 32)
            sumsq(0, [(P, X0[:, u, :]) for u in range(6)] + [(DB, X0[0:DB, 6, :])],
                  PS[:, 0:2, :].rearrange("p a c -> p (a c)"))
            for n in range(TURN):
                xt_copy(n, n)

            for j in range(first_job("dq")):
                t, u = JOBS[j]
                name, c0, _ = WTILES[t]
                if j >= 4:
                    act.wait_ge(mem_stored[j % 4], 16 * (j // 4))
                take(j, MSTAGE[j % 4])
                act.wait_ge(s["job_taken_act"], j + 1)
                act.dma_start(mem_out[name][u][:, c0:c0 + 512], MSTAGE[j % 4]).then_inc(mem_stored[j % 4], 16)

            def taken(j):
                act.wait_ge(s["job_taken_act"], taken_by(j)[1])

            for b in range(NB):
                take(first_job("dq") + b, RK[0:ROWS[b], b, :])
            for kind, dst, outp, outs in (("dk", RG, kp_out, ks_out), ("dv", DV, vp_out, vs_out)):
                for b in range(NB):
                    j = first_job(kind) + b
                    take(j, dst[0:ROWS[b], b, :])
                    taken(j)
                    act.dma_start(outs if b == SMP else outp[b], dst[0:ROWS[b], b, :]).then_inc(s["new_kv_stored"], 16)

            for i in range(4):
                act.wait_ge(mem_stored[i], 32)
            for st in range(NBLK * H + 1):
                if st < NBLK * H:
                    n = P * (st // H + 1)
                    act.wait_ge(s["nmax_ready"], st + 1)
                    for c in range(2):
                        last = act.activation(SC[st % 2][:, c, 0:n], SC[st % 2][:, c, 0:n], ACT.Exp,
                                              bias=nmx[:, 2 * (st % 2) + c:2 * (st % 2) + c + 1],
                                              accum_out=zsum[:, 2 * (st % 2) + c:2 * (st % 2) + c + 1])
                    last.then_inc(s["exp_done"], 1)
                if st >= 1:
                    q = st - 1
                    n = P * (q // H + 1)
                    act.wait_ge(s["wmat_turned"], q + 1)
                    if q >= 2:
                        act.wait_ge(s["av_done"], q - 1)
                    act.copy(WT[q % 2][:, 0:n], PS[:, 6, 0:n]).then_inc(s["wT_ready"], 1)
                    if q % H == H - 1:
                        act.wait_ge(s["av_done"], q + 1)
                        act.copy(DIF[:, q // H, :], PS[:, 7, :]).then_inc(s["dif_taken"], 1)

            act.wait_ge(s["new_kv_stored"], 16 * NSTORES)
            act.wait_ge(s["srow_saved"], 1)
            for kind, dst in (("rv", DV), ("rg", RG)):
                for b in range(NB):
                    if kind == "rg" and b == 0:
                        act.wait_ge(s["rowsT_done"], 20)
                    take(first_job(kind) + b, dst[0:ROWS[b], b, :])

            act.wait_ge(s["s_scored"], 1)
            act.activation(S, S, ACT.Exp).then_inc(s["sexp_done"], 1)
            act.wait_ge(s["sarg_ready"], 1)
            act.activation(sself_e[0:DB], sself_e[0:DB], ACT.Exp).then_inc(s["sexp_done"], 1)

            for b in range(DB):
                n = tile_no("st", b)
                act.wait_ge(s["ns_ready"], b + 1)
                act.dma_start(state_s[0, b].rearrange("h d e -> d h e"),
                              SLOT[n % RING][:, 0:512].rearrange("p (h e) -> p h e", h=H)).then_inc(ns_stored[n % RING], 16)
            act.wait_ge(s["ret_state"], NBLK)
            act.dma_start(state_p[0, 0].rearrange("h d e -> d h e"), STATE.rearrange("p (h e) -> p h e", h=H)
                          ).then_inc(s["state_stored"], 16)
            act.wait_ge(s["hsq_ready"], 1)
            act.activation(hss, hss, ACT.Sqrt).then_inc(s["hrstd_done"], 1)
            for b in range(NB):
                xt_copy(N_MIX + b, NMEM + b)
            act.wait_ge(s["job_taken_dve"], taken_by(first_job("mq") - 1)[1])
            junk = PS[:, 6:8, :].rearrange("p a c -> p (a c)")
            h_rows = [(ROWS[b], HR[0:ROWS[b], b, :]) for b in range(NB)]
            sumsq(1, h_rows, junk)
            for b in range(NB):
                xt_copy(N_CROSS + b, NMEM + b)
            for j in [j for j in range(len(JOBS)) if job_kind(j) == "mq"]:
                t, b = JOBS[j]
                c0 = WTILES[t][1]
                take(j, QR[0:ROWS[b], b, c0:c0 + 512])
            for b in range(NB):
                xt_copy(N_Q + b, NMEM + b)

            for st in range(NBLK + 1):
                if st < NBLK:
                    act.wait_ge(s["cmax_ready"], st + 1)
                    if st >= 2:
                        act.wait_ge(s["ce_turned"], st - 1)
                    for h in range(H):
                        z = H * (st % 2) + h
                        last = act.activation(CE[st % 2][:, h, :], PS[:, 2 * (st % 2) + h // 2, MEM * (h % 2):MEM * (h % 2) + MEM],
                                              ACT.Exp, bias=cneg[:, z:z + 1], scale=MSCALE, accum_out=csum[:, z:z + 1])
                    last.then_inc(s["cexp_done"], 1)
                if st >= 1:
                    q = st - 1
                    act.wait_ge(s["ce_turned"], q + 1)
                    if q >= 2:
                        act.wait_ge(s["co_ready"], q - 1)
                    act.copy(CET[q % 2], PS[:, 4:6, :].rearrange("p a c -> p (a c)")).then_inc(s["ceT_ready"], 1)
            act.wait_ge(s["cs_scored"], 1)
            act.activation(CS, CS, ACT.Exp, scale=MSCALE).then_inc(s["csexp_done"], 1)
            for b in range(NB):
                xt_copy(N_O + b, NMEM + b)
            act.wait_ge(s["job_taken_dve"], taken_by(len(JOBS) - 1)[1])
            sumsq(2, h_rows, junk)
            for b in range(NB):
                xt_copy(N_FFN + b, NMEM + b)

            for x in range(NSUB):
                act.wait_ge(s["rqp_ready"], x + 1)
                if x >= 2:
                    act.wait_ge(s["rs_ready"], x - 1)
                act.copy(QPT[x % 2][:, 0:SEQ], PS[:, 4 + x % 2, :])
                act.copy(QPT[x % 2][:, SEQ:TOK], PS[:, 6 + x % 2, 0:DB]).then_inc(s["rqp_taken"], 1)
            for b in range(NB):
                r = ROWS[b]
                act.wait_ge(s["sarg_ready"], 2 + b)
                act.activation(GATE[0:r, b, :], GATE[0:r, b, :], ACT.Exp).then_inc(s["sexp_done"], 1)

            act.wait_ge(s["u_used"], DB)
            act.activation(sgl, sdot, ACT.Gelu).then_inc(s["diag_ready"], 1)
            for blk in range(NBLK):
                with act.Fori(0, NCH) as c:
                    act.wait_ge(s["u_used"], c * CHUNK + CHUNK * (NCH * blk + 2))
                    act.activation(gl, dots, ACT.Gelu).then_inc(s["gelu_done"], 1)
                    act.wait_ge(s["weight_ready"], c + (NCH * blk + 1))
                    for k in range(CHUNK):
                        act.wait_ge(s["v_used"], c * CHUNK + (CHUNK * NCH * blk + k + 1))
                        act.activation(DIAG[k], ident, ACT.Copy, scale=WCH[:, k:k + 1]).then_inc(s["diag_ready"], 1)
            act.wait_ge(s["y_ready"], NB)
            sumsq(3, h_rows, junk)

        @block.vector
        def _(dve):
            steps = [0]

            def link(ins):
                steps[0] += 1
                ins.then_inc(s["vstep"], 1)
                dve.wait_ge(s["vstep"], steps[0])

            def tt(out, a, b, op):
                return dve.tensor_tensor(out, a, b, op)

            def invert(stage):
                dve.wait_ge(s["sumsq_done"], stage + 1)
                link(dve.tensor_scalar(rstd[stage], ss[stage], 1.0 / D, EPS, ALU.mult, ALU.add))
                dve.reciprocal(rstd[stage], rstd[stage]).then_inc(s["inv_done"], 1)
                dve.wait_ge(s["rstd_done"], stage + 1)

            def normed(stage, u, r, src, gain, dst):
                return dve.scalar_tensor_tensor(out=dst[0:r, :], in0=src, scalar=rstd[stage][0:r, u:u + 1],
                                                in1=gain[0:r, :], op0=ALU.mult, op1=ALU.mult)

            for x in ss:
                dve.memset(x, 1.0)
            dve.memset(hss[:, :, :], 1.0).then_inc(s["ss_cleared"], 1)
            dve.wait_ge(s["ss_cleared"], 1)
            dve.wait_ge(s["const_loaded"], 16)
            dve.wait_ge(s["small_loaded"], 16 * 6)
            for q in range(PPG):
                last = dve.tensor_copy(pt_f[32 * q:32 * q + 32, :],
                                       PTAB[32 * q:32 * q + 32, :].bitcast(I32).rearrange("p (x q) -> p x q", q=PPG)[:, :, q])
            link(last)
            link(dve.tensor_scalar(pt_f, pt_f, 32.0, const("part32"), ALU.mult, ALU.add))
            dve.tensor_copy(kv_idx.bitcast(U32), pt_f).then_inc(s["kvidx_ready"], 1)
            link(dve.memset(tab[NBUCKET:NBUCKET + 1, :], NEG))
            dve.tensor_copy(TABB[0:NBUCKET + 1], tab[0:NBUCKET + 1, :].unsqueeze(2).broadcast_to([NBUCKET + 1, H, P])
                            ).then_inc(s["past_ready"], 1)
            lv = lamv.rearrange("p (a c d) -> p a c d", a=2, c=2)
            link(tt(lv[:, :, 0, :], lv[:, :, 0, :], lv[:, :, 1, :], ALU.mult))
            dve.tensor_reduce(lsum, lv[:, :, 0, :], AX.X, ALU.add).then_inc(s["lam_sums"], 1)
            dve.wait_ge(s["lam_exp"], 1)
            dve.scalar_tensor_tensor(out=nlam, in0=lexp[:, 1:2], scalar=-LAM_INIT, in1=lexp[:, 0:1], op0=ALU.add,
                                     op1=ALU.subtract).then_inc(s["lam_ready"], 1)
            dve.wait_ge(s["lam_ready"], 1)
            dve.wait_ge(s["past_ps"], 1)
            dve.tensor_copy(bias_s, PS[:, 7, 0:24].rearrange("p (j h) -> p j h", j=6)).then_inc(s["past_ready"], 1)
            dve.wait_ge(s["past_ready"], 2)

            invert(0)
            dve.wait_ge(s["gains_loaded"], 16)
            for u in range(7):
                if u >= 2:
                    dve.wait_ge(s["turned"], u - 1)
                r = DB if u == 6 else P
                normed(0, u, r, X0[0:r, u, :], GM if u < NMEM else G, XN[u % 2]).then_inc(s["xn_ready"], 1)

            def rows_t(e, dst):
                b = e % NB
                r = ROWS[b]
                dve.wait_ge(s["rows_turned"], e + 1)
                dve.tensor_copy(dst[:, :, P * b:P * b + r],
                                PS[:, e % 4, :].rearrange("p (h t) -> p h t", h=H)[:, :, 0:r]).then_inc(s["rowsT_done"], 1)

            for e in range(NB):
                rows_t(e, DQT)
            for e in range(NB, 2 * NB):
                rows_t(e, DKT)
            dve.wait_ge(s["job_taken_act"], taken_by(first_job("dv") + SMP)[1])
            dve.tensor_copy(SRQ[0:DB, :], RK[0:DB, SMP, :])
            dve.tensor_copy(SRK[0:DB, :], RG[0:DB, SMP, :])
            dve.tensor_copy(DVS[0:DB, :], DV[0:DB, SMP, :]).then_inc(s["srow_saved"], 1)
            dve.wait_ge(s["srow_saved"], 1)

            dve.wait_ge(s["toe_loaded"], 16 * H)
            for st in range(NBLK * H + 1):
                if st < NBLK * H:
                    i, h = st // H, st % H
                    n = P * (i + 1)
                    z = slice(2 * (st % 2), 2 * (st % 2) + 2)
                    dve.wait_ge(s["scores_ready"], st + 1)
                    b0 = 2 * (st % 2)
                    dve.scalar_tensor_tensor(out=SC[st % 2][:, :, 0:n], in0=PS[:, b0:b0 + 2, 0:n], scalar=SCALE,
                                             in1=TOE[:, h, 512 - n:512].unsqueeze(1).broadcast_to([P, 2, n]),
                                             op0=ALU.mult, op1=ALU.add).then_inc(s["sc_biased"], 1)
                    dve.wait_ge(s["sc_biased"], st + 1)
                    dve.tensor_reduce(nmx[:, z], SC[st % 2][:, :, 0:n], AX.X, ALU.max, negate=True).then_inc(s["nmax_ready"], 1)
                if st >= 1:
                    q = st - 1
                    n = P * (q // H + 1)
                    z = 2 * (q % 2)
                    dve.wait_ge(s["exp_done"], q + 1)
                    link(dve.reciprocal(zsum[:, z:z + 2], zsum[:, z:z + 2]))
                    link(tt(zsum[:, z + 1:z + 2], zsum[:, z + 1:z + 2], nlam, ALU.mult))
                    if q >= 2:
                        dve.wait_ge(s["wmat_turned"], q - 1)
                    link(dve.tensor_scalar(WM[q % 2][:, 0:n], SC[q % 2][:, 0, 0:n], zsum[:, z:z + 1], None, ALU.mult))
                    dve.scalar_tensor_tensor(out=WM[q % 2][:, 0:n], in0=SC[q % 2][:, 1, 0:n], scalar=zsum[:, z + 1:z + 2],
                                             in1=WM[q % 2][:, 0:n], op0=ALU.mult, op1=ALU.add).then_inc(s["w_ready"], 1)

            ntile_dve = [0]

            def key_tile(b, g):
                n = tile_no("k", b, g)
                tile_arrived(dve, n)
                dve.wait_ge(s["qb_ready"], b + 1)
                t = SLOT[n % RING].rearrange("p (j x) -> p j x", j=TPR)
                link(tt(t, t, PS[:, 6 + b % 2, :].unsqueeze(1).broadcast_to([P, TPR, 512]), ALU.mult))
                dve.tensor_reduce(S[:, 128 * b + 32 * g:128 * b + 32 * g + 32],
                                  SLOT[n % RING].rearrange("p (x d) -> p x d", d=DH), AX.X, ALU.add).then_inc(s["tile_used_dve"], 1)

            def rotary(j, dst, tq):
                b = JOBS[j][1]
                r = ROWS[b]
                dve.wait_ge(s["job_ready"], j + 1)
                src = PS[0:r, PSUM_JOB + j % 2, :].rearrange("p (x d) -> p x d", d=64)
                cos = rot[0:r, b, tq, :].unsqueeze(1).broadcast_to([r, 2 * H, 64])
                sin = rot[0:r, b, tq + 1, :].unsqueeze(1).broadcast_to([r, 2 * H, 64])
                a = ROT_A[0:r, :].rearrange("p (x d) -> p x d", d=64)
                c = ROT_B[0:r, :].rearrange("p (x d) -> p x d", d=64)
                tt(a, src, cos, ALU.mult)
                tt(c, src, sin, ALU.mult).then_inc(s["job_taken_dve"], 1)
                dve.wait_ge(s["job_taken_dve"], taken_by(j)[1])
                a4 = ROT_A[0:r, :].rearrange("p (h c d) -> p h c d", h=H, c=2)
                c4 = ROT_B[0:r, :].rearrange("p (h c d) -> p h c d", h=H, c=2)
                d4 = dst[0:r, b, :].rearrange("p (h c d) -> p h c d", h=H, c=2)
                tt(d4[:, :, 0, :], a4[:, :, 0, :], c4[:, :, 1, :], ALU.subtract)
                tt(d4[:, :, 1, :], a4[:, :, 1, :], c4[:, :, 0, :], ALU.add).then_inc(s["ret_rows"], 1)

            keys = [(b, g) for b in range(DB) for g in range(GRP)]
            dve.wait_ge(s["new_kv_stored"], 16 * NSTORES)
            done = 0
            for kind, dst, tq, tdst, e0 in (("rq", RG, 0, DQT, 2 * NB), ("rk", RK, 2, DKT, 3 * NB)):
                for b in range(NB):
                    rotary(first_job(kind) + b, dst, tq)
                    key_tile(*keys[done])
                    done += 1
                dve.wait_ge(s["av_done"], NBLK * H)
                for b in range(NB):
                    rows_t(e0 + b, tdst)
            for k in keys[done:]:
                key_tile(*k)

            b5 = BFULL[:, :, :].rearrange("p (g j) (h c) -> p g j h c", j=TPR, h=H)
            for g in range(GRP):
                for j in range(TPR):
                    src = bias_s[:, j if g == GRP - 1 else 4, :].unsqueeze(2).broadcast_to([P, H, 2])
                    last = dve.tensor_copy(b5[:, g, j], src)
            link(last)
            S3 = S.rearrange("p (b x) -> p b x", b=DB)
            S4 = S.rearrange("p (b x c) -> p b x c", b=DB, c=HC)
            link(dve.scalar_tensor_tensor(out=S3, in0=S3, scalar=SCALE,
                                          in1=BFULL.rearrange("p x c -> p (x c)").unsqueeze(1).broadcast_to([P, DB, 128]),
                                          op0=ALU.mult, op1=ALU.add))
            link(dve.tensor_reduce(colmax.rearrange("p (b c) -> p b c", b=DB), S4.rearrange("p b x c -> p b c x"),
                                   AX.X, ALU.max))
            link(tt(ROT_A[0:DB, :], SRQ[0:DB, :], SRK[0:DB, :], ALU.mult))
            link(dve.tensor_reduce(sself[0:DB, :], ROT_A[0:DB, :].rearrange("p (x d) -> p x d", d=DH), AX.X, ALU.add))
            link(dve.scalar_tensor_tensor(out=sself[0:DB, :].rearrange("p (h c) -> p h c", h=H),
                                          in0=sself[0:DB, :].rearrange("p (h c) -> p h c", h=H), scalar=SCALE,
                                          in1=bias_s[0:DB, 5, :].unsqueeze(2).broadcast_to([DB, H, 2]),
                                          op0=ALU.mult, op1=ALU.add))
            link(tt(sself_e[0:DB], sself[0:DB, :].unsqueeze(1).broadcast_to([DB, DB, HC]), dmask[0:DB], ALU.mult))
            link(dve.tensor_scalar(sself_m[0:DB], dmask[0:DB], 1.0, -NEG, ALU.subtract, ALU.mult))
            link(tt(sself_m[0:DB], sself_m[0:DB], sself_e[0:DB], ALU.add))
            tt(colmax[0:DB, :].rearrange("p (b c) -> p b c", b=DB), colmax[0:DB, :].rearrange("p (b c) -> p b c", b=DB),
               sself_m[0:DB], ALU.max).then_inc(s["colmax_ready"], 1)
            dve.wait_ge(s["colmax_turned"], 1)
            link(dve.tensor_reduce(mcol[0:64, :], PS[0:64, 0, 0:P], AX.X, ALU.max))
            dve.tensor_scalar(mdiag[0:64, :], ident[0:64, 0:64], mcol[0:64, :], None, ALU.mult).then_inc(s["maxdiag_ready"], 1)
            dve.wait_ge(s["maxbc_ready"], 1)
            mbc = PS[:, 1, 0:64].rearrange("p (b c) -> p b c", b=DB)
            tt(S4, S4, mbc.unsqueeze(2).broadcast_to([P, DB, 16, HC]), ALU.subtract).then_inc(s["s_scored"], 1)
            link(tt(sself_e[0:DB], sself_e[0:DB], mbc[0:DB], ALU.subtract))
            tt(sself_e[0:DB], sself_e[0:DB], dmask[0:DB], ALU.mult).then_inc(s["sarg_ready"], 1)
            dve.wait_ge(s["sexp_done"], 2)
            tt(sself_e[0:DB], sself_e[0:DB], dmask[0:DB], ALU.mult)
            dve.tensor_reduce(esum, S4.rearrange("p b x c -> p b c x"), AX.X, ALU.add).then_inc(s["esum_ready"], 1)
            dve.wait_ge(s["z_ready"], 1)
            link(dve.reciprocal(rz[0:HC, :], PS[0:HC, 0, 0:DB]))
            link(dve.scalar_tensor_tensor(out=coef[0:HC, :], in0=const("odd")[0:HC, :], scalar=nlam[0:HC, :],
                                          in1=const("even")[0:HC, :], op0=ALU.mult, op1=ALU.add))
            link(dve.tensor_scalar(rz[0:HC, :], rz[0:HC, :], coef[0:HC, :], None, ALU.mult))
            tt(cl[0:HC], mask8[0:HC], rz[0:HC, :].unsqueeze(2).broadcast_to([HC, DB, DB]), ALU.mult).then_inc(s["coef_ready"], 1)

            dve.wait_ge(s["rowsT_done"], 20)
            for h in range(H):
                last = tt(RQM[:, h], mask8, DQT[:, h, SEQ:TOK].unsqueeze(2).broadcast_to([P, DB, DB]), ALU.mult)
            last.then_inc(s["rqm_ready"], 1)
            gam4 = const("gam").unsqueeze(2).broadcast_to([P, H, P])
            for b in range(DB):
                n = tile_no("st", b)
                if b >= 2:
                    dve.wait_ge(s["outer_ready"], b - 1)
                dve.tensor_scalar(KEXP[b % 2][0:DB, :], RK[0:DB, SMP, :], dmask[0:DB, b, 0:1], None, ALU.mult
                                  ).then_inc(s["kexp_ready"], 1)
                tile_arrived(dve, n)
                st = SLOT[n % RING][:, 0:512]
                link(tt(st.rearrange("p (h e) -> p h e", h=H), st.rearrange("p (h e) -> p h e", h=H), gam4, ALU.mult))
                dve.wait_ge(s["outer_ready"], b + 1)
                tt(st, st, PS[:, 2 + b % 2, :], ALU.add).then_inc(s["ns_ready"], 1)
            dve.wait_ge(s["tile_used_pe"], DB)
            dve.tensor_copy(RK[0:DB, SMP, :], PS[0:DB, 7, :])

            gl4 = const("gL").unsqueeze(2).broadcast_to([P, H, P])
            for i in range(NBLK):
                if i:
                    dve.wait_ge(s["ret_out"], i)
                tt(RQD.rearrange("p (h t) -> p h t", h=H), DQT[:, :, P * i:P * i + P],
                   const("qdec").rearrange("p (h t) -> p h t", h=H), ALU.mult)
                tt(RKD.rearrange("p (h d) -> p h d", h=H), RK[:, i, :].rearrange("p (h d) -> p h d", h=H),
                   const("kdec").unsqueeze(2).broadcast_to([P, H, P]), ALU.mult).then_inc(s["rqd_ready"], 1)
                dve.wait_ge(s["ret_scores"], i + 1)
                tt(RSC, PS[:, 0, :], const("decayT"), ALU.mult).then_inc(s["ret_sc_ready"], 1)
                dve.wait_ge(s["rqd_ready"], i + 1)
                dve.wait_ge(s["ret_out"], i + 1)
                dve.tensor_copy(RK[:, i, :], PS[:, 2, :])
                if i == 0:
                    dve.tensor_copy(STATE, PS[:, 3, :]).then_inc(s["ret_state"], 1)
                else:
                    link(tt(STATE.rearrange("p (h e) -> p h e", h=H), STATE.rearrange("p (h e) -> p h e", h=H), gl4, ALU.mult))
                    tt(STATE, STATE, PS[:, 3, :], ALU.add).then_inc(s["ret_state"], 1)
                dve.wait_ge(s["ret_state"], i + 1)

            for b in range(DB):
                dve.wait_ge(s["pv_done"], b + 1)
                if b == 0:
                    dve.wait_ge(s["tile_used_pe"], DB)
                if b >= 2:
                    dve.wait_ge(s["dif_row_ready"], b - 1)
                tt(OM[b % 2][0:HC, :], PS[0:HC, 4 + b % 2, :], const("hmask")[0:HC, :], ALU.mult).then_inc(s["om_ready"], 1)
            dve.wait_ge(s["dif_row_ready"], DB)
            link(dve.tensor_copy(DIF[0:DB, SMP, :], PS[0:DB, 6, :]))
            dve.wait_ge(s["state_stored"], 16)
            for r, b0, b1 in ((P, 0, NBLK), (DB, SMP, NB)):
                w = 512 * (b1 - b0)
                for i, src in ((0, RK), (1, DIF)):
                    last = tt(SQ[i][0:r, 0:w].rearrange("p (b d) -> p b d", b=b1 - b0), src[0:r, b0:b1, :], src[0:r, b0:b1, :], ALU.mult)
                link(last)
                for i in range(2):
                    last = dve.tensor_reduce(hss[0:r, b0:b1, H * i:H * i + H],
                                             SQ[i][0:r, 0:w].rearrange("p (b h d) -> p b h d", b=b1 - b0, h=H), AX.X, ALU.add)
                link(last)
            link(dve.tensor_scalar(hss, hss, 1.0 / P, EPS, ALU.mult, ALU.add))
            dve.reciprocal(hss, hss).then_inc(s["hsq_ready"], 1)
            dve.wait_ge(s["hrstd_done"], 1)
            link(dve.tensor_scalar(hss[:, :, H:2 * H], hss[:, :, H:2 * H], 1.0 - LAM_INIT, None, ALU.mult))
            for b in range(NB):
                r = ROWS[b]

                def heads(x):
                    return x[0:r, b, :].rearrange("p (h d) -> p h d", h=H)

                link(tt(heads(RK), heads(RK), hss[0:r, b, 0:H].unsqueeze(2).broadcast_to([r, H, P]), ALU.mult))
                tt(RK[0:r, b, :], RK[0:r, b, :], RG[0:r, b, :], ALU.mult)
                tt(heads(DIF), heads(DIF), hss[0:r, b, H:2 * H].unsqueeze(2).broadcast_to([r, H, P]), ALU.mult
                   ).then_inc(s["mix_ready"], 1)

            def residual(kind):
                for j in [j for j in range(len(JOBS)) if job_kind(j) == kind]:
                    t, b = JOBS[j]
                    c0, r = WTILES[t][1], ROWS[b]
                    dve.wait_ge(s["job_ready"], j + 1)
                    tt(HR[0:r, b, c0:c0 + 512], HR[0:r, b, c0:c0 + 512], PS[0:r, PSUM_JOB + j % 2, :], ALU.add
                       ).then_inc(s["job_taken_dve"], 1)

            dve.wait_ge(s["x_again"], 32)
            residual("mix")
            for e in range(4):
                dve.wait_ge(s["mkr_turned"], e + 1)
                dve.tensor_copy(MKT[:, 2 * e:2 * e + 2, :].rearrange("p k m -> p (k m)"), PS[:, e, :]).then_inc(s["mkT_done"], 1)
            invert(1)
            dve.wait_ge(s["gains_loaded"], 32)
            dve.wait_ge(s["job_taken_dve"], taken_by(first_job("mq") - 1)[1])
            for b in range(NB):
                n = N_CROSS + b
                if b >= 2:
                    dve.wait_ge(s["turned"], n - 1)
                normed(1, b, ROWS[b], HR[0:ROWS[b], b, :], G, XN[b % 2]).then_inc(s["xn_ready"], 1)

            for st in range(NBLK + 1):
                if st < NBLK:
                    z = slice(H * (st % 2), H * (st % 2) + H)
                    dve.wait_ge(s["cs_ready"], st + 1)
                    link(dve.tensor_reduce(cneg[:, z], PS[:, 2 * (st % 2):2 * (st % 2) + 2, :].rearrange("p a (c m) -> p (a c) m", c=2),
                                           AX.X, ALU.max, negate=True))
                    dve.tensor_scalar(cneg[:, z], cneg[:, z], MSCALE, None, ALU.mult).then_inc(s["cmax_ready"], 1)
                if st >= 1:
                    q = st - 1
                    z = slice(H * (q % 2), H * (q % 2) + H)
                    dve.wait_ge(s["co_ready"], q + 1)
                    link(dve.reciprocal(csum[:, z], csum[:, z]))
                    tt(QR[:, q, :].rearrange("p (h d) -> p h d", h=H),
                       PS[:, 6:8, :].rearrange("p a (c d) -> p (a c) d", c=2),
                       csum[:, z].unsqueeze(2).broadcast_to([P, H, MDH]), ALU.mult).then_inc(s["co_taken"], 1)

            for b in range(DB):
                n = tile_no("mk", b)
                tile_arrived(dve, n)
                dve.wait_ge(s["cqb_ready"], b + 1)
                t = SLOT[n % RING].rearrange("p (j x) -> p j x", j=NMEM)
                q = PS[:, 2 * (b % 2):2 * (b % 2) + 2, :].rearrange("p a c -> p (a c)")
                link(tt(t, t, q.unsqueeze(1).broadcast_to([P, NMEM, D]), ALU.mult))
                dve.tensor_reduce(CS4[:, b], SLOT[n % RING].rearrange("p (j h d) -> p j h d", j=NMEM, h=H), AX.X, ALU.add
                                  ).then_inc(s["tile_used_dve"], 1)
            dve.wait_ge(s["tile_used_dve"], tile_used(tile_no("mk", DB - 1))[1])
            dve.tensor_reduce(ccol.rearrange("p (b h) -> p b h", b=DB), CS4.rearrange("p b j h -> p b h j"), AX.X, ALU.max
                              ).then_inc(s["ccolmax_ready"], 1)
            dve.wait_ge(s["ccolmax_turned"], 1)
            link(dve.tensor_reduce(cmx[0:32, :], PS[0:32, 4, 0:P], AX.X, ALU.max))
            dve.tensor_scalar(cmd[0:32, :], ident[0:32, 0:32], cmx[0:32, :], None, ALU.mult).then_inc(s["cmaxdiag_ready"], 1)
            dve.wait_ge(s["cmaxbc_ready"], 1)
            tt(CS4, CS4, PS[:, 5, 0:32].rearrange("p (b h) -> p b h", b=DB).unsqueeze(2).broadcast_to([P, DB, NMEM, H]),
               ALU.subtract).then_inc(s["cs_scored"], 1)
            dve.wait_ge(s["csexp_done"], 1)
            dve.tensor_reduce(cesum.rearrange("p (b h) -> p b h", b=DB), CS4.rearrange("p b j h -> p b h j"), AX.X, ALU.add
                              ).then_inc(s["cesum_ready"], 1)
            dve.wait_ge(s["cz_ready"], 1)
            link(dve.reciprocal(crz[0:H, :], PS[0:H, 4, 0:DB]))
            tt(ccl[0:H], mask8[0:H], crz[0:H, :].unsqueeze(2).broadcast_to([H, DB, DB]), ALU.mult).then_inc(s["ccoef_ready"], 1)
            for b in range(DB):
                dve.wait_ge(s["cpv_done"], b + 1)
                if b >= 2:
                    dve.wait_ge(s["crow_ready"], b - 1)
                tt(COM[b % 2][0:H, :], PS[0:H, 2 * (b % 2):2 * (b % 2) + 2, :].rearrange("p a c -> p (a c)"),
                   const("hmask4")[0:H, :], ALU.mult).then_inc(s["com_ready"], 1)
            dve.wait_ge(s["crow_ready"], DB)
            dve.tensor_copy(QR[0:DB, SMP, :], PS[0:DB, 6:8, :].rearrange("p a c -> p (a c)")).then_inc(s["crow_ready"], 1)
            residual("mo")

            invert(2)
            dve.wait_ge(s["gains_loaded"], 48)
            dve.wait_ge(s["turned"], N_FFN)
            for b in range(NB):
                normed(2, b, ROWS[b], HR[0:ROWS[b], b, :], G, QR[:, b, :]).then_inc(s["xn_ready"], 1)
            for e in range(4):
                dve.wait_ge(s["sk_turned"], e + 1)
                dve.tensor_copy(SKT[:, 4 * e:4 * e + 4, :].rearrange("p x k -> p (x k)"), PS[:, e, :]).then_inc(s["skT_done"], 1)

            def scores_of(x, b):
                r = ROWS[b]
                if b == SMP:
                    return PS[0:r, 2 * (x % 2) + 1, 0:NK]
                return PS[0:r, 2 * (x % 2), NK * b:NK * b + NK]

            for x in range(NSUB):
                dve.wait_ge(s["rs_ready"], x + 1)
                for step in range(5):
                    for b in range(NB):
                        r = ROWS[b]
                        src, work = scores_of(x, b), WORK[0:r, b, :]
                        v, i = TV[0:r, b, x, :], TI[0:r, b, x, :].bitcast(U32)
                        if step == 0:
                            last = dve.max(v[:, 0:8], src)
                        elif step == 1:
                            last = dve.max_index(i[:, 0:8], v[:, 0:8], src)
                        elif step == 2:
                            last = dve.match_replace(work, v[:, 0:8], src, NEG)
                        elif step == 3:
                            last = dve.max(v[:, 8:16], work)
                        else:
                            last = dve.max_index(i[:, 8:16], v[:, 8:16], work)
                    if step == 4:
                        last.then_inc(s["rs_taken"], 1)
                    elif step != 1:
                        link(last)
            dve.wait_ge(s["rs_taken"], NSUB)

            for b in range(NB):
                r = ROWS[b]
                v = TV[0:r, b, :, :].rearrange("p (h c) k -> p h c k", c=2)
                cand = CAND[0:r].rearrange("p (h a c) -> p h a c", h=PH, a=TOPK)
                link(dve.tensor_copy(TIF[0:r].rearrange("p (x k) -> p x k", x=NSUB), TI[0:r, b].bitcast(U32)))
                link(tt(cand, v[:, :, 0, :].unsqueeze(3).broadcast_to([r, PH, TOPK, TOPK]),
                        v[:, :, 1, :].unsqueeze(2).broadcast_to([r, PH, TOPK, TOPK]), ALU.add))
                for step in range(5):
                    for h in range(PH):
                        src, work = CAND[0:r, 256 * h:256 * h + 256], CAND2[0:r, 256 * h:256 * h + 256]
                        bv, bi = BV[0:r, TOPK * h:TOPK * h + TOPK], BI[0:r, TOPK * h:TOPK * h + TOPK].bitcast(U32)
                        if step == 0:
                            last = dve.max(bv[:, 0:8], src)
                        elif step == 1:
                            last = dve.max_index(bi[:, 0:8], bv[:, 0:8], src)
                        elif step == 2:
                            last = dve.match_replace(work, bv[:, 0:8], src, NEG)
                        elif step == 3:
                            last = dve.max(bv[:, 8:16], work)
                        else:
                            last = dve.max_index(bi[:, 8:16], bv[:, 8:16], work)
                    if step != 1:
                        link(last)
                bv3 = BV[0:r].rearrange("p (h k) -> p h k", h=PH)
                gate3 = GATE[0:r, b, :].rearrange("p (h k) -> p h k", h=PH)
                tt(gate3, bv3, bv3[:, :, 0:1].broadcast_to([r, PH, TOPK]), ALU.subtract).then_inc(s["sarg_ready"], 1)
                dve.tensor_scalar(AU[0:r].bitcast(U32), BI[0:r].bitcast(U32), 4, None, ALU.logical_shift_right)
                link(dve.tensor_scalar(CU[0:r].bitcast(U32), BI[0:r].bitcast(U32), TOPK - 1, None, ALU.bitwise_and))
                dve.tensor_copy(AF[0:r], AU[0:r].bitcast(U32))
                link(dve.tensor_copy(CF[0:r], CU[0:r].bitcast(U32)))
                tif = TIF[0:r].rearrange("p (h c k) -> p h c k", h=PH, c=2)
                hot = HOT[0:r].rearrange("p (h k a) -> p h k a", h=PH, k=TOPK)
                for half, pos, out in ((0, AF, GA), (1, CF, GC)):
                    link(tt(HOT[0:r].rearrange("p (n a) -> p n a", a=TOPK), pos[0:r].unsqueeze(2).broadcast_to([r, NSEL, TOPK]),
                            const("iota16")[0:r].unsqueeze(1).broadcast_to([r, NSEL, TOPK]), ALU.is_equal))
                    link(tt(hot, hot, tif[:, :, half, :].unsqueeze(2).broadcast_to([r, PH, TOPK, TOPK]), ALU.mult))
                    link(dve.tensor_reduce(out[0:r], HOT[0:r].rearrange("p (n a) -> p n a", a=TOPK), AX.X, ALU.add))
                link(dve.scalar_tensor_tensor(out=GA[0:r], in0=GA[0:r], scalar=float(NK), in1=GC[0:r], op0=ALU.mult, op1=ALU.add))
                if b == SMP:
                    link(dve.tensor_copy(sidx_row[0:r], GA[0:r]))
                dve.tensor_copy(IDX[0:r, b, :].bitcast(U32), GA[0:r])
                dve.wait_ge(s["sexp_done"], 3 + b)
                link(dve.tensor_reduce(bsum[0:r], gate3, AX.X, ALU.add))
                link(dve.reciprocal(bsum[0:r], bsum[0:r]))
                tt(gate3, gate3, bsum[0:r].unsqueeze(2).broadcast_to([r, PH, TOPK]), ALU.mult).then_inc(s["sel_ready"], 1)
            dve.wait_ge(s["sidx_turned"], 1)
            dve.tensor_copy(SIDX.bitcast(U32), PS[:, 0, 0:DB])
            link(dve.tensor_copy(SGATE, PS[:, 0, P:P + DB]))
            dve.memset(sidx_row[0:1, 0:1], 0.0).then_inc(s["sel_ready"], 1)

            for b in range(DB):
                dve.wait_ge(s["u_in0"] if b == 0 else uv_in[0][b], 16)
                dve.wait_ge(s["xb_ready"], b + 1)
                x = PS[:, 2 * (b % 2):2 * (b % 2) + 2, :].rearrange("p a c -> p (a c)")
                dve.tensor_tensor_reduce(USLOT[b], USLOT[b], x, 1.0, 0.0, ALU.mult, ALU.add, sdot[:, b:b + 1]).then_inc(s["u_used"], 1)
            dve.wait_ge(s["u_used"], DB)
            dve.wait_ge(s["diag_ready"], 1)
            link(tt(sgl, sgl, SGATE, ALU.mult))
            tt(SWM, mask8, sgl.unsqueeze(2).broadcast_to([P, DB, DB]), ALU.mult).then_inc(s["smp_w"], 1)

            def add_expert_rows(b):
                banks = 6 if b == SMP else 2 * (b % 2)
                r = ROWS[b]
                dve.wait_ge(s["v_used"], CHUNK if b == SMP else CHUNK * (NCH * (b + 1) + 1))
                tt(HR[0:r, b, :], HR[0:r, b, :], PS[0:r, banks:banks + 2, :].rearrange("p a c -> p (a c)"), ALU.add
                   ).then_inc(s["y_ready"], 1)

            for blk in range(NBLK):
                with dve.Fori(0, NCH) as c:
                    for k in range(CHUNK):
                        dve.wait_ge(uv_in[0][k], c * 16 + 16 * (NCH * blk + 2))
                        dve.tensor_tensor_reduce(USLOT[k], USLOT[k], QR[:, blk, :], 1.0, 0.0, ALU.mult, ALU.add,
                                                 dots[:, k:k + 1]).then_inc(s["u_used"], 1)
                    dve.wait_ge(s["gelu_done"], c + (NCH * blk + 1))
                    dve.wait_ge(s["diag_ready"], c * CHUNK + (CHUNK * NCH * blk + 1))
                    tt(WCH, gl, GATE[:, blk, bass.ds(c * CHUNK, CHUNK)], ALU.mult).then_inc(s["weight_ready"], 1)
                add_expert_rows(SMP if blk == 0 else blk - 1)
            add_expert_rows(NBLK - 1)

            invert(3)
            dve.wait_ge(s["gains_loaded"], 64)
            for b in range(NB):
                normed(3, b, ROWS[b], HR[0:ROWS[b], b, :], G, QR[:, b, :]).then_inc(s["final_ready"], 1)

        @block.tensor
        def _(pe):
            pe.wait_ge(s["const_loaded"], 16)
            pe.wait_ge(s["past_ready"], 1)
            for h in range(H):
                if h:
                    pe.wait_ge(s["line_row"], h)
                    pe.wait_ge(s["line_cols"], h)
                pe.matmul(PS[:, 6, :], TABB[0:NBUCKET + 1, h, :], const("line")[0:NBUCKET + 1, 0:512], start=True, stop=True)
                pe.matmul(PS[:, 7, 0:TL - 512], TABB[0:NBUCKET + 1, h, :], const("line")[0:NBUCKET + 1, 512:TL],
                          start=True, stop=True).then_inc(s["line_ps"], 1)
            pe.wait_ge(s["line_row"], H)
            for j in range(6):
                last = pe.matmul(PS[:, 7, 4 * j:4 * j + 4], const("past")[0:NBUCKET, P * j:P * j + P], tab[0:NBUCKET, :],
                                 start=True, stop=True)
            last.then_inc(s["past_ps"], 1)

            def turn(n, chunks, r):
                if n >= 2:
                    pe.wait_ge(s["xt_done"], n - 1)
                tb = turn_banks(n)
                for k, c in enumerate(chunks):
                    last = pe.transpose(tb[:, P * k:P * k + r], c, ident[0:r, 0:r])
                last.then_inc(s["turned"], 1)

            def pieces(row, r):
                return [row[0:r, P * k:P * k + P] for k in range(row.shape[-1] // P)]

            for n in range(TURN):
                pe.wait_ge(s["xn_ready"], n + 1)
                r = DB if n == 6 else P
                turn(n, pieces(XN[n % 2], r), r)
            pe.wait_ge(s["xt_done"], TURN)

            def job(j, x0):
                t, u = JOBS[j]
                r = P if job_kind(j) == "mem" else ROWS[u]
                w_arrived(pe, t)
                if j >= 2:
                    dve, c = taken_by(j - 2)
                    pe.wait_ge(s["job_taken_dve"] if dve else s["job_taken_act"], c)
                for k in range(KD):
                    last = pe.matmul(PS[0:r, PSUM_JOB + j % 2, :], XT[:, k, x0:x0 + r], W[t % 2][:, k, :],
                                     start=(k == 0), stop=(k == KD - 1))
                last.then_inc(s["job_ready"], 1)

            def jobs(kind, x0=0, between=None):
                done = [j for j in range(len(JOBS)) if job_kind(j) == kind]
                for j in done:
                    job(j, x0 + P * JOBS[j][1])
                    if between:
                        between(j - done[0])

            jobs("mem")

            def rows_turn(e, row, b, ready, count):
                r = ROWS[b]
                pe.wait_ge(ready, count)
                if e >= 4:
                    pe.wait_ge(s["rowsT_done"], e - 3)
                for h in range(H):
                    last = pe.transpose(PS[:, e % 4, P * h:P * h + r], row[0:r, P * h:P * h + P], ident[0:r, 0:r])
                last.then_inc(s["rows_turned"], 1)

            X1 = NMEM * P
            for kind, src, e0 in (("dq", RK, 0), ("dk", RG, NB)):
                jobs(kind, X1)
                for b in range(NB):
                    rows_turn(e0 + b, src[:, b, :], b, s["job_taken_act"], taken_by(first_job(kind) + b)[1])
            jobs("dv", X1)

            pe.wait_ge(s["rowsT_done"], 2 * NB)
            pe.wait_ge(s["job_taken_act"], taken_by(first_job("dv") + SMP)[1])
            pe.wait_ge(s["past_ready"], 2)
            for st in range(NBLK * H + 1):
                if st < NBLK * H:
                    i, h = st // H, st % H
                    n = P * (i + 1)
                    if st >= 2:
                        pe.wait_ge(s["sc_biased"], st - 1)
                    for c in range(2):
                        last = pe.matmul(PS[:, 2 * (st % 2) + c, 0:n], DQT[DH * c:DH * c + DH, h, P * i:P * i + P],
                                         DKT[DH * c:DH * c + DH, h, 0:n], start=True, stop=True)
                    last.then_inc(s["scores_ready"], 1)
                if st >= 1:
                    q = st - 1
                    i, h = q // H, q % H
                    pe.wait_ge(s["w_ready"], q + 1)
                    if q >= 1:
                        pe.wait_ge(s["wT_ready"], q)
                    for k in range(i + 1):
                        last = pe.transpose(PS[:, 6, P * k:P * k + P], WM[q % 2][:, P * k:P * k + P], ident)
                    last.then_inc(s["wmat_turned"], 1)
                    if h == 0 and i >= 1:
                        pe.wait_ge(s["dif_taken"], i)
                    pe.wait_ge(s["wT_ready"], q + 1)
                    for k in range(i + 1):
                        last = pe.matmul(PS[:, 7, P * h:P * h + P], WT[q % 2][:, P * k:P * k + P], DV[:, k, P * h:P * h + P],
                                         start=(k == 0), stop=(k == i))
                    last.then_inc(s["av_done"], 1)
            pe.wait_ge(s["dif_taken"], NBLK)
            pe.wait_ge(s["srow_saved"], 1)

            def query_bc(b):
                if b >= 2:
                    pe.wait_ge(s["tile_used_dve"], GRP * (b - 1))
                pe.matmul(PS[:, 6 + b % 2, :], sel[0:DB, b, :], SRQ[0:DB, :], start=True, stop=True).then_inc(s["qb_ready"], 1)

            query_bc(0)
            query_bc(1)
            jobs("rq", X1)
            for b in range(NB):
                rows_turn(2 * NB + b, RG[:, b, :], b, s["ret_rows"], b + 1)
            jobs("rk", X1)
            query_bc(2)
            for b in range(NB):
                rows_turn(3 * NB + b, RK[:, b, :], b, s["ret_rows"], NB + b + 1)
            query_bc(3)
            jobs("rv", X1, lambda i: query_bc(4 + i // 4) if i in (1, 4) else None)
            jobs("rg", X1, lambda i: query_bc(6 + i // 4) if i in (1, 4) else None)

            pe.wait_ge(s["rowsT_done"], 20)
            pe.wait_ge(s["colmax_ready"], 1)
            pe.transpose(PS[0:64, 0, 0:P], colmax, ident).then_inc(s["colmax_turned"], 1)
            pe.wait_ge(s["maxdiag_ready"], 1)
            pe.matmul(PS[:, 1, 0:64], ones[0:64, :], mdiag[0:64, :], start=True, stop=True).then_inc(s["maxbc_ready"], 1)
            pe.wait_ge(s["esum_ready"], 1)
            for b in range(DB):
                pe.matmul(PS[0:HC, 0, b:b + 1], esum[:, b, :], ones[:, 0:1], start=True, stop=False)
                last = pe.matmul(PS[0:HC, 0, b:b + 1], sself_e[0:DB, b, :], ones[0:DB, 0:1], start=False, stop=True)
            last.then_inc(s["z_ready"], 1)

            pe.wait_ge(s["tile_used_dve"], GRP * DB)
            pe.wait_ge(s["job_taken_act"], taken_by(first_job("rg") + SMP)[1])
            pe.wait_ge(s["rqm_ready"], 1)
            pe.matmul(PS[0:DB, 7, :], zeros[:, 0:DB], const("decayT"), start=True, stop=False, skip_group_check=True)
            for b in range(DB):
                pe.wait_ge(s["kexp_ready"], b + 1)
                if b >= 2:
                    pe.wait_ge(s["ns_ready"], b - 1)
                for h in range(H):
                    last = pe.matmul(PS[:, 2 + b % 2, P * h:P * h + P], KEXP[b % 2][0:DB, P * h:P * h + P],
                                     DV[0:DB, SMP, P * h:P * h + P], start=True, stop=True)
                last.then_inc(s["outer_ready"], 1)
                pe.wait_ge(s["ns_ready"], b + 1)
                n = tile_no("st", b)
                for h in range(H):
                    last = pe.matmul(PS[0:DB, 7, P * h:P * h + P], RQM[:, h, b, :], SLOT[n % RING][:, P * h:P * h + P],
                                     start=False, stop=(b == DB - 1 and h == H - 1), skip_group_check=True)
                last.then_inc(s["tile_used_pe"], 1)

            pe.wait_ge(s["coef_ready"], 1)
            pe.wait_ge(s["ns_ready"], DB)
            for i in range(NBLK):
                if i:
                    pe.wait_ge(s["ret_sc_ready"], i)
                for h in range(H):
                    last = pe.matmul(PS[:, 0, P * h:P * h + P], DKT[:, h, P * i:P * i + P], DQT[:, h, P * i:P * i + P],
                                     start=True, stop=True)
                last.then_inc(s["ret_scores"], 1)
                pe.wait_ge(s["rqd_ready"], i + 1)
                pe.wait_ge(s["ret_sc_ready"], i + 1)
                if i:
                    pe.wait_ge(s["ret_state"], i)
                for h in range(H):
                    pe.matmul(PS[:, 2, P * h:P * h + P], RSC[:, P * h:P * h + P], DV[:, i, P * h:P * h + P],
                              start=True, stop=(i == 0))
                    if i:
                        pe.matmul(PS[:, 2, P * h:P * h + P], RQD[:, P * h:P * h + P], STATE[:, P * h:P * h + P],
                                  start=False, stop=True)
                    last = pe.matmul(PS[:, 3, P * h:P * h + P], RKD[:, P * h:P * h + P], DV[:, i, P * h:P * h + P],
                                     start=True, stop=True)
                last.then_inc(s["ret_out"], 1)

            pe.matmul(PS[0:DB, 6, :], zeros[:, 0:DB], const("decayT"), start=True, stop=False, skip_group_check=True)

            def weigh(b):
                pe.wait_ge(s["om_ready"], b + 1)
                pe.matmul(PS[0:DB, 6, :], cl[0:HC, b, :], OM[b % 2][0:HC, :], start=False, stop=(b == DB - 1),
                          skip_group_check=True).then_inc(s["dif_row_ready"], 1)

            for b in range(DB):
                if b >= 2:
                    pe.wait_ge(s["om_ready"], b - 1)
                for g in range(GRP):
                    n = tile_no("v", b, g)
                    tile_arrived(pe, n)
                    for j in range(TPR):
                        c0 = 128 * b + 32 * g + 8 * j
                        last = pe.matmul(PS[0:HC, 4 + b % 2, :], S[:, c0:c0 + HC], SLOT[n % RING][:, 512 * j:512 * j + 512],
                                         start=(g == 0 and j == 0), stop=False)
                    last.then_inc(s["tile_used_pe"], 1)
                pe.matmul(PS[0:HC, 4 + b % 2, :], sself_e[0:DB, b, :], DVS[0:DB, :], start=False, stop=True
                          ).then_inc(s["pv_done"], 1)
                if b >= 1:
                    weigh(b - 1)
            weigh(DB - 1)
            for b in range(NB):
                pe.wait_ge(s["mix_ready"], b + 1)
                r = ROWS[b]
                turn(N_MIX + b, pieces(RK[:, b, :], r) + pieces(DIF[:, b, :], r), r)

            def xt_ready(n):
                pe.wait_ge(s["xt_done"], n)

            xt_ready(N_CROSS)
            jobs("mix", X1)
            pe.wait_ge(s["mkr_loaded"], 16)
            for e in range(4):
                for k in range(2):
                    for m in range(NMEM):
                        last = pe.transpose(PS[:, e, MEM * k + P * m:MEM * k + P * m + P],
                                            MKR[:, m, P * (2 * e + k):P * (2 * e + k) + P], ident)
                last.then_inc(s["mkr_turned"], 1)
            pe.wait_ge(s["mkT_done"], 4)

            for b in range(NB):
                pe.wait_ge(s["xn_ready"], TURN + b + 1)
                turn(N_CROSS + b, pieces(XN[b % 2], ROWS[b]), ROWS[b])
            xt_ready(N_Q)
            jobs("mq", X1)
            for b in range(NB):
                pe.wait_ge(s["job_taken_act"], taken_by(first_job("mq") + NB + b)[1])
                turn(N_Q + b, pieces(QR[:, b, :], ROWS[b]), ROWS[b])
            xt_ready(N_O)

            pe.wait_ge(s["mv_loaded"], 16)
            for st in range(NBLK + 1):
                if st < NBLK:
                    if st >= 2:
                        pe.wait_ge(s["cexp_done"], st - 1)
                    for h in range(H):
                        for k in range(2):
                            last = pe.matmul(PS[:, 2 * (st % 2) + h // 2, MEM * (h % 2):MEM * (h % 2) + MEM],
                                             XT[:, 2 * h + k, X1 + P * st:X1 + P * st + P], MKT[:, 2 * h + k, :],
                                             start=(k == 0), stop=(k == 1))
                    last.then_inc(s["cs_ready"], 1)
                if st >= 1:
                    q = st - 1
                    pe.wait_ge(s["cexp_done"], q + 1)
                    if q >= 1:
                        pe.wait_ge(s["ceT_ready"], q)
                    for h in range(H):
                        for m in range(NMEM):
                            x = NMEM * h + m
                            last = pe.transpose(PS[:, 4 + x // 4, P * (x % 4):P * (x % 4) + P], CE[q % 2][:, h, P * m:P * m + P], ident)
                    last.then_inc(s["ce_turned"], 1)
                    pe.wait_ge(s["ceT_ready"], q + 1)
                    if q >= 1:
                        pe.wait_ge(s["co_taken"], q)
                    for h in range(H):
                        for m in range(NMEM):
                            x = P * (NMEM * h + m)
                            last = pe.matmul(PS[:, 6 + h // 2, MDH * (h % 2):MDH * (h % 2) + MDH], CET[q % 2][:, x:x + P],
                                             MV[:, m, MDH * h:MDH * h + MDH], start=(m == 0), stop=(m == NMEM - 1))
                    last.then_inc(s["co_ready"], 1)

            for b in range(DB):
                if b >= 2:
                    pe.wait_ge(s["tile_used_dve"], tile_used(tile_no("mk", b - 2))[1])
                for i in range(2):
                    last = pe.matmul(PS[:, 2 * (b % 2) + i, :], sel[0:DB, b, :], QR[0:DB, SMP, 512 * i:512 * i + 512],
                                     start=True, stop=True)
                last.then_inc(s["cqb_ready"], 1)
            pe.wait_ge(s["ccolmax_ready"], 1)
            pe.transpose(PS[0:32, 4, 0:P], ccol, ident).then_inc(s["ccolmax_turned"], 1)
            pe.wait_ge(s["cmaxdiag_ready"], 1)
            pe.matmul(PS[:, 5, 0:32], ones[0:32, :], cmd[0:32, :], start=True, stop=True).then_inc(s["cmaxbc_ready"], 1)
            pe.wait_ge(s["cesum_ready"], 1)
            for b in range(DB):
                last = pe.matmul(PS[0:H, 4, b:b + 1], cesum[:, H * b:H * b + H], ones[:, 0:1], start=True, stop=True)
            last.then_inc(s["cz_ready"], 1)
            pe.wait_ge(s["co_taken"], NBLK)
            pe.wait_ge(s["ccoef_ready"], 1)
            for i in range(2):
                pe.matmul(PS[0:DB, 6 + i, :], zeros[:, 0:DB], const("decayT"), start=True, stop=False, skip_group_check=True)

            def cweigh(b):
                pe.wait_ge(s["com_ready"], b + 1)
                for i in range(2):
                    last = pe.matmul(PS[0:DB, 6 + i, :], ccl[0:H, b, :], COM[b % 2][0:H, 512 * i:512 * i + 512],
                                     start=False, stop=(b == DB - 1), skip_group_check=True)
                last.then_inc(s["crow_ready"], 1)

            for b in range(DB):
                n = tile_no("mv", b)
                if b >= 2:
                    pe.wait_ge(s["com_ready"], b - 1)
                tile_arrived(pe, n)
                for i in range(2):
                    for j in range(NMEM):
                        last = pe.matmul(PS[0:H, 2 * (b % 2) + i, :], CS4[:, b, j, :],
                                         SLOT[n % RING][:, D * j + 512 * i:D * j + 512 * i + 512], start=(j == 0), stop=(j == 1))
                last.then_inc(s["cpv_done"], 1)
                if b >= 1:
                    cweigh(b - 1)
            cweigh(DB - 1)
            for b in range(NB):
                if b < NBLK:
                    pe.wait_ge(s["co_taken"], b + 1)
                else:
                    pe.wait_ge(s["crow_ready"], DB + 1)
                turn(N_O + b, pieces(QR[:, b, :], ROWS[b]), ROWS[b])
            xt_ready(N_FFN)
            jobs("mo", X1)

            for b in range(NB):
                pe.wait_ge(s["xn_ready"], TURN + NB + b + 1)
                turn(N_FFN + b, pieces(QR[:, b, :], ROWS[b]), ROWS[b])
            xt_ready(N_END)
            pe.wait_ge(s["sk_loaded"], 16)
            for e in range(4):
                for k in range(4):
                    last = pe.transpose(PS[:, e, P * k:P * k + P], SKR[:, 4 * e + k, :], ident)
                last.then_inc(s["sk_turned"], 1)
            pe.wait_ge(s["skT_done"], 4)

            def router_scores(x):
                pe.wait_ge(s["rqp_taken"], x + 1)
                if x >= 2:
                    pe.wait_ge(s["rs_taken"], x - 1)
                for b in range(NB):
                    r = ROWS[b]
                    last = pe.matmul(PS[0:r, 2 * (x % 2) + (b == SMP), (0 if b == SMP else NK * b):(NK if b == SMP else NK * b + NK)],
                                     QPT[x % 2][:, P * b:P * b + r], SKT[:, x, :], start=True, stop=True)
                last.then_inc(s["rs_ready"], 1)

            for x in range(NSUB):
                t = PQ0 + x // 4
                w_arrived(pe, t)
                if x >= 2:
                    pe.wait_ge(s["rqp_taken"], x - 1)
                for k in range(KD):
                    w = W[t % 2][:, k, P * (x % 4):P * (x % 4) + P]
                    pe.matmul(PS[:, 4 + x % 2, :], w, XT[:, k, X1:X1 + SEQ], start=(k == 0), stop=(k == KD - 1))
                    last = pe.matmul(PS[:, 6 + x % 2, 0:DB], w, XT[:, k, X1 + SEQ:X1 + TOK], start=(k == 0), stop=(k == KD - 1))
                last.then_inc(s["rqp_ready"], 1)
                if x >= 1:
                    router_scores(x - 1)
            router_scores(NSUB - 1)

            pe.wait_ge(s["sel_ready"], NB)
            pe.transpose(PS[:, 0, 0:DB], sidx_row[0:DB, :], ident[0:DB, 0:DB])
            pe.transpose(PS[:, 0, P:P + DB], GATE[0:DB, SMP, :], ident[0:DB, 0:DB]).then_inc(s["sidx_turned"], 1)
            pe.wait_ge(s["sel_ready"], NB + 1)
            for b in range(DB):
                if b >= 2:
                    pe.wait_ge(s["u_used"], b - 1)
                for i in range(2):
                    last = pe.matmul(PS[:, 2 * (b % 2) + i, :], sel[0:DB, b, :], QR[0:DB, SMP, 512 * i:512 * i + 512],
                                     start=True, stop=True)
                last.then_inc(s["xb_ready"], 1)
            pe.wait_ge(s["u_used"], DB)

            def open_group(bank, r):
                for i in range(2):
                    pe.matmul(PS[0:r, bank + i, :], zeros[:, 0:r], const("decayT"), start=True, stop=False, skip_group_check=True)

            open_group(6, DB)
            pe.wait_ge(s["smp_w"], 1)
            for b in range(DB):
                pe.wait_ge(uv_in[1][b], 16)
                for i in range(2):
                    last = pe.matmul(PS[0:DB, 6 + i, :], SWM[:, b, :], VSLOT[b][:, 512 * i:512 * i + 512], start=False,
                                     stop=(b == DB - 1), skip_group_check=True)
                last.then_inc(s["v_used"], 1)

            for blk in range(NBLK):
                bank = 2 * (blk % 2)
                if blk >= 2:
                    pe.wait_ge(s["y_ready"], blk)
                open_group(bank, P)
                with pe.Fori(0, NCH) as c:
                    for k in range(CHUNK):
                        pe.wait_ge(uv_in[1][k], c * 16 + 16 * (NCH * blk + 2))
                        pe.wait_ge(s["diag_ready"], c * CHUNK + (CHUNK * NCH * blk + k + 2))
                        for i in range(2):
                            last = pe.matmul(PS[:, bank + i, :], DIAG[k], VSLOT[k][:, 512 * i:512 * i + 512], start=False,
                                             stop=False, skip_group_check=True)
                        last.then_inc(s["v_used"], 1)


_INS = ["x_prompt", "x_sample", "mem_prompt", "cache_diff_k", "cache_diff_v", "page_table", "state_ret", "cache_mem_k",
        "cache_mem_v", "g_mix", "w_in", "w_out", "lam_q1", "lam_k1", "lam_q2", "lam_k2", "rel_bias", "g_cross", "g_mem",
        "w_mq", "w_mk", "w_mv", "w_mo", "g_ffn", "w_pq", "sub_keys", "peer_u", "peer_v", "g_final"]
_OUTS = [(1, SEQ, D), (DB, 1, D), (1, 1, SEQ, H, 2, DH), (1, 1, SEQ, H, 2 * DH), (1, 1, H, P, P), (1, 1, MEM, H, MDH),
         (1, 1, MEM, H, MDH), (1, DB, 1, H, 2, DH), (1, DB, 1, H, 2 * DH), (1, DB, H, P, P)]


def kernel(**inputs):
    import concourse.bacc as bacc
    from concourse.bass_utils import run_bass_kernel_spmd as run

    nc = bacc.Bacc("TRN2", target_bir_lowering=False, num_devices=1)
    arrays, args = {}, []
    for name in _INS:
        a = np.ascontiguousarray(inputs[name])
        arrays[f"in_{name}"] = a
        args.append(nc.dram_tensor(f"in_{name}", a.shape, mybir.dt.from_np(a.dtype), kind="ExternalInput").ap())
    arrays["in_consts"] = shape_constants()
    args.append(nc.dram_tensor("in_consts", (P, CW), F32, kind="ExternalInput").ap())
    args.append(nc.dram_tensor("bias_lines", (H * P * TL,), F32, kind="Internal").ap())
    for i, shape in enumerate(_OUTS):
        args.append(nc.dram_tensor(f"out_{i}", shape, F32, kind="ExternalOutput").ap())
    build(nc, *args)
    r = run(nc, [arrays], core_ids=[0])
    return tuple(r.results[0][f"out_{i}"] for i in range(len(_OUTS)))
```

```python
from contextlib import ExitStack
import math

import numpy as np
import concourse.bass as bass
from concourse import mybir

F32 = mybir.dt.float32
U32 = mybir.dt.uint32
I32 = mybir.dt.int32
ALU = mybir.AluOpType
ACT = mybir.ActivationFunctionType
AX = mybir.AxisListType

P = 128
D = 1024
KD = D // P
SEQ = 512
NBLK = SEQ // P
DB = 8
NB = NBLK + 1
SMP = NBLK
ROWS = [P] * NBLK + [DB]
TOK = SEQ + DB
MEM = 256
NMEM = MEM // P
H = 4
HC = 2 * H
DH = 64
MDH = D // H
PAGES = 16
PAGE = 128
PAST = PAGES * PAGE
PPG = 4
GRP = PAGES // PPG
TPR = PAGE // 32
NBUCKET = 32
EPS = 1e-6
NEG = -1e30
LAM_INIT = 0.8 - 0.6 * math.exp(-0.0)
SCALE = DH ** -0.5
MSCALE = MDH ** -0.5
PH = 8
NSUB = 2 * PH
NK = 128
TOPK = 16
NSEL = PH * TOPK
NEXP = NK * NK
CHUNK = 8

TL = 640
PIECES = [("ident", 128), ("ones", 128), ("zeros", 128), ("rot", NB * 256), ("decayT", H * P), ("qdec", H * P),
          ("kdec", H), ("gL", H), ("gam", H), ("sel", DB * P), ("mask8", DB * DB), ("hmask", 512),
          ("hmask4", D), ("line", TL), ("past", 6 * P), ("even", 1), ("odd", 1), ("dmask", DB * DB),
          ("part32", 1), ("iota16", TOPK)]
CO = {}
_o = 0
for _n, _w in PIECES:
    CO[_n] = (_o, _w)
    _o += _w
CW = _o


def shape_constants():
    c = np.zeros((P, CW), np.float32)

    def put(name, value, rows=P):
        o, w = CO[name]
        c[:rows, o:o + w] = np.asarray(value, np.float32).reshape(-1, w)

    p = np.arange(P)
    put("ident", np.eye(P))
    put("ones", np.ones((P, P)))
    half = P // 2
    inv = (np.float32(1.0) / (np.float32(10000.0) ** (np.arange(half, dtype=np.float32) / np.float32(half)))).astype(np.float32)
    rot = np.zeros((P, NB, 4, half), np.float32)
    for b in range(NB):
        pos = np.float32(PAST) * np.ones(P, np.float32) if b == SMP else (b * P + p).astype(np.float32)
        ang = (pos[:, None] * inv[None, :]).astype(np.float32).astype(np.float64)
        rot[:, b, 0] = np.cos(ang) * P ** -0.5
        rot[:, b, 1] = np.sin(ang) * P ** -0.5
        rot[:, b, 2] = np.cos(ang)
        rot[:, b, 3] = np.sin(ang)
    put("rot", rot)
    lg = np.log(1.0 - 2.0 ** (-5.0 - np.arange(H)))
    dif = p[None, :] - p[:, None]
    dec = np.where(dif[:, None, :] >= 0, np.exp(np.maximum(dif, 0)[:, None, :] * lg[None, :, None]), 0.0)
    put("decayT", dec)
    put("qdec", np.broadcast_to(np.exp((p[None, :] + 1.0) * lg[:, None])[None], (P, H, P)))
    put("kdec", np.exp((P - 1.0 - p)[:, None] * lg[None, :]))
    put("gL", np.broadcast_to(np.exp(P * lg)[None], (P, H)))
    put("gam", np.broadcast_to(np.exp(lg)[None], (P, H)))
    sel = np.zeros((DB, DB, P))
    for b in range(DB):
        sel[b, b] = 1.0
    put("sel", sel, DB)
    put("mask8", np.broadcast_to(np.eye(DB)[None], (P, DB, DB)))
    dm = np.zeros((DB, DB, DB))
    for b in range(DB):
        dm[b, b] = 1.0
    put("dmask", dm, DB)
    hc = np.arange(HC)
    put("hmask", hc[:, None] // 2 == np.arange(512)[None, :] // P, HC)
    put("hmask4", np.arange(H)[:, None] == np.arange(D)[None, :] // MDH, H)

    def bucket(n):
        n = np.maximum(n, 0)
        me = NBUCKET // 2
        nf = np.maximum(n, 1).astype(np.float32)
        large = me + (np.log(nf / np.float32(me)) / np.float32(math.log(128 / me)) * np.float32(NBUCKET - me)).astype(np.int32)
        return np.where(n < me, n, np.minimum(large, NBUCKET - 1))

    rel = SEQ - 1 - np.arange(TL)
    line = np.zeros((NBUCKET + 1, TL))
    for m in range(TL):
        line[bucket(rel[m:m + 1])[0] if rel[m] >= 0 else NBUCKET, m] = 1.0
    put("line", line, NBUCKET + 1)
    past = np.zeros((NBUCKET, 6, P))
    for j in range(TPR):
        pos = ((GRP - 1) * PPG + p // 32) * PAGE + (p % 32) * TPR + j
        past[bucket(PAST - pos), j, p] = 1.0
    past[NBUCKET - 1, 4] = 1.0
    past[0, 5] = 1.0
    put("past", past, NBUCKET)
    put("even", hc % 2 == 0, HC)
    put("odd", hc % 2 == 1, HC)
    put("part32", p % 32)
    put("iota16", np.broadcast_to(np.arange(TOPK)[None], (P, TOPK)))
    return c


LAYOUT = [("const", 6912), ("misc", 1024), ("dvs", 512), ("xt", 8 * 776), ("w", 2 * 4096), ("r1", 5120), ("r2", 7680),
          ("r3", 2560), ("ring", 3 * 2048), ("s", 1104), ("toe", 2048), ("g", 1024), ("t", 4096)]
BASE = {}
_o = 0
for _n, _w in LAYOUT:
    BASE[_n] = _o
    _o += _w
SBW = _o
KEYS_AHEAD = 16
RING = 3
PSUM_TURN, PSUM_JOB = 0, 4

WTILES = ([("w_in", 512 * c, k) for c, k in ((4, "dq"), (5, "dk"), (6, "dv"))]
          + [("w_mk", 512 * i, "mem") for i in range(2)] + [("w_mv", 512 * i, "mem") for i in range(2)]
          + [("w_in", 512 * c, k) for c, k in ((3, "rg"), (0, "rq"), (1, "rk"), (2, "rv"))]
          + [("w_out", 512 * i, "mix") for i in range(2)] + [("w_mq", 512 * i, "mq") for i in range(2)]
          + [("w_mo", 512 * i, "mo") for i in range(2)] + [("w_pq", 512 * i, "pq") for i in range(4)])
JOBS = [(t, u) for t, (_, _, k) in enumerate(WTILES) if k != "pq" for u in range(NMEM if k == "mem" else NB)]
PQ0 = len(WTILES) - 4
BY_DVE = ("rq", "rk", "mix", "mo")


def job_kind(j):
    return WTILES[JOBS[j][0]][2]


def first_job(kind):
    return next(j for j in range(len(JOBS)) if job_kind(j) == kind)


def taken_by(j):
    dve = job_kind(j) in BY_DVE
    return dve, sum((job_kind(i) in BY_DVE) == dve for i in range(j + 1))


TILES = ([("k", b, g) for b in range(DB) for g in range(GRP)] + [("st", b, 0) for b in range(DB)]
         + [("v", b, g) for b in range(DB) for g in range(GRP)] + [("mk", b, 0) for b in range(DB)]
         + [("mv", b, 0) for b in range(DB)])
TILE_BY_DVE = ("k", "mk")


def tile_no(kind, b, g=0):
    return TILES.index((kind, b, g))


def tile_used(n):
    dve = TILES[n][0] in TILE_BY_DVE
    return dve, sum((TILES[i][0] in TILE_BY_DVE) == dve for i in range(n + 1))


SEMS = """ident_loaded sq_saved const_loaded small_loaded mem_loaded x_loaded gains_loaded w_loaded0 w_loaded1
        tile_in0 tile_in1 tile_in2 tile_used_dve tile_used_pe ss_cleared sumsq_done inv_done rstd_done xn_ready
        turned xt_done job_ready job_taken_dve job_taken_act vstep astep mem_stored0 mem_stored1 mem_stored2
        mem_stored3 new_kv_stored lam_sums lam_exp lam_ready line_cols line_ps line_row line_stored toe_loaded
        past_ps past_ready kvidx_ready rows_turned rowsT_done scores_ready sc_biased nmax_ready exp_done w_ready
        wmat_turned wT_ready av_done dif_taken srow_saved qb_ready s_scored colmax_ready colmax_turned maxdiag_ready
        maxbc_ready sarg_ready sexp_done esum_ready z_ready coef_ready pv_done om_ready dif_row_ready rqd_ready
        ret_scores ret_sc_ready ret_out ret_state ret_rows rqm_ready kexp_ready outer_ready ns_ready ns_stored0
        ns_stored1 ns_stored2 state_stored hsq_ready hrstd_done mix_ready x_again done_stored final_ready mkr_loaded
        mkr_turned mkT_done mv_loaded cs_ready cmax_ready cexp_done ce_turned ceT_ready co_ready co_taken cqb_ready
        cs_scored ccolmax_ready ccolmax_turned cmaxdiag_ready cmaxbc_ready csexp_done cesum_ready cz_ready
        ccoef_ready cpv_done com_ready crow_ready sk_loaded sk_turned skT_done rqp_ready rqp_taken rs_ready rs_taken
        sel_ready sidx_turned xb_ready gelu_done weight_ready diag_ready y_ready u_in0 u_in1 u_in2 u_in3 u_in4 u_in5
        u_in6 u_in7 v_in0 v_in1 v_in2 v_in3 v_in4 v_in5 v_in6 v_in7 u_used v_used idx_copied smp_w select_steps""".split()


def build(nc, x_prompt, x_sample, mem_prompt, cache_diff_k, cache_diff_v, page_table, state_ret, cache_mem_k,
          cache_mem_v, g_mix, w_in, w_out, lam_q1, lam_k1, lam_q2, lam_k2, rel_bias, g_cross, g_mem, w_mq, w_mk,
          w_mv, w_mo, g_ffn, w_pq, sub_keys, peer_u, peer_v, g_final, consts, line_dram,
          y_prompt, y_sample, new_k_p, new_v_p, state_p, mk_p, mv_p, new_k_s, new_v_s, state_s):
    weights = {"w_mk": w_mk, "w_mv": w_mv, "w_in": w_in, "w_out": w_out, "w_mq": w_mq, "w_mo": w_mo, "w_pq": w_pq}
    with ExitStack() as ctx:
        A = ctx.enter_context(nc.sbuf_tensor("arena", [P, SBW], F32))
        PS = ctx.enter_context(nc.psum_tensor("ps", [P, 8, 512], F32))
        s = {n: ctx.enter_context(nc.semaphore(n)) for n in SEMS}

        def at(region, off, n):
            return A[:, BASE[region] + off:BASE[region] + off + n]

        def const(name):
            return at("const", CO[name][0], CO[name][1])

        small_used = [0]

        def small(n):
            small_used[0] += n
            assert small_used[0] <= 1024
            return at("misc", small_used[0] - n, n)

        ident, ones, zeros = const("ident"), const("ones"), const("zeros")
        rot = const("rot").rearrange("p (b t d) -> p b t d", b=NB, t=4)
        sel = const("sel").rearrange("p (b m) -> p b m", b=DB)
        mask8 = const("mask8").rearrange("p (b j) -> p b j", b=DB)
        dmask = const("dmask").rearrange("p (b j) -> p b j", b=DB)

        XT = at("xt", 0, 8 * 776).rearrange("p (k t) -> p k t", k=KD)
        W = [at("w", 4096 * i, 4096).rearrange("p (k n) -> p k n", k=KD) for i in range(2)]
        G = at("g", 0, 1024)
        GM = at("t", 0, 1024)
        XN = [at("t", 2048 + 1024 * i, 1024) for i in range(2)]
        X0 = at("r1", 0, 7 * 1024).rearrange("p (u d) -> p u d", u=7)
        DQT = at("r1", 0, H * TOK).rearrange("p (h t) -> p h t", h=H)
        DKT = at("r1", 2560, H * TOK).rearrange("p (h t) -> p h t", h=H)
        HR = at("r1", 0, NB * D).rearrange("p (b d) -> p b d", b=NB)
        DV = at("r2", 0, 2560).rearrange("p (b d) -> p b d", b=NB)
        RK = at("r2", 2560, 2560).rearrange("p (b d) -> p b d", b=NB)
        RG = at("r2", 5120, 2560).rearrange("p (b d) -> p b d", b=NB)
        QR = at("r2", 0, NB * D).rearrange("p (b d) -> p b d", b=NB)
        DIF = at("r3", 0, 2560).rearrange("p (b d) -> p b d", b=NB)
        MSTAGE = [at("r2", 2560 + 512 * i, 512) for i in range(4)]
        SLOT = [at("ring", 2048 * i, 2048) for i in range(RING)]
        S = at("s", 0, 1024)
        TOE = at("toe", 0, 2048).rearrange("p (h c) -> p h c", h=H)
        DVS = at("dvs", 0, 512)
        SRQ, SRK = at("g", 0, 512), at("g", 512, 512)
        SC = [at("t", 1024 * i, 1024).rearrange("p (c n) -> p c n", c=2) for i in range(2)]
        WM = [at("t", 2048 + 512 * i, 512) for i in range(2)]
        WT = [at("t", 3072 + 512 * i, 512) for i in range(2)]
        RQD, RKD = at("t", 0, 512), at("t", 512, 512)
        RSC = at("t", 1024, 512)
        STATE = at("t", 1536, 512)
        ROT_A, ROT_B = at("t", 2048, 512), at("t", 2560, 512)
        KEXP = [at("t", 2048 + 512 * i, 512) for i in range(2)]
        RQM = at("t", 3072, H * DB * DB).rearrange("p (h b j) -> p h b j", h=H, b=DB)
        OM = [at("t", 3072 + 512 * i, 512) for i in range(2)]
        SQ = [at("t", 2048 * i, 2048) for i in range(2)]

        ss = [small(8) for _ in range(4)]
        rstd = [small(8) for _ in range(4)]
        lamv = small(256)
        lsum, lexp, nlam = small(2), small(2), small(1)
        tab = small(H)
        pt_f, kv_idx = small(32), small(32)
        nmx, zsum = small(4), small(4)
        bias_s = small(24).rearrange("p (j h) -> p j h", j=6)
        sself, sself_e = small(HC), small(DB * HC).rearrange("p (b c) -> p b c", b=DB)
        sself_m = small(DB * HC).rearrange("p (b c) -> p b c", b=DB)
        colmax, mcol = small(64), small(1)
        esum = small(DB * HC).rearrange("p (b c) -> p b c", b=DB)
        rz, coef = small(DB), small(1)
        cl = small(DB * DB).rearrange("p (b j) -> p b j", b=DB)
        hss = small(NB * 8).rearrange("p (b h) -> p b h", b=NB)
        mdiag = small(64)
        TABB = at("t", 1024, 512).rearrange("p (h m) -> p h m", h=H)
        PTAB = at("t", 1536, DB * PAGES)
        LROW = at("ring", 0, H * TL).rearrange("p (h c) -> p h c", h=H)
        BFULL = at("t", 1536, 128).rearrange("p (x c) -> p x c", x=16)

        k_rows = cache_diff_k.rearrange("l g (r t) h c d -> (l g r) (t h c d)", t=TPR)
        v_rows = cache_diff_v.rearrange("l g (r t) h d -> (l g r) (t h d)", t=TPR)
        mk_rows = cache_mem_k.rearrange("l b (p t) h d -> (l b) p (t h d)", t=NMEM)
        mv_rows = cache_mem_v.rearrange("l b (p t) h d -> (l b) p (t h d)", t=NMEM)
        mem_out = {"w_mk": mk_p.rearrange("l b (u p) h d -> (l b u) p (h d)", p=P),
                   "w_mv": mv_p.rearrange("l b (u p) h d -> (l b u) p (h d)", p=P)}
        kp_out = new_k_p.rearrange("l b (u p) h c d -> (l b u) p (h c d)", p=P)
        vp_out = new_v_p.rearrange("l b (u p) h d -> (l b u) p (h d)", p=P)
        ks_out = new_k_s.rearrange("l b t h c d -> (l b t) (h c d)")
        vs_out = new_v_s.rearrange("l b t h d -> (l b t) (h d)")
        xp = x_prompt.rearrange("b (u p) d -> (b u) p d", p=P)
        yp = y_prompt.rearrange("b (u p) d -> (b u) p d", p=P)
        line_rows = line_dram[0:H * P * TL].rearrange("(h p c) -> p h c", h=H, p=P)

        TURN = 7
        X1 = NMEM * P
        N_MIX, N_CROSS, N_Q, N_O, N_FFN, N_END = (TURN + NB * i for i in range(6))

        def turn_banks(n):
            return PS[:, 2 * (n % 2):2 * (n % 2) + 2, :].rearrange("p a c -> p (a c)")

        mem_jobs = [j for j in range(len(JOBS)) if job_kind(j) == "mem"]
        extra_jobs = [j for j in range(len(JOBS)) if job_kind(j) in ("mem", "rg")]

        def w_arrived(eng, t):
            eng.wait_ge((s["w_loaded0"], s["w_loaded1"])[t % 2], 16 * (t // 2 + 1))

        tile_in = (s["tile_in0"], s["tile_in1"], s["tile_in2"])
        mem_stored = (s["mem_stored0"], s["mem_stored1"], s["mem_stored2"], s["mem_stored3"])
        ns_stored = (s["ns_stored0"], s["ns_stored1"], s["ns_stored2"])

        def tile_arrived(eng, n):
            eng.wait_ge(tile_in[n % RING], 16 * (n // RING + 1))

        NSTORES = 2 * NB

        MKR = at("t", 0, 2048).rearrange("p (m d) -> p m d", m=NMEM)
        MKT = at("toe", 0, 2048).rearrange("p (k m) -> p k m", k=KD)
        MV = at("r3", 0, 2048).rearrange("p (m d) -> p m d", m=NMEM)
        CE = [at("t", 1024 * i, 1024).rearrange("p (h m) -> p h m", h=H) for i in range(2)]
        CET = [at("t", 2048 + 1024 * i, 1024) for i in range(2)]
        COM = [at("t", 1024 * i, 1024) for i in range(2)]
        CS = at("s", 0, DB * NMEM * H)
        CS4 = CS.rearrange("p (b j h) -> p b j h", b=DB, j=NMEM)
        cneg, csum = small(2 * H), small(2 * H)
        ccol, cesum = at("s", 128, DB * H), at("s", 160, DB * H)
        cmd = at("s", 192, DB * H)
        cmx = at("s", 224, 1)
        crz = at("s", 232, DB)
        ccl = at("s", 240, DB * DB).rearrange("p (b j) -> p b j", b=DB)
        SKR = at("t", 0, 2048).rearrange("p (x d) -> p x d", x=NSUB)
        SKT = at("toe", 0, 2048).rearrange("p (x k) -> p x k", x=NSUB)
        QPT = [at("t", 2048 + TOK * i, TOK) for i in range(2)]
        WORK = at("t", 3200, NB * NK).rearrange("p (b k) -> p b k", b=NB)
        TV = at("r2", 5120, NB * NSUB * TOPK).rearrange("p (b x k) -> p b x k", b=NB, x=NSUB)
        TI = at("r3", 1280, NB * NSUB * TOPK).rearrange("p (b x k) -> p b x k", b=NB, x=NSUB)
        CAND, CAND2 = at("t", 0, 256), at("t", 256, 256)
        HOT = at("t", 512, 512)
        BV, BI = at("t", 1024, TOPK), at("t", 1040, TOPK)
        AF, CF, AU, CU = (at("t", 1056 + TOPK * i, TOPK) for i in range(4))
        TIF, GAC = at("t", 1120, 2 * TOPK), at("t", 1152, 2 * TOPK)
        bsum, bmax = at("t", 1184, PH), at("t", 1192, PH)
        SELECT_LINKS = 12
        IDX = at("r3", 0, NB * NSEL).rearrange("p (b k) -> p b k", b=NB)
        GATE = at("r3", 640, NB * NSEL).rearrange("p (b k) -> p b k", b=NB)
        sidx_row = at("t", 3968, NSEL)
        SIDX, SGATE = at("t", 1200, DB), at("t", 1208, DB)
        sdot, sgl = at("t", 1216, DB), at("t", 1224, DB)
        SWM = at("t", 1232, DB * DB).rearrange("p (b j) -> p b j", b=DB)
        dots, gl, WCH = at("t", 1296, CHUNK), at("t", 1304, CHUNK), at("t", 1312, CHUNK)
        ICH = [at("t", 1320 + CHUNK * i, CHUNK) for i in range(2)]
        USLOT = [at("xt", 1024 * i, 1024) for i in range(6)] + [at("w", 2048 + 1024 * i, 1024) for i in range(2)]
        VSLOT = [at("ring", 1024 * i, 1024) for i in range(CHUNK)]
        DIAG = [at("t", 2048 + 128 * i, 128) for i in range(CHUNK)]
        uv_in = ((s["u_in0"], s["u_in1"], s["u_in2"], s["u_in3"], s["u_in4"], s["u_in5"], s["u_in6"], s["u_in7"]),
                 (s["v_in0"], s["v_in1"], s["v_in2"], s["v_in3"], s["v_in4"], s["v_in5"], s["v_in6"], s["v_in7"]))
        NCH = NSEL // CHUNK

        block = ctx.enter_context(nc.Block())

        @block.sync
        def _(sp):
            m = mem_prompt.rearrange("b (u p) d -> p (b u) d", p=P)
            sp.dma_start(X0[:, 0:NMEM, :], m).then_inc(s["mem_loaded"], 16)
            sp.dma_start(X0[:, NMEM:NMEM + NBLK, :], x_prompt.rearrange("b (u p) d -> p (b u) d", p=P)).then_inc(s["x_loaded"], 16)
            sp.dma_start(X0[0:DB, NMEM + SMP, :], x_sample.rearrange("b t d -> (b t) d")).then_inc(s["x_loaded"], 16)
            sp.dma_start(at("const", 0, 3 * P), consts[:, 0:3 * P]).then_inc(s["ident_loaded"], 16)
            sp.dma_start(GM, g_mem[0].partition_broadcast(P)).then_inc(s["mem_loaded"], 16)
            sp.dma_start(G, g_mix[0].partition_broadcast(P)).then_inc(s["gains_loaded"], 16)
            for i, v in enumerate((lam_q1, lam_k1, lam_q2, lam_k2)):
                sp.dma_start(lamv[:, 64 * i:64 * i + 64], v[0].partition_broadcast(P)).then_inc(s["small_loaded"], 16)
            sp.dma_start(tab[0:NBUCKET, :], rel_bias).then_inc(s["small_loaded"], 16)
            sp.dma_start(PTAB.bitcast(I32), page_table.rearrange("b g -> (b g)").partition_broadcast(P)
                         ).then_inc(s["small_loaded"], 16)
            for t, (name, c0, kind) in enumerate(WTILES):
                if t == 1:
                    sp.dma_start(at("const", 3 * P, CW - 3 * P), consts[:, 3 * P:CW]).then_inc(s["const_loaded"], 16)
                if t == 13:
                    sp.wait_ge(s["hsq_ready"], 1)
                    sp.wait_ge(s["state_stored"], 16)
                    sp.dma_start(HR[:, 0:NBLK, :], x_prompt.rearrange("b (u p) d -> p (b u) d", p=P)).then_inc(s["x_again"], 16)
                    sp.dma_start(HR[0:DB, SMP, :], x_sample.rearrange("b t d -> (b t) d")).then_inc(s["x_again"], 16)
                    sp.dma_start(G, g_cross[0].partition_broadcast(P)).then_inc(s["gains_loaded"], 16)
                    for i in range(4):
                        sp.wait_ge(mem_stored[i], 32)
                    sp.dma_start(MKR, mk_p.rearrange("l b (u p) h d -> p (l b u) (h d)", p=P)).then_inc(s["mkr_loaded"], 16)
                    sp.wait_ge(s["turned"], N_CROSS)
                    sp.dma_start(MV, mv_p.rearrange("l b (u p) h d -> p (l b u) (h d)", p=P)).then_inc(s["mv_loaded"], 16)
                if t == 15:
                    sp.wait_ge(s["xn_ready"], TURN + NB)
                    sp.dma_start(G, g_ffn[0].partition_broadcast(P)).then_inc(s["gains_loaded"], 16)
                if t == 18:
                    sp.wait_ge(s["crow_ready"], DB + 1)
                    sp.dma_start(SKR, sub_keys[0].rearrange("h c k d -> k (h c) d")).then_inc(s["sk_loaded"], 16)
                if t >= 2:
                    last_job = max(j for j in range(len(JOBS)) if JOBS[j][0] <= t - 2) if t - 2 < PQ0 else 0
                    if t - 2 < PQ0:
                        sp.wait_ge(s["job_ready"], last_job + 1)
                    else:
                        sp.wait_ge(s["rqp_ready"], 4 * (t - 1 - PQ0))
                w = weights[name][0].rearrange("(k p) n -> p k n", p=P)
                sp.dma_start(W[t % 2], w[:, :, c0:c0 + 512]).then_inc((s["w_loaded0"], s["w_loaded1"])[t % 2], 16)

            sp.wait_ge(s["xn_ready"], TURN + 2 * NB)
            sp.dma_start(G, g_final.partition_broadcast(P)).then_inc(s["gains_loaded"], 16)
            for b in range(NB):
                sp.wait_ge(s["final_ready"], b + 1)
                if b == SMP:
                    sp.dma_start(y_sample.rearrange("b t d -> (b t) d"), QR[0:DB, b, :]).then_inc(s["done_stored"], 16)
                else:
                    sp.dma_start(yp[b], QR[:, b, :]).then_inc(s["done_stored"], 16)
            sp.wait_ge(s["done_stored"], 16 * NB)

        @block.gpsimd
        def _(pool):
            pool.wait_ge(s["kvidx_ready"], 1)
            for n, (kind, b, g) in enumerate(TILES):
                if n >= RING:
                    dve, c = tile_used(n - RING)
                    if TILES[n - RING][0] == "mv":
                        pool.wait_ge(s["cpv_done"], TILES[n - RING][1] + 1)
                    else:
                        pool.wait_ge(s["tile_used_dve"] if dve else s["tile_used_pe"], c)
                    if TILES[n - RING][0] == "st":
                        prior = [m for m in range(n - RING + 1) if TILES[m][0] == "st" and m % RING == n % RING]
                        pool.wait_ge(ns_stored[n % RING], 16 * len(prior))
                else:
                    pool.wait_ge(s["line_stored"], 16)
                if kind in ("k", "v"):
                    pool.indirect_dma_start(SLOT[n % RING], None, k_rows if kind == "k" else v_rows,
                                            bass.IndirectOffsetOnAxis(kv_idx[:, b * GRP + g:b * GRP + g + 1].bitcast(U32), 0)
                                            ).then_inc(tile_in[n % RING], 16)
                elif kind == "st":
                    pool.dma_start(SLOT[n % RING][:, 0:512].rearrange("p (h e) -> p h e", h=H),
                                   state_ret[0, b].rearrange("h d e -> d h e")).then_inc(tile_in[n % RING], 16)
                else:
                    pool.dma_start(SLOT[n % RING], (mk_rows if kind == "mk" else mv_rows)[b]).then_inc(tile_in[n % RING], 16)

            def gather(slot, which, idx):
                pool.indirect_dma_start((USLOT, VSLOT)[which][slot], None, (peer_u, peer_v)[which][0],
                                        bass.IndirectOffsetOnAxis(idx.bitcast(U32), 0)).then_inc(uv_in[which][slot], 16)

            pool.wait_ge(s["skT_done"], 4)
            for blk in range(NBLK):
                pool.wait_ge(s["sel_ready"], blk + 1)
                with pool.Fori(0, NCH // 2) as c2:
                    for half in range(2):
                        pool.tensor_copy(ICH[half].bitcast(U32), IDX[:, blk, bass.ds(c2 * (2 * CHUNK) + half * CHUNK, CHUNK)].bitcast(U32)
                                         ).then_inc(s["idx_copied"], 1)
                        pool.wait_ge(s["idx_copied"], c2 * 2 + (NCH * blk + half + 1))
                        for which, used in ((0, s["u_used"]), (1, s["v_used"])):
                            for k in range(CHUNK):
                                pool.wait_ge(used, c2 * (2 * CHUNK) + (CHUNK * (NCH * blk + half) + k + 1))
                                pool.nop(nofuse=True)
                                gather(k, which, ICH[half][:, k:k + 1])
            pool.wait_ge(s["sel_ready"], NB + 1)
            for which, used in ((0, s["u_used"]), (1, s["v_used"])):
                for b in range(DB):
                    pool.wait_ge(used, CHUNK * NCH * NBLK + b + 1)
                    gather(b, which, SIDX[:, b:b + 1])

        @block.scalar
        def _(act):
            steps = [0]

            def link(ins):
                steps[0] += 1
                ins.then_inc(s["astep"], 1)
                act.wait_ge(s["astep"], steps[0])

            def sumsq(stage, rows_of, junk):
                if stage == 0:
                    act.wait_ge(s["ss_cleared"], 1)
                last = None
                for u, (r, src) in enumerate(rows_of):
                    last = act.activation(junk[0:r, :], src, ACT.Square, accum_out=ss[stage][0:r, u:u + 1])
                    if u < len(rows_of) - 1:
                        link(last)
                last.then_inc(s["sumsq_done"], 1)
                act.wait_ge(s["inv_done"], stage + 1)
                act.activation(rstd[stage], rstd[stage], ACT.Sqrt).then_inc(s["rstd_done"], 1)

            def xt_copy(n, b0):
                r = P if n < 6 or (n - TURN) % NB != SMP else DB
                if n == 6:
                    r = DB
                act.wait_ge(s["turned"], n + 1)
                act.copy(XT[:, :, P * b0:P * b0 + r],
                         turn_banks(n).rearrange("p (k t) -> p k t", k=KD)[:, :, 0:r]).then_inc(s["xt_done"], 1)

            def job_rows(j):
                return P if job_kind(j) == "mem" else ROWS[JOBS[j][1]]

            def take(j, dst):
                act.wait_ge(s["job_ready"], j + 1)
                kind = job_kind(j)
                act.activation(dst, PS[0:job_rows(j), PSUM_JOB + j % 2, :], ACT.Silu if kind == "rg" else ACT.Copy
                               ).then_inc(s["job_taken_act"], 1)

            act.wait_ge(s["mem_loaded"], 32)
            act.wait_ge(s["x_loaded"], 32)
            sumsq(0, [(P, X0[:, u, :]) for u in range(6)] + [(DB, X0[0:DB, 6, :])],
                  PS[:, 0:2, :].rearrange("p a c -> p (a c)"))
            for n in range(TURN):
                xt_copy(n, n)
            for h in range(H):
                act.wait_ge(s["line_ps"], h + 1)
                act.copy(LROW[:, h, 0:512], PS[:, 6, :]).then_inc(s["line_cols"], 1)
                act.copy(LROW[:, h, 512:TL], PS[:, 7, 0:TL - 512]).then_inc(s["line_row"], 1)
            act.wait_ge(s["line_row"], H)
            act.wait_ge(s["line_cols"], H)
            act.dma_start(line_rows, LROW).then_inc(s["line_stored"], 16)
            act.wait_ge(s["line_stored"], 16)
            for h in range(H):
                o = h * P * TL + P - 1
                act.dma_start(TOE[:, h, :], line_dram[o:o + P * (TL - 1)].rearrange("(p c) -> p c", p=P)[:, 0:512]
                              ).then_inc(s["toe_loaded"], 16)
            act.wait_ge(s["lam_sums"], 1)
            act.activation(lexp, lsum, ACT.Exp).then_inc(s["lam_exp"], 1)

            def take_extra(j):
                t, u = JOBS[j]
                if job_kind(j) == "rg":
                    take(j, RG[0:ROWS[u], u, :])
                    return
                name, c0, _ = WTILES[t]
                i = j - mem_jobs[0]
                if i >= 4:
                    act.wait_ge(mem_stored[i % 4], 16 * (i // 4))
                take(j, MSTAGE[i % 4])
                taken(j)
                act.dma_start(mem_out[name][u][:, c0:c0 + 512], MSTAGE[i % 4]).then_inc(mem_stored[i % 4], 16)

            def taken(j):
                act.wait_ge(s["job_taken_act"], taken_by(j)[1])

            for b in range(NB):
                take(first_job("dq") + b, RK[0:ROWS[b], b, :])
            for kind, dst, outp, outs in (("dk", RG, kp_out, ks_out), ("dv", DV, vp_out, vs_out)):
                for b in range(NB):
                    j = first_job(kind) + b
                    take(j, dst[0:ROWS[b], b, :])
                    taken(j)
                    act.dma_start(outs if b == SMP else outp[b], dst[0:ROWS[b], b, :]).then_inc(s["new_kv_stored"], 16)

            act.wait_ge(s["new_kv_stored"], 16 * NSTORES)
            act.wait_ge(s["srow_saved"], 1)
            for st in range(NBLK * H + 1):
                if st < NBLK * H:
                    n = P * (st // H + 1)
                    act.wait_ge(s["nmax_ready"], st + 1)
                    for c in range(2):
                        last = act.activation(SC[st % 2][:, c, 0:n], SC[st % 2][:, c, 0:n], ACT.Exp,
                                              bias=nmx[:, 2 * (st % 2) + c:2 * (st % 2) + c + 1],
                                              accum_out=zsum[:, 2 * (st % 2) + c:2 * (st % 2) + c + 1])
                    last.then_inc(s["exp_done"], 1)
                if st < len(extra_jobs):
                    take_extra(extra_jobs[st])
                if st >= 1:
                    q = st - 1
                    n = P * (q // H + 1)
                    act.wait_ge(s["wmat_turned"], q + 1)
                    if q >= 2:
                        act.wait_ge(s["av_done"], q - 1)
                    act.copy(WT[q % 2][:, 0:n], PS[:, 6, 0:n]).then_inc(s["wT_ready"], 1)
                    if q % H == H - 1:
                        act.wait_ge(s["av_done"], q + 1)
                        act.copy(DIF[:, q // H, :], PS[:, 7, :]).then_inc(s["dif_taken"], 1)

            act.wait_ge(s["rowsT_done"], 3 * NB)
            for b in range(NB):
                take(first_job("rv") + b, DV[0:ROWS[b], b, :])

            act.wait_ge(s["s_scored"], 1)
            act.activation(S, S, ACT.Exp).then_inc(s["sexp_done"], 1)
            act.wait_ge(s["sarg_ready"], 1)
            act.activation(sself_e[0:DB], sself_e[0:DB], ACT.Exp).then_inc(s["sexp_done"], 1)

            for b in range(DB):
                n = tile_no("st", b)
                act.wait_ge(s["ns_ready"], b + 1)
                act.dma_start(state_s[0, b].rearrange("h d e -> d h e"),
                              SLOT[n % RING][:, 0:512].rearrange("p (h e) -> p h e", h=H)).then_inc(ns_stored[n % RING], 16)
            act.wait_ge(s["ret_state"], NBLK)
            act.dma_start(state_p[0, 0].rearrange("h d e -> d h e"), STATE.rearrange("p (h e) -> p h e", h=H)
                          ).then_inc(s["state_stored"], 16)
            act.wait_ge(s["hsq_ready"], 1)
            act.activation(hss, hss, ACT.Sqrt).then_inc(s["hrstd_done"], 1)
            for b in range(NB):
                xt_copy(N_MIX + b, NMEM + b)
            act.wait_ge(s["job_taken_dve"], taken_by(first_job("mq") - 1)[1])
            junk = PS[:, 6:8, :].rearrange("p a c -> p (a c)")
            h_rows = [(ROWS[b], HR[0:ROWS[b], b, :]) for b in range(NB)]
            sumsq(1, h_rows, junk)
            for b in range(NB):
                xt_copy(N_CROSS + b, NMEM + b)
            for j in [j for j in range(len(JOBS)) if job_kind(j) == "mq"]:
                t, b = JOBS[j]
                c0 = WTILES[t][1]
                take(j, QR[0:ROWS[b], b, c0:c0 + 512])
            for b in range(NB):
                xt_copy(N_Q + b, NMEM + b)

            for st in range(NBLK + 1):
                if st < NBLK:
                    act.wait_ge(s["cmax_ready"], st + 1)
                    if st >= 2:
                        act.wait_ge(s["ce_turned"], st - 1)
                    for h in range(H):
                        z = H * (st % 2) + h
                        last = act.activation(CE[st % 2][:, h, :], PS[:, 2 * (st % 2) + h // 2, MEM * (h % 2):MEM * (h % 2) + MEM],
                                              ACT.Exp, bias=cneg[:, z:z + 1], scale=MSCALE, accum_out=csum[:, z:z + 1])
                    last.then_inc(s["cexp_done"], 1)
                if st >= 1:
                    q = st - 1
                    act.wait_ge(s["ce_turned"], q + 1)
                    if q >= 2:
                        act.wait_ge(s["co_ready"], q - 1)
                    act.copy(CET[q % 2], PS[:, 4:6, :].rearrange("p a c -> p (a c)")).then_inc(s["ceT_ready"], 1)
            act.wait_ge(s["cs_scored"], 1)
            act.activation(CS, CS, ACT.Exp, scale=MSCALE).then_inc(s["csexp_done"], 1)
            for b in range(NB):
                xt_copy(N_O + b, NMEM + b)
            act.wait_ge(s["job_taken_dve"], taken_by(len(JOBS) - 1)[1])
            sumsq(2, h_rows, junk)
            for b in range(NB):
                xt_copy(N_FFN + b, NMEM + b)

            for x in range(NSUB):
                act.wait_ge(s["rqp_ready"], x + 1)
                if x >= 2:
                    act.wait_ge(s["rs_ready"], x - 1)
                bank = 4 + 2 * (x % 2)
                act.copy(QPT[x % 2].rearrange("p (a t) -> p a t", a=2), PS[:, bank:bank + 2, 0:TOK // 2]).then_inc(s["rqp_taken"], 1)
            def gate_exp(b):
                act.wait_ge(s["sarg_ready"], 2 + b)
                act.activation(GATE[0:ROWS[b], b, :], GATE[0:ROWS[b], b, :], ACT.Exp).then_inc(s["sexp_done"], 1)

            gate_exp(0)

            for blk in range(NBLK):
                with act.Fori(0, NCH) as c:
                    act.wait_ge(s["u_used"], c * CHUNK + CHUNK * (NCH * blk + 2))
                    act.activation(gl, dots, ACT.Gelu).then_inc(s["gelu_done"], 1)
                    act.wait_ge(s["weight_ready"], c + (NCH * blk + 1))
                    for k in range(CHUNK):
                        act.wait_ge(s["v_used"], c * CHUNK + (CHUNK * NCH * blk + k + 1))
                        act.activation(DIAG[k], ident, ACT.Copy, scale=WCH[:, k:k + 1]).then_inc(s["diag_ready"], 1)
                gate_exp(blk + 1)
            act.wait_ge(s["u_used"], CHUNK * (NCH * NBLK + 2))
            act.activation(sgl, sdot, ACT.Gelu).then_inc(s["gelu_done"], 1)
            act.wait_ge(s["y_ready"], NB)
            sumsq(3, h_rows, junk)

        @block.vector
        def _(dve):
            steps = [0]

            def link(ins):
                steps[0] += 1
                ins.then_inc(s["vstep"], 1)
                dve.wait_ge(s["vstep"], steps[0])

            def tt(out, a, b, op):
                return dve.tensor_tensor(out, a, b, op)

            def invert(stage):
                dve.wait_ge(s["sumsq_done"], stage + 1)
                link(dve.tensor_scalar(rstd[stage], ss[stage], 1.0 / D, EPS, ALU.mult, ALU.add))
                dve.reciprocal(rstd[stage], rstd[stage]).then_inc(s["inv_done"], 1)
                dve.wait_ge(s["rstd_done"], stage + 1)

            def normed(stage, u, r, src, gain, dst):
                return dve.scalar_tensor_tensor(out=dst[0:r, :], in0=src, scalar=rstd[stage][0:r, u:u + 1],
                                                in1=gain[0:r, :], op0=ALU.mult, op1=ALU.mult)

            for x in ss:
                dve.memset(x, 1.0)
            dve.memset(hss[:, :, :], 1.0).then_inc(s["ss_cleared"], 1)
            dve.wait_ge(s["ss_cleared"], 1)
            invert(0)
            dve.wait_ge(s["gains_loaded"], 16)
            for u in range(7):
                if u >= 2:
                    dve.wait_ge(s["turned"], u - 1)
                r = DB if u == 6 else P
                normed(0, u, r, X0[0:r, u, :], GM if u < NMEM else G, XN[u % 2]).then_inc(s["xn_ready"], 1)
            dve.wait_ge(s["const_loaded"], 16)
            dve.wait_ge(s["small_loaded"], 16 * 6)
            for q in range(PPG):
                last = dve.tensor_copy(pt_f[32 * q:32 * q + 32, :],
                                       PTAB[32 * q:32 * q + 32, :].bitcast(I32).rearrange("p (x q) -> p x q", q=PPG)[:, :, q])
            link(last)
            link(dve.tensor_scalar(pt_f, pt_f, 32.0, const("part32"), ALU.mult, ALU.add))
            dve.tensor_copy(kv_idx.bitcast(U32), pt_f).then_inc(s["kvidx_ready"], 1)
            link(dve.memset(tab[NBUCKET:NBUCKET + 1, :], NEG))
            dve.tensor_copy(TABB[0:NBUCKET + 1], tab[0:NBUCKET + 1, :].unsqueeze(2).broadcast_to([NBUCKET + 1, H, P])
                            ).then_inc(s["past_ready"], 1)
            lv = lamv.rearrange("p (a c d) -> p a c d", a=2, c=2)
            link(tt(lv[:, :, 0, :], lv[:, :, 0, :], lv[:, :, 1, :], ALU.mult))
            dve.tensor_reduce(lsum, lv[:, :, 0, :], AX.X, ALU.add).then_inc(s["lam_sums"], 1)
            dve.wait_ge(s["lam_exp"], 1)
            dve.scalar_tensor_tensor(out=nlam, in0=lexp[:, 1:2], scalar=-LAM_INIT, in1=lexp[:, 0:1], op0=ALU.add,
                                     op1=ALU.subtract).then_inc(s["lam_ready"], 1)
            dve.wait_ge(s["lam_ready"], 1)
            dve.wait_ge(s["past_ps"], 1)
            dve.tensor_copy(bias_s, PS[:, 7, 0:24].rearrange("p (j h) -> p j h", j=6)).then_inc(s["past_ready"], 1)
            dve.wait_ge(s["past_ready"], 2)

            def rows_t(e, dst):
                b = e % NB
                r = ROWS[b]
                dve.wait_ge(s["rows_turned"], e + 1)
                dve.tensor_copy(dst[:, :, P * b:P * b + r],
                                PS[:, e % 4, :].rearrange("p (h t) -> p h t", h=H)[:, :, 0:r]).then_inc(s["rowsT_done"], 1)

            def key_tile(b, g):
                n = tile_no("k", b, g)
                tile_arrived(dve, n)
                dve.wait_ge(s["qb_ready"], b + 1)
                t = SLOT[n % RING].rearrange("p (j x) -> p j x", j=TPR)
                link(tt(t, t, PS[:, 6 + b % 2, :].unsqueeze(1).broadcast_to([P, TPR, 512]), ALU.mult))
                dve.tensor_reduce(S[:, 128 * b + 32 * g:128 * b + 32 * g + 32],
                                  SLOT[n % RING].rearrange("p (x d) -> p x d", d=DH), AX.X, ALU.add).then_inc(s["tile_used_dve"], 1)

            keys = [(b, g) for b in range(DB) for g in range(GRP)]
            dve.wait_ge(s["job_taken_act"], taken_by(first_job("dq") + SMP)[1])
            dve.tensor_copy(SRQ[0:DB, :], RK[0:DB, SMP, :]).then_inc(s["sq_saved"], 1)
            for e in range(NB):
                rows_t(e, DQT)
            for k in keys[0:KEYS_AHEAD]:
                key_tile(*k)
            for e in range(NB, 2 * NB):
                rows_t(e, DKT)
            dve.wait_ge(s["job_taken_act"], taken_by(first_job("dv") + SMP)[1])
            dve.tensor_copy(SRK[0:DB, :], RG[0:DB, SMP, :])
            dve.tensor_copy(DVS[0:DB, :], DV[0:DB, SMP, :]).then_inc(s["srow_saved"], 1)
            dve.wait_ge(s["srow_saved"], 1)

            dve.wait_ge(s["toe_loaded"], 16 * H)
            for st in range(NBLK * H + 1):
                if st < NBLK * H:
                    i, h = st // H, st % H
                    n = P * (i + 1)
                    z = slice(2 * (st % 2), 2 * (st % 2) + 2)
                    dve.wait_ge(s["scores_ready"], st + 1)
                    b0 = 2 * (st % 2)
                    dve.scalar_tensor_tensor(out=SC[st % 2][:, :, 0:n], in0=PS[:, b0:b0 + 2, 0:n], scalar=SCALE,
                                             in1=TOE[:, h, 512 - n:512].unsqueeze(1).broadcast_to([P, 2, n]),
                                             op0=ALU.mult, op1=ALU.add).then_inc(s["sc_biased"], 1)
                    dve.wait_ge(s["sc_biased"], st + 1)
                    dve.tensor_reduce(nmx[:, z], SC[st % 2][:, :, 0:n], AX.X, ALU.max, negate=True).then_inc(s["nmax_ready"], 1)
                if st >= 1:
                    q = st - 1
                    n = P * (q // H + 1)
                    z = 2 * (q % 2)
                    dve.wait_ge(s["exp_done"], q + 1)
                    link(dve.reciprocal(zsum[:, z:z + 2], zsum[:, z:z + 2]))
                    link(tt(zsum[:, z + 1:z + 2], zsum[:, z + 1:z + 2], nlam, ALU.mult))
                    if q >= 2:
                        dve.wait_ge(s["wmat_turned"], q - 1)
                    link(dve.tensor_scalar(WM[q % 2][:, 0:n], SC[q % 2][:, 0, 0:n], zsum[:, z:z + 1], None, ALU.mult))
                    dve.scalar_tensor_tensor(out=WM[q % 2][:, 0:n], in0=SC[q % 2][:, 1, 0:n], scalar=zsum[:, z + 1:z + 2],
                                             in1=WM[q % 2][:, 0:n], op0=ALU.mult, op1=ALU.add).then_inc(s["w_ready"], 1)

            def rotary(j, dst, tq):
                b = JOBS[j][1]
                r = ROWS[b]
                dve.wait_ge(s["job_ready"], j + 1)
                src = PS[0:r, PSUM_JOB + j % 2, :].rearrange("p (x d) -> p x d", d=64)
                cos = rot[0:r, b, tq, :].unsqueeze(1).broadcast_to([r, 2 * H, 64])
                sin = rot[0:r, b, tq + 1, :].unsqueeze(1).broadcast_to([r, 2 * H, 64])
                a = ROT_A[0:r, :].rearrange("p (x d) -> p x d", d=64)
                c = ROT_B[0:r, :].rearrange("p (x d) -> p x d", d=64)
                tt(a, src, cos, ALU.mult)
                tt(c, src, sin, ALU.mult).then_inc(s["job_taken_dve"], 1)
                dve.wait_ge(s["job_taken_dve"], taken_by(j)[1])
                a4 = ROT_A[0:r, :].rearrange("p (h c d) -> p h c d", h=H, c=2)
                c4 = ROT_B[0:r, :].rearrange("p (h c d) -> p h c d", h=H, c=2)
                d4 = dst[0:r, b, :].rearrange("p (h c d) -> p h c d", h=H, c=2)
                tt(d4[:, :, 0, :], a4[:, :, 0, :], c4[:, :, 1, :], ALU.subtract)
                tt(d4[:, :, 1, :], a4[:, :, 1, :], c4[:, :, 0, :], ALU.add).then_inc(s["ret_rows"], 1)

            dve.wait_ge(s["new_kv_stored"], 16 * NSTORES)
            done = KEYS_AHEAD
            for kind, dst, tq, tdst, e0 in (("rq", DV, 0, DQT, 2 * NB), ("rk", RK, 2, DKT, 3 * NB)):
                if kind == "rk":
                    for i in range(4):
                        dve.wait_ge(mem_stored[i], 32)
                dve.wait_ge(s["av_done"], NBLK * H)
                for b in range(NB):
                    rotary(first_job(kind) + b, dst, tq)
                    key_tile(*keys[done])
                    done += 1
                for b in range(NB):
                    rows_t(e0 + b, tdst)
            for k in keys[done:]:
                key_tile(*k)

            b5 = BFULL[:, :, :].rearrange("p (g j) (h c) -> p g j h c", j=TPR, h=H)
            for g in range(GRP):
                for j in range(TPR):
                    src = bias_s[:, j if g == GRP - 1 else 4, :].unsqueeze(2).broadcast_to([P, H, 2])
                    last = dve.tensor_copy(b5[:, g, j], src)
            link(last)
            S3 = S.rearrange("p (b x) -> p b x", b=DB)
            S4 = S.rearrange("p (b x c) -> p b x c", b=DB, c=HC)
            link(dve.scalar_tensor_tensor(out=S3, in0=S3, scalar=SCALE,
                                          in1=BFULL.rearrange("p x c -> p (x c)").unsqueeze(1).broadcast_to([P, DB, 128]),
                                          op0=ALU.mult, op1=ALU.add))
            link(dve.tensor_reduce(colmax.rearrange("p (b c) -> p b c", b=DB), S4.rearrange("p b x c -> p b c x"),
                                   AX.X, ALU.max))
            link(tt(ROT_A[0:DB, :], SRQ[0:DB, :], SRK[0:DB, :], ALU.mult))
            link(dve.tensor_reduce(sself[0:DB, :], ROT_A[0:DB, :].rearrange("p (x d) -> p x d", d=DH), AX.X, ALU.add))
            link(dve.scalar_tensor_tensor(out=sself[0:DB, :].rearrange("p (h c) -> p h c", h=H),
                                          in0=sself[0:DB, :].rearrange("p (h c) -> p h c", h=H), scalar=SCALE,
                                          in1=bias_s[0:DB, 5, :].unsqueeze(2).broadcast_to([DB, H, 2]),
                                          op0=ALU.mult, op1=ALU.add))
            link(tt(sself_e[0:DB], sself[0:DB, :].unsqueeze(1).broadcast_to([DB, DB, HC]), dmask[0:DB], ALU.mult))
            link(dve.tensor_scalar(sself_m[0:DB], dmask[0:DB], 1.0, -NEG, ALU.subtract, ALU.mult))
            link(tt(sself_m[0:DB], sself_m[0:DB], sself_e[0:DB], ALU.add))
            tt(colmax[0:DB, :].rearrange("p (b c) -> p b c", b=DB), colmax[0:DB, :].rearrange("p (b c) -> p b c", b=DB),
               sself_m[0:DB], ALU.max).then_inc(s["colmax_ready"], 1)
            dve.wait_ge(s["colmax_turned"], 1)
            link(dve.tensor_reduce(mcol[0:64, :], PS[0:64, 0, 0:P], AX.X, ALU.max))
            dve.tensor_scalar(mdiag[0:64, :], ident[0:64, 0:64], mcol[0:64, :], None, ALU.mult).then_inc(s["maxdiag_ready"], 1)
            dve.wait_ge(s["maxbc_ready"], 1)
            mbc = PS[:, 1, 0:64].rearrange("p (b c) -> p b c", b=DB)
            tt(S4, S4, mbc.unsqueeze(2).broadcast_to([P, DB, 16, HC]), ALU.subtract).then_inc(s["s_scored"], 1)
            link(tt(sself_e[0:DB], sself_e[0:DB], mbc[0:DB], ALU.subtract))
            tt(sself_e[0:DB], sself_e[0:DB], dmask[0:DB], ALU.mult).then_inc(s["sarg_ready"], 1)
            dve.wait_ge(s["sexp_done"], 2)
            tt(sself_e[0:DB], sself_e[0:DB], dmask[0:DB], ALU.mult)
            dve.tensor_reduce(esum, S4.rearrange("p b x c -> p b c x"), AX.X, ALU.add).then_inc(s["esum_ready"], 1)
            dve.wait_ge(s["z_ready"], 1)
            link(dve.reciprocal(rz[0:HC, :], PS[0:HC, 0, 0:DB]))
            link(dve.scalar_tensor_tensor(out=coef[0:HC, :], in0=const("odd")[0:HC, :], scalar=nlam[0:HC, :],
                                          in1=const("even")[0:HC, :], op0=ALU.mult, op1=ALU.add))
            link(dve.tensor_scalar(rz[0:HC, :], rz[0:HC, :], coef[0:HC, :], None, ALU.mult))
            tt(cl[0:HC], mask8[0:HC], rz[0:HC, :].unsqueeze(2).broadcast_to([HC, DB, DB]), ALU.mult).then_inc(s["coef_ready"], 1)

            dve.wait_ge(s["rowsT_done"], 20)
            for h in range(H):
                last = tt(RQM[:, h], mask8, DQT[:, h, SEQ:TOK].unsqueeze(2).broadcast_to([P, DB, DB]), ALU.mult)
            last.then_inc(s["rqm_ready"], 1)
            gam4 = const("gam").unsqueeze(2).broadcast_to([P, H, P])
            for b in range(DB):
                n = tile_no("st", b)
                if b >= 2:
                    dve.wait_ge(s["outer_ready"], b - 1)
                dve.tensor_scalar(KEXP[b % 2][0:DB, :], RK[0:DB, SMP, :], dmask[0:DB, b, 0:1], None, ALU.mult
                                  ).then_inc(s["kexp_ready"], 1)
                tile_arrived(dve, n)
                st = SLOT[n % RING][:, 0:512]
                link(tt(st.rearrange("p (h e) -> p h e", h=H), st.rearrange("p (h e) -> p h e", h=H), gam4, ALU.mult))
                dve.wait_ge(s["outer_ready"], b + 1)
                tt(st, st, PS[:, 2 + b % 2, :], ALU.add).then_inc(s["ns_ready"], 1)
            dve.wait_ge(s["tile_used_pe"], DB)
            dve.tensor_copy(RK[0:DB, SMP, :], PS[0:DB, 7, :]).then_inc(s["ret_rows"], 1)

            gl4 = const("gL").unsqueeze(2).broadcast_to([P, H, P])
            for i in range(NBLK):
                if i:
                    dve.wait_ge(s["ret_out"], i)
                tt(RQD.rearrange("p (h t) -> p h t", h=H), DQT[:, :, P * i:P * i + P],
                   const("qdec").rearrange("p (h t) -> p h t", h=H), ALU.mult)
                tt(RKD.rearrange("p (h d) -> p h d", h=H), RK[:, i, :].rearrange("p (h d) -> p h d", h=H),
                   const("kdec").unsqueeze(2).broadcast_to([P, H, P]), ALU.mult).then_inc(s["rqd_ready"], 1)
                dve.wait_ge(s["ret_scores"], i + 1)
                tt(RSC, PS[:, 0, :], const("decayT"), ALU.mult).then_inc(s["ret_sc_ready"], 1)
                dve.wait_ge(s["rqd_ready"], i + 1)
                dve.wait_ge(s["ret_out"], i + 1)
                dve.tensor_copy(RK[:, i, :], PS[:, 2, :])
                if i == 0:
                    dve.tensor_copy(STATE, PS[:, 3, :]).then_inc(s["ret_state"], 1)
                else:
                    link(tt(STATE.rearrange("p (h e) -> p h e", h=H), STATE.rearrange("p (h e) -> p h e", h=H), gl4, ALU.mult))
                    tt(STATE, STATE, PS[:, 3, :], ALU.add).then_inc(s["ret_state"], 1)
                dve.wait_ge(s["ret_state"], i + 1)

            for b in range(DB):
                dve.wait_ge(s["pv_done"], b + 1)
                if b == 0:
                    dve.wait_ge(s["tile_used_pe"], DB)
                if b >= 2:
                    dve.wait_ge(s["dif_row_ready"], b - 1)
                tt(OM[b % 2][0:HC, :], PS[0:HC, 4 + b % 2, :], const("hmask")[0:HC, :], ALU.mult).then_inc(s["om_ready"], 1)
            dve.wait_ge(s["dif_row_ready"], DB)
            link(dve.tensor_copy(DIF[0:DB, SMP, :], PS[0:DB, 6, :]))
            dve.wait_ge(s["state_stored"], 16)
            for r, b0, b1 in ((P, 0, NBLK), (DB, SMP, NB)):
                w = 512 * (b1 - b0)
                for i, src in ((0, RK), (1, DIF)):
                    last = tt(SQ[i][0:r, 0:w].rearrange("p (b d) -> p b d", b=b1 - b0), src[0:r, b0:b1, :], src[0:r, b0:b1, :], ALU.mult)
                link(last)
                for i in range(2):
                    last = dve.tensor_reduce(hss[0:r, b0:b1, H * i:H * i + H],
                                             SQ[i][0:r, 0:w].rearrange("p (b h d) -> p b h d", b=b1 - b0, h=H), AX.X, ALU.add)
                link(last)
            link(dve.tensor_scalar(hss, hss, 1.0 / P, EPS, ALU.mult, ALU.add))
            dve.reciprocal(hss, hss).then_inc(s["hsq_ready"], 1)
            dve.wait_ge(s["hrstd_done"], 1)
            link(dve.tensor_scalar(hss[:, :, H:2 * H], hss[:, :, H:2 * H], 1.0 - LAM_INIT, None, ALU.mult))
            for b in range(NB):
                r = ROWS[b]

                def heads(x):
                    return x[0:r, b, :].rearrange("p (h d) -> p h d", h=H)

                link(tt(heads(RK), heads(RK), hss[0:r, b, 0:H].unsqueeze(2).broadcast_to([r, H, P]), ALU.mult))
                tt(RK[0:r, b, :], RK[0:r, b, :], RG[0:r, b, :], ALU.mult)
                tt(heads(DIF), heads(DIF), hss[0:r, b, H:2 * H].unsqueeze(2).broadcast_to([r, H, P]), ALU.mult
                   ).then_inc(s["mix_ready"], 1)

            def residual(kind):
                for j in [j for j in range(len(JOBS)) if job_kind(j) == kind]:
                    t, b = JOBS[j]
                    c0, r = WTILES[t][1], ROWS[b]
                    dve.wait_ge(s["job_ready"], j + 1)
                    tt(HR[0:r, b, c0:c0 + 512], HR[0:r, b, c0:c0 + 512], PS[0:r, PSUM_JOB + j % 2, :], ALU.add
                       ).then_inc(s["job_taken_dve"], 1)

            dve.wait_ge(s["x_again"], 32)
            residual("mix")
            for e in range(4):
                dve.wait_ge(s["mkr_turned"], e + 1)
                dve.tensor_copy(MKT[:, 2 * e:2 * e + 2, :].rearrange("p k m -> p (k m)"), PS[:, e, :]).then_inc(s["mkT_done"], 1)
            invert(1)
            dve.wait_ge(s["gains_loaded"], 32)
            dve.wait_ge(s["job_taken_dve"], taken_by(first_job("mq") - 1)[1])
            for b in range(NB):
                n = N_CROSS + b
                if b >= 2:
                    dve.wait_ge(s["turned"], n - 1)
                normed(1, b, ROWS[b], HR[0:ROWS[b], b, :], G, XN[b % 2]).then_inc(s["xn_ready"], 1)

            for st in range(NBLK + 1):
                if st < NBLK:
                    z = slice(H * (st % 2), H * (st % 2) + H)
                    dve.wait_ge(s["cs_ready"], st + 1)
                    link(dve.tensor_reduce(cneg[:, z], PS[:, 2 * (st % 2):2 * (st % 2) + 2, :].rearrange("p a (c m) -> p (a c) m", c=2),
                                           AX.X, ALU.max, negate=True))
                    dve.tensor_scalar(cneg[:, z], cneg[:, z], MSCALE, None, ALU.mult).then_inc(s["cmax_ready"], 1)
                if st >= 1:
                    q = st - 1
                    z = slice(H * (q % 2), H * (q % 2) + H)
                    dve.wait_ge(s["co_ready"], q + 1)
                    link(dve.reciprocal(csum[:, z], csum[:, z]))
                    tt(QR[:, q, :].rearrange("p (h d) -> p h d", h=H),
                       PS[:, 6:8, :].rearrange("p a (c d) -> p (a c) d", c=2),
                       csum[:, z].unsqueeze(2).broadcast_to([P, H, MDH]), ALU.mult).then_inc(s["co_taken"], 1)

            for b in range(DB):
                n = tile_no("mk", b)
                tile_arrived(dve, n)
                dve.wait_ge(s["cqb_ready"], b + 1)
                t = SLOT[n % RING].rearrange("p (j x) -> p j x", j=NMEM)
                q = PS[:, 2 * (b % 2):2 * (b % 2) + 2, :].rearrange("p a c -> p (a c)")
                link(tt(t, t, q.unsqueeze(1).broadcast_to([P, NMEM, D]), ALU.mult))
                dve.tensor_reduce(CS4[:, b], SLOT[n % RING].rearrange("p (j h d) -> p j h d", j=NMEM, h=H), AX.X, ALU.add
                                  ).then_inc(s["tile_used_dve"], 1)
            dve.wait_ge(s["tile_used_dve"], tile_used(tile_no("mk", DB - 1))[1])
            dve.tensor_reduce(ccol.rearrange("p (b h) -> p b h", b=DB), CS4.rearrange("p b j h -> p b h j"), AX.X, ALU.max
                              ).then_inc(s["ccolmax_ready"], 1)
            dve.wait_ge(s["ccolmax_turned"], 1)
            link(dve.tensor_reduce(cmx[0:32, :], PS[0:32, 4, 0:P], AX.X, ALU.max))
            dve.tensor_scalar(cmd[0:32, :], ident[0:32, 0:32], cmx[0:32, :], None, ALU.mult).then_inc(s["cmaxdiag_ready"], 1)
            dve.wait_ge(s["cmaxbc_ready"], 1)
            tt(CS4, CS4, PS[:, 5, 0:32].rearrange("p (b h) -> p b h", b=DB).unsqueeze(2).broadcast_to([P, DB, NMEM, H]),
               ALU.subtract).then_inc(s["cs_scored"], 1)
            dve.wait_ge(s["csexp_done"], 1)
            dve.tensor_reduce(cesum.rearrange("p (b h) -> p b h", b=DB), CS4.rearrange("p b j h -> p b h j"), AX.X, ALU.add
                              ).then_inc(s["cesum_ready"], 1)
            dve.wait_ge(s["cz_ready"], 1)
            link(dve.reciprocal(crz[0:H, :], PS[0:H, 4, 0:DB]))
            tt(ccl[0:H], mask8[0:H], crz[0:H, :].unsqueeze(2).broadcast_to([H, DB, DB]), ALU.mult).then_inc(s["ccoef_ready"], 1)
            for b in range(DB):
                dve.wait_ge(s["cpv_done"], b + 1)
                if b >= 2:
                    dve.wait_ge(s["crow_ready"], b - 1)
                tt(COM[b % 2][0:H, :], PS[0:H, 2 * (b % 2):2 * (b % 2) + 2, :].rearrange("p a c -> p (a c)"),
                   const("hmask4")[0:H, :], ALU.mult).then_inc(s["com_ready"], 1)
            dve.wait_ge(s["crow_ready"], DB)
            dve.tensor_copy(QR[0:DB, SMP, :], PS[0:DB, 6:8, :].rearrange("p a c -> p (a c)")).then_inc(s["crow_ready"], 1)
            residual("mo")

            invert(2)
            dve.wait_ge(s["gains_loaded"], 48)
            dve.wait_ge(s["turned"], N_FFN)
            for b in range(NB):
                normed(2, b, ROWS[b], HR[0:ROWS[b], b, :], G, QR[:, b, :]).then_inc(s["xn_ready"], 1)
            for e in range(4):
                dve.wait_ge(s["sk_turned"], e + 1)
                dve.tensor_copy(SKT[:, 4 * e:4 * e + 4, :].rearrange("p x k -> p (x k)"), PS[:, e, :]).then_inc(s["skT_done"], 1)

            def scores_of(x, b):
                r = ROWS[b]
                if b == SMP:
                    return PS[0:r, 2 * (x % 2) + 1, 0:NK]
                return PS[0:r, 2 * (x % 2), NK * b:NK * b + NK]

            TVF = TV.rearrange("p b x k -> p b (x k)")
            TIFB = TI.rearrange("p b x k -> p b (x k)")
            chain = [0]

            def select_head(order, b, h):
                r, k = ROWS[b], [0]

                def slink(ins, alone=False):
                    k[0] += 1
                    ins.then_inc(s["select_steps"], 1)
                    dve.wait_ge(s["select_steps"], h * SELECT_LINKS + (PH * SELECT_LINKS * order + k[0]))
                    if alone:
                        dve.nop(nofuse=True)

                v1, v2 = TVF[0:r, b, bass.ds(h * 32, TOPK)], TVF[0:r, b, bass.ds(h * 32 + TOPK, TOPK)]
                cand, work = CAND[0:r], CAND2[0:r]
                slink(tt(cand.rearrange("p (a c) -> p a c", a=TOPK), v1.unsqueeze(2).broadcast_to([r, TOPK, TOPK]),
                         v2.unsqueeze(1).broadcast_to([r, TOPK, TOPK]), ALU.add), alone=True)
                bv, bi = BV[0:r], BI[0:r].bitcast(U32)
                slink(dve.max(bv[:, 0:8], cand), alone=True)
                dve.max_index(bi[:, 0:8], bv[:, 0:8], cand)
                slink(dve.match_replace(work, bv[:, 0:8], cand, NEG), alone=True)
                slink(dve.max(bv[:, 8:16], work), alone=True)
                dve.tensor_copy(TIF[0:r], TIFB[0:r, b, bass.ds(h * 32, 2 * TOPK)].bitcast(U32))
                slink(dve.max_index(bi[:, 8:16], bv[:, 8:16], work))
                dve.tensor_copy(GATE[0:r, b, bass.ds(h * TOPK, TOPK)], bv)
                dve.tensor_scalar(AU[0:r].bitcast(U32), bi, 4, None, ALU.logical_shift_right)
                slink(dve.tensor_scalar(CU[0:r].bitcast(U32), bi, TOPK - 1, None, ALU.bitwise_and))
                dve.tensor_copy(AF[0:r], AU[0:r].bitcast(U32))
                slink(dve.tensor_copy(CF[0:r], CU[0:r].bitcast(U32)))
                hots = (HOT[0:r, 0:256].rearrange("p (k a) -> p k a", a=TOPK), HOT[0:r, 256:512].rearrange("p (k a) -> p k a", a=TOPK))
                iota = const("iota16")[0:r].unsqueeze(1).broadcast_to([r, TOPK, TOPK])
                for hot, pos in zip(hots, (AF, CF)):
                    last = tt(hot, pos[0:r].unsqueeze(2).broadcast_to([r, TOPK, TOPK]), iota, ALU.is_equal)
                slink(last)
                for half, hot in enumerate(hots):
                    last = tt(hot, hot, TIF[0:r, TOPK * half:TOPK * half + TOPK].unsqueeze(1).broadcast_to([r, TOPK, TOPK]), ALU.mult)
                slink(last)
                slink(dve.tensor_reduce(GAC[0:r], HOT[0:r, 0:512].rearrange("p (n a) -> p n a", a=TOPK), AX.X, ALU.add))
                slink(dve.scalar_tensor_tensor(out=GAC[0:r, 0:TOPK], in0=GAC[0:r, 0:TOPK], scalar=float(NK),
                                               in1=GAC[0:r, TOPK:2 * TOPK], op0=ALU.mult, op1=ALU.add))
                if b == SMP:
                    dve.tensor_copy(sidx_row[0:r, bass.ds(h * TOPK, TOPK)], GAC[0:r, 0:TOPK])
                slink(dve.tensor_copy(IDX[0:r, b, bass.ds(h * TOPK, TOPK)].bitcast(U32), GAC[0:r, 0:TOPK]))
                assert k[0] == SELECT_LINKS

            def gates(order, b):
                r = ROWS[b]
                gate3 = GATE[0:r, b, :].rearrange("p (h k) -> p h k", h=PH)
                link(dve.tensor_copy(bmax[0:r], gate3[:, :, 0]))
                tt(gate3, gate3, bmax[0:r].unsqueeze(2).broadcast_to([r, PH, TOPK]), ALU.subtract).then_inc(s["sarg_ready"], 1)
                dve.wait_ge(s["sexp_done"], 3 + order)
                link(dve.tensor_reduce(bsum[0:r], gate3, AX.X, ALU.add))
                link(dve.reciprocal(bsum[0:r], bsum[0:r]))
                tt(gate3, gate3, bsum[0:r].unsqueeze(2).broadcast_to([r, PH, TOPK]), ALU.mult).then_inc(s["sel_ready"], 1)

            for x in range(NSUB):
                dve.wait_ge(s["rs_ready"], x + 1)
                for step in range(5):
                    for b in range(NB):
                        r = ROWS[b]
                        src, work = scores_of(x, b), WORK[0:r, b, :]
                        v, i = TV[0:r, b, x, :], TI[0:r, b, x, :].bitcast(U32)
                        if step == 0:
                            last = dve.max(v[:, 0:8], src)
                        elif step == 1:
                            last = dve.max_index(i[:, 0:8], v[:, 0:8], src)
                        elif step == 2:
                            last = dve.match_replace(work, v[:, 0:8], src, NEG)
                        elif step == 3:
                            last = dve.max(v[:, 8:16], work)
                        else:
                            last = dve.max_index(i[:, 8:16], v[:, 8:16], work)
                    if step == 4:
                        last.then_inc(s["rs_taken"], 1)
                    elif step != 1:
                        link(last)
                if x % 2:
                    dve.wait_ge(s["rs_taken"], x + 1)
                    select_head(0, 0, x // 2)
            gates(0, 0)
            dve.memset(bmax[0:1, 0:1], 0.0).then_inc(s["u_used"], CHUNK)

            def add_expert_rows(b):
                banks = 6 if b == SMP else 2 * (b % 2)
                r = ROWS[b]
                dve.wait_ge(s["v_used"], CHUNK * (NCH * min(b + 1, NBLK) + 1 + (b == SMP)))
                tt(HR[0:r, b, :], HR[0:r, b, :], PS[0:r, banks:banks + 2, :].rearrange("p a c -> p (a c)"), ALU.add
                   ).then_inc(s["y_ready"], 1)

            for blk in range(NBLK):
                with dve.Fori(0, PH) as h:
                    for half in range(NCH // PH):
                        c0 = NCH * blk + half
                        for k in range(CHUNK):
                            dve.wait_ge(uv_in[0][k], h * 32 + 16 * (c0 + 1))
                            dve.tensor_tensor_reduce(USLOT[k], USLOT[k], QR[:, blk, :], 1.0, 0.0, ALU.mult, ALU.add,
                                                     dots[:, k:k + 1]).then_inc(s["u_used"], 1)
                        dve.wait_ge(s["gelu_done"], h * 2 + (c0 + 1))
                        dve.wait_ge(s["v_used"], h * (2 * CHUNK) + CHUNK * (c0 + 1))
                        tt(WCH, gl, GATE[:, blk, bass.ds(h * (2 * CHUNK) + half * CHUNK, CHUNK)], ALU.mult).then_inc(s["weight_ready"], 1)
                    select_head(blk + 1, blk + 1, h)
                gates(blk + 1, blk + 1)
                if blk:
                    add_expert_rows(blk - 1)

            dve.wait_ge(s["sidx_turned"], 1)
            dve.tensor_copy(SIDX.bitcast(U32), PS[:, 4, 0:DB])
            dve.tensor_copy(SGATE, PS[:, 4, P:P + DB]).then_inc(s["sel_ready"], 1)
            dve.wait_ge(s["sel_ready"], NB + 1)
            for b in range(DB):
                dve.wait_ge(uv_in[0][b], 16 * (NCH * NBLK + 1))
                dve.wait_ge(s["xb_ready"], b + 1)
                x = PS[:, 4 + 2 * (b % 2):6 + 2 * (b % 2), :].rearrange("p a c -> p (a c)")
                dve.tensor_tensor_reduce(USLOT[b], USLOT[b], x, 1.0, 0.0, ALU.mult, ALU.add, sdot[:, b:b + 1]).then_inc(s["u_used"], 1)
            add_expert_rows(NBLK - 1)
            dve.wait_ge(s["gelu_done"], NCH * NBLK + 1)
            link(tt(sgl, sgl, SGATE, ALU.mult))
            tt(SWM, mask8, sgl.unsqueeze(2).broadcast_to([P, DB, DB]), ALU.mult).then_inc(s["smp_w"], 1)
            add_expert_rows(SMP)

            invert(3)
            dve.wait_ge(s["gains_loaded"], 64)
            for b in range(NB):
                normed(3, b, ROWS[b], HR[0:ROWS[b], b, :], G, QR[:, b, :]).then_inc(s["final_ready"], 1)

        @block.tensor
        def _(pe):
            def turn(n, chunks, r):
                if n >= 2:
                    pe.wait_ge(s["xt_done"], n - 1)
                tb = turn_banks(n)
                for k, c in enumerate(chunks):
                    last = pe.transpose(tb[:, P * k:P * k + r], c, ident[0:r, 0:r])
                last.then_inc(s["turned"], 1)

            def pieces(row, r):
                return [row[0:r, P * k:P * k + P] for k in range(row.shape[-1] // P)]

            pe.wait_ge(s["ident_loaded"], 16)
            for n in range(TURN):
                pe.wait_ge(s["xn_ready"], n + 1)
                r = DB if n == 6 else P
                turn(n, pieces(XN[n % 2], r), r)
            pe.wait_ge(s["const_loaded"], 16)
            pe.wait_ge(s["past_ready"], 1)
            for h in range(H):
                if h:
                    pe.wait_ge(s["line_row"], h)
                    pe.wait_ge(s["line_cols"], h)
                pe.matmul(PS[:, 6, :], TABB[0:NBUCKET + 1, h, :], const("line")[0:NBUCKET + 1, 0:512], start=True, stop=True)
                pe.matmul(PS[:, 7, 0:TL - 512], TABB[0:NBUCKET + 1, h, :], const("line")[0:NBUCKET + 1, 512:TL],
                          start=True, stop=True).then_inc(s["line_ps"], 1)
            pe.wait_ge(s["line_row"], H)
            for j in range(6):
                last = pe.matmul(PS[:, 7, 4 * j:4 * j + 4], const("past")[0:NBUCKET, P * j:P * j + P], tab[0:NBUCKET, :],
                                 start=True, stop=True)
            last.then_inc(s["past_ps"], 1)
            pe.wait_ge(s["xt_done"], TURN)

            def job(j, x0):
                t, u = JOBS[j]
                r = P if job_kind(j) == "mem" else ROWS[u]
                w_arrived(pe, t)
                if j >= 2:
                    dve, c = taken_by(j - 2)
                    pe.wait_ge(s["job_taken_dve"] if dve else s["job_taken_act"], c)
                for k in range(KD):
                    last = pe.matmul(PS[0:r, PSUM_JOB + j % 2, :], XT[:, k, x0:x0 + r], W[t % 2][:, k, :],
                                     start=(k == 0), stop=(k == KD - 1))
                last.then_inc(s["job_ready"], 1)

            def jobs(kind, x0=0, between=None):
                done = [j for j in range(len(JOBS)) if job_kind(j) == kind]
                for j in done:
                    job(j, x0 + P * JOBS[j][1])
                    if between:
                        between(j - done[0])

            def rows_turn(e, row, b, ready, count):
                r = ROWS[b]
                pe.wait_ge(ready, count)
                if e >= 4:
                    pe.wait_ge(s["rowsT_done"], e - 3)
                for h in range(H):
                    last = pe.transpose(PS[:, e % 4, P * h:P * h + r], row[0:r, P * h:P * h + P], ident[0:r, 0:r])
                last.then_inc(s["rows_turned"], 1)

            def query_bc(b):
                if b >= 2:
                    pe.wait_ge(s["tile_used_dve"], GRP * (b - 1))
                pe.matmul(PS[:, 6 + b % 2, :], sel[0:DB, b, :], SRQ[0:DB, :], start=True, stop=True).then_inc(s["qb_ready"], 1)

            jobs("dq", X1)
            pe.wait_ge(s["past_ready"], 2)
            pe.wait_ge(s["sq_saved"], 1)
            query_bc(0)
            query_bc(1)
            for b in range(NB):
                rows_turn(b, RK[:, b, :], b, s["job_taken_act"], taken_by(first_job("dq") + b)[1])
            jobs("dk", X1, lambda i: query_bc(2) if i == 3 else None)
            jobs("dv", X1, lambda i: query_bc(3) if i == 1 else None)
            for b in range(NB):
                rows_turn(NB + b, RG[:, b, :], b, s["job_taken_act"], taken_by(first_job("dk") + b)[1])

            pe.wait_ge(s["rowsT_done"], 2 * NB)
            pe.wait_ge(s["job_taken_act"], taken_by(first_job("dv") + SMP)[1])
            pe.wait_ge(s["past_ready"], 2)
            for st in range(NBLK * H + 1):
                if st < NBLK * H:
                    i, h = st // H, st % H
                    n = P * (i + 1)
                    if st >= 2:
                        pe.wait_ge(s["sc_biased"], st - 1)
                    for c in range(2):
                        last = pe.matmul(PS[:, 2 * (st % 2) + c, 0:n], DQT[DH * c:DH * c + DH, h, P * i:P * i + P],
                                         DKT[DH * c:DH * c + DH, h, 0:n], start=True, stop=True)
                    last.then_inc(s["scores_ready"], 1)
                if st < len(extra_jobs):
                    j = extra_jobs[st]
                    job(j, P * JOBS[j][1] + (0 if job_kind(j) == "mem" else X1))
                if st >= 1:
                    q = st - 1
                    i, h = q // H, q % H
                    pe.wait_ge(s["w_ready"], q + 1)
                    if q >= 1:
                        pe.wait_ge(s["wT_ready"], q)
                    for k in range(i + 1):
                        last = pe.transpose(PS[:, 6, P * k:P * k + P], WM[q % 2][:, P * k:P * k + P], ident)
                    last.then_inc(s["wmat_turned"], 1)
                    if h == 0 and i >= 1:
                        pe.wait_ge(s["dif_taken"], i)
                    pe.wait_ge(s["wT_ready"], q + 1)
                    for k in range(i + 1):
                        last = pe.matmul(PS[:, 7, P * h:P * h + P], WT[q % 2][:, P * k:P * k + P], DV[:, k, P * h:P * h + P],
                                         start=(k == 0), stop=(k == i))
                    last.then_inc(s["av_done"], 1)
            pe.wait_ge(s["dif_taken"], NBLK)
            pe.wait_ge(s["srow_saved"], 1)

            query_bc(4)
            query_bc(5)
            jobs("rq", X1)
            for b in range(NB):
                rows_turn(2 * NB + b, DV[:, b, :], b, s["ret_rows"], b + 1)
            query_bc(6)
            jobs("rk", X1)
            for b in range(NB):
                rows_turn(3 * NB + b, RK[:, b, :], b, s["ret_rows"], NB + b + 1)
            jobs("rv", X1, lambda i: query_bc(7) if i == 2 else None)

            pe.wait_ge(s["rowsT_done"], 20)
            pe.wait_ge(s["colmax_ready"], 1)
            pe.transpose(PS[0:64, 0, 0:P], colmax, ident).then_inc(s["colmax_turned"], 1)
            pe.wait_ge(s["maxdiag_ready"], 1)
            pe.matmul(PS[:, 1, 0:64], ones[0:64, :], mdiag[0:64, :], start=True, stop=True).then_inc(s["maxbc_ready"], 1)
            pe.wait_ge(s["esum_ready"], 1)
            for b in range(DB):
                pe.matmul(PS[0:HC, 0, b:b + 1], esum[:, b, :], ones[:, 0:1], start=True, stop=False)
                last = pe.matmul(PS[0:HC, 0, b:b + 1], sself_e[0:DB, b, :], ones[0:DB, 0:1], start=False, stop=True)
            last.then_inc(s["z_ready"], 1)

            pe.wait_ge(s["tile_used_dve"], GRP * DB)
            pe.wait_ge(s["job_taken_act"], taken_by(first_job("rv") + SMP)[1])
            pe.wait_ge(s["rqm_ready"], 1)
            pe.matmul(PS[0:DB, 7, :], zeros[:, 0:DB], const("decayT"), start=True, stop=False, skip_group_check=True)
            for b in range(DB):
                pe.wait_ge(s["kexp_ready"], b + 1)
                if b >= 2:
                    pe.wait_ge(s["ns_ready"], b - 1)
                for h in range(H):
                    last = pe.matmul(PS[:, 2 + b % 2, P * h:P * h + P], KEXP[b % 2][0:DB, P * h:P * h + P],
                                     DV[0:DB, SMP, P * h:P * h + P], start=True, stop=True)
                last.then_inc(s["outer_ready"], 1)
                pe.wait_ge(s["ns_ready"], b + 1)
                n = tile_no("st", b)
                for h in range(H):
                    last = pe.matmul(PS[0:DB, 7, P * h:P * h + P], RQM[:, h, b, :], SLOT[n % RING][:, P * h:P * h + P],
                                     start=False, stop=(b == DB - 1 and h == H - 1), skip_group_check=True)
                last.then_inc(s["tile_used_pe"], 1)

            pe.wait_ge(s["coef_ready"], 1)
            pe.wait_ge(s["ns_ready"], DB)
            for i in range(NBLK):
                if i:
                    pe.wait_ge(s["ret_sc_ready"], i)
                for h in range(H):
                    last = pe.matmul(PS[:, 0, P * h:P * h + P], DKT[:, h, P * i:P * i + P], DQT[:, h, P * i:P * i + P],
                                     start=True, stop=True)
                last.then_inc(s["ret_scores"], 1)
                pe.wait_ge(s["rqd_ready"], i + 1)
                pe.wait_ge(s["ret_sc_ready"], i + 1)
                if i:
                    pe.wait_ge(s["ret_state"], i)
                for h in range(H):
                    pe.matmul(PS[:, 2, P * h:P * h + P], RSC[:, P * h:P * h + P], DV[:, i, P * h:P * h + P],
                              start=True, stop=(i == 0))
                    if i:
                        pe.matmul(PS[:, 2, P * h:P * h + P], RQD[:, P * h:P * h + P], STATE[:, P * h:P * h + P],
                                  start=False, stop=True)
                    last = pe.matmul(PS[:, 3, P * h:P * h + P], RKD[:, P * h:P * h + P], DV[:, i, P * h:P * h + P],
                                     start=True, stop=True)
                last.then_inc(s["ret_out"], 1)

            pe.matmul(PS[0:DB, 6, :], zeros[:, 0:DB], const("decayT"), start=True, stop=False, skip_group_check=True)

            def weigh(b):
                pe.wait_ge(s["om_ready"], b + 1)
                pe.matmul(PS[0:DB, 6, :], cl[0:HC, b, :], OM[b % 2][0:HC, :], start=False, stop=(b == DB - 1),
                          skip_group_check=True).then_inc(s["dif_row_ready"], 1)

            for b in range(DB):
                if b >= 2:
                    pe.wait_ge(s["om_ready"], b - 1)
                for g in range(GRP):
                    n = tile_no("v", b, g)
                    tile_arrived(pe, n)
                    for j in range(TPR):
                        c0 = 128 * b + 32 * g + 8 * j
                        last = pe.matmul(PS[0:HC, 4 + b % 2, :], S[:, c0:c0 + HC], SLOT[n % RING][:, 512 * j:512 * j + 512],
                                         start=(g == 0 and j == 0), stop=False)
                    last.then_inc(s["tile_used_pe"], 1)
                pe.matmul(PS[0:HC, 4 + b % 2, :], sself_e[0:DB, b, :], DVS[0:DB, :], start=False, stop=True
                          ).then_inc(s["pv_done"], 1)
                if b >= 1:
                    weigh(b - 1)
            weigh(DB - 1)
            for b in range(NB):
                pe.wait_ge(s["mix_ready"], b + 1)
                r = ROWS[b]
                turn(N_MIX + b, pieces(RK[:, b, :], r) + pieces(DIF[:, b, :], r), r)

            def xt_ready(n):
                pe.wait_ge(s["xt_done"], n)

            xt_ready(N_CROSS)
            jobs("mix", X1)
            pe.wait_ge(s["mkr_loaded"], 16)
            for e in range(4):
                for k in range(2):
                    for m in range(NMEM):
                        last = pe.transpose(PS[:, e, MEM * k + P * m:MEM * k + P * m + P],
                                            MKR[:, m, P * (2 * e + k):P * (2 * e + k) + P], ident)
                last.then_inc(s["mkr_turned"], 1)
            pe.wait_ge(s["mkT_done"], 4)

            for b in range(NB):
                pe.wait_ge(s["xn_ready"], TURN + b + 1)
                turn(N_CROSS + b, pieces(XN[b % 2], ROWS[b]), ROWS[b])
            xt_ready(N_Q)
            jobs("mq", X1)
            for b in range(NB):
                pe.wait_ge(s["job_taken_act"], taken_by(first_job("mq") + NB + b)[1])
                turn(N_Q + b, pieces(QR[:, b, :], ROWS[b]), ROWS[b])
            xt_ready(N_O)

            pe.wait_ge(s["mv_loaded"], 16)
            for st in range(NBLK + 1):
                if st < NBLK:
                    if st >= 2:
                        pe.wait_ge(s["cexp_done"], st - 1)
                    for h in range(H):
                        for k in range(2):
                            last = pe.matmul(PS[:, 2 * (st % 2) + h // 2, MEM * (h % 2):MEM * (h % 2) + MEM],
                                             XT[:, 2 * h + k, X1 + P * st:X1 + P * st + P], MKT[:, 2 * h + k, :],
                                             start=(k == 0), stop=(k == 1))
                    last.then_inc(s["cs_ready"], 1)
                if st >= 1:
                    q = st - 1
                    pe.wait_ge(s["cexp_done"], q + 1)
                    if q >= 1:
                        pe.wait_ge(s["ceT_ready"], q)
                    for h in range(H):
                        for m in range(NMEM):
                            x = NMEM * h + m
                            last = pe.transpose(PS[:, 4 + x // 4, P * (x % 4):P * (x % 4) + P], CE[q % 2][:, h, P * m:P * m + P], ident)
                    last.then_inc(s["ce_turned"], 1)
                    pe.wait_ge(s["ceT_ready"], q + 1)
                    if q >= 1:
                        pe.wait_ge(s["co_taken"], q)
                    for h in range(H):
                        for m in range(NMEM):
                            x = P * (NMEM * h + m)
                            last = pe.matmul(PS[:, 6 + h // 2, MDH * (h % 2):MDH * (h % 2) + MDH], CET[q % 2][:, x:x + P],
                                             MV[:, m, MDH * h:MDH * h + MDH], start=(m == 0), stop=(m == NMEM - 1))
                    last.then_inc(s["co_ready"], 1)

            for b in range(DB):
                if b >= 2:
                    pe.wait_ge(s["tile_used_dve"], tile_used(tile_no("mk", b - 2))[1])
                for i in range(2):
                    last = pe.matmul(PS[:, 2 * (b % 2) + i, :], sel[0:DB, b, :], QR[0:DB, SMP, 512 * i:512 * i + 512],
                                     start=True, stop=True)
                last.then_inc(s["cqb_ready"], 1)
            pe.wait_ge(s["ccolmax_ready"], 1)
            pe.transpose(PS[0:32, 4, 0:P], ccol, ident).then_inc(s["ccolmax_turned"], 1)
            pe.wait_ge(s["cmaxdiag_ready"], 1)
            pe.matmul(PS[:, 5, 0:32], ones[0:32, :], cmd[0:32, :], start=True, stop=True).then_inc(s["cmaxbc_ready"], 1)
            pe.wait_ge(s["cesum_ready"], 1)
            for b in range(DB):
                last = pe.matmul(PS[0:H, 4, b:b + 1], cesum[:, H * b:H * b + H], ones[:, 0:1], start=True, stop=True)
            last.then_inc(s["cz_ready"], 1)
            pe.wait_ge(s["co_taken"], NBLK)
            pe.wait_ge(s["ccoef_ready"], 1)
            for i in range(2):
                pe.matmul(PS[0:DB, 6 + i, :], zeros[:, 0:DB], const("decayT"), start=True, stop=False, skip_group_check=True)

            def cweigh(b):
                pe.wait_ge(s["com_ready"], b + 1)
                for i in range(2):
                    last = pe.matmul(PS[0:DB, 6 + i, :], ccl[0:H, b, :], COM[b % 2][0:H, 512 * i:512 * i + 512],
                                     start=False, stop=(b == DB - 1), skip_group_check=True)
                last.then_inc(s["crow_ready"], 1)

            for b in range(DB):
                n = tile_no("mv", b)
                if b >= 2:
                    pe.wait_ge(s["com_ready"], b - 1)
                tile_arrived(pe, n)
                for i in range(2):
                    for j in range(NMEM):
                        last = pe.matmul(PS[0:H, 2 * (b % 2) + i, :], CS4[:, b, j, :],
                                         SLOT[n % RING][:, D * j + 512 * i:D * j + 512 * i + 512], start=(j == 0), stop=(j == 1))
                last.then_inc(s["cpv_done"], 1)
                if b >= 1:
                    cweigh(b - 1)
            cweigh(DB - 1)
            for b in range(NB):
                if b < NBLK:
                    pe.wait_ge(s["co_taken"], b + 1)
                else:
                    pe.wait_ge(s["crow_ready"], DB + 1)
                turn(N_O + b, pieces(QR[:, b, :], ROWS[b]), ROWS[b])
            xt_ready(N_FFN)
            jobs("mo", X1)

            for b in range(NB):
                pe.wait_ge(s["xn_ready"], TURN + NB + b + 1)
                turn(N_FFN + b, pieces(QR[:, b, :], ROWS[b]), ROWS[b])
            xt_ready(N_END)
            pe.wait_ge(s["sk_loaded"], 16)
            for e in range(4):
                for k in range(4):
                    last = pe.transpose(PS[:, e, P * k:P * k + P], SKR[:, 4 * e + k, :], ident)
                last.then_inc(s["sk_turned"], 1)
            pe.wait_ge(s["skT_done"], 4)

            def router_scores(x):
                pe.wait_ge(s["rqp_taken"], x + 1)
                if x >= 2:
                    pe.wait_ge(s["rs_taken"], x - 1)
                for b in range(NB):
                    r = ROWS[b]
                    last = pe.matmul(PS[0:r, 2 * (x % 2) + (b == SMP), (0 if b == SMP else NK * b):(NK if b == SMP else NK * b + NK)],
                                     QPT[x % 2][:, P * b:P * b + r], SKT[:, x, :], start=True, stop=True)
                last.then_inc(s["rs_ready"], 1)

            for x in range(NSUB):
                t = PQ0 + x // 4
                w_arrived(pe, t)
                if x >= 2:
                    pe.wait_ge(s["rqp_taken"], x - 1)
                for k in range(KD):
                    w = W[t % 2][:, k, P * (x % 4):P * (x % 4) + P]
                    for i in range(2):
                        t0 = X1 + TOK // 2 * i
                        last = pe.matmul(PS[:, 4 + 2 * (x % 2) + i, 0:TOK // 2], w, XT[:, k, t0:t0 + TOK // 2],
                                         start=(k == 0), stop=(k == KD - 1))
                last.then_inc(s["rqp_ready"], 1)
                if x >= 1:
                    router_scores(x - 1)
            router_scores(NSUB - 1)

            def open_group(bank, r):
                for i in range(2):
                    last = pe.matmul(PS[0:r, bank + i, :], zeros[:, 0:r], const("decayT"), start=True, stop=False, skip_group_check=True)
                return last

            for blk in range(NBLK):
                bank = 2 * (blk % 2)
                if blk >= 2:
                    pe.wait_ge(s["y_ready"], blk - 1)
                else:
                    pe.wait_ge(s["rs_taken"], NSUB)
                last = open_group(bank, P)
                if blk == 0:
                    last.then_inc(s["v_used"], CHUNK)
                with pe.Fori(0, NCH) as c:
                    for k in range(CHUNK):
                        pe.wait_ge(uv_in[1][k], c * 16 + 16 * (NCH * blk + 1))
                        pe.wait_ge(s["diag_ready"], c * CHUNK + (CHUNK * NCH * blk + k + 1))
                        for i in range(2):
                            last = pe.matmul(PS[:, bank + i, :], DIAG[k], VSLOT[k][:, 512 * i:512 * i + 512], start=False,
                                             stop=False, skip_group_check=True)
                        last.then_inc(s["v_used"], 1)

            pe.wait_ge(s["sel_ready"], NB)
            pe.transpose(PS[:, 4, 0:DB], sidx_row[0:DB, :], ident[0:DB, 0:DB])
            pe.transpose(PS[:, 4, P:P + DB], GATE[0:DB, SMP, :], ident[0:DB, 0:DB]).then_inc(s["sidx_turned"], 1)
            pe.wait_ge(s["sel_ready"], NB + 1)
            for b in range(DB):
                if b >= 2:
                    pe.wait_ge(s["u_used"], CHUNK * (NCH * NBLK + 1) + b - 1)
                for i in range(2):
                    last = pe.matmul(PS[:, 4 + 2 * (b % 2) + i, :], sel[0:DB, b, :], QR[0:DB, SMP, 512 * i:512 * i + 512],
                                     start=True, stop=True)
                last.then_inc(s["xb_ready"], 1)
            pe.wait_ge(s["u_used"], CHUNK * (NCH * NBLK + 2))
            open_group(6, DB)
            pe.wait_ge(s["smp_w"], 1)
            for b in range(DB):
                pe.wait_ge(uv_in[1][b], 16 * (NCH * NBLK + 1))
                for i in range(2):
                    last = pe.matmul(PS[0:DB, 6 + i, :], SWM[:, b, :], VSLOT[b][:, 512 * i:512 * i + 512], start=False,
                                     stop=(b == DB - 1), skip_group_check=True)
                last.then_inc(s["v_used"], 1)


_INS = ["x_prompt", "x_sample", "mem_prompt", "cache_diff_k", "cache_diff_v", "page_table", "state_ret", "cache_mem_k",
        "cache_mem_v", "g_mix", "w_in", "w_out", "lam_q1", "lam_k1", "lam_q2", "lam_k2", "rel_bias", "g_cross", "g_mem",
        "w_mq", "w_mk", "w_mv", "w_mo", "g_ffn", "w_pq", "sub_keys", "peer_u", "peer_v", "g_final"]
_OUTS = [(1, SEQ, D), (DB, 1, D), (1, 1, SEQ, H, 2, DH), (1, 1, SEQ, H, 2 * DH), (1, 1, H, P, P), (1, 1, MEM, H, MDH),
         (1, 1, MEM, H, MDH), (1, DB, 1, H, 2, DH), (1, DB, 1, H, 2 * DH), (1, DB, H, P, P)]


def kernel(**inputs):
    import concourse.bacc as bacc
    from concourse.bass_utils import run_bass_kernel_spmd as run

    nc = bacc.Bacc("TRN2", target_bir_lowering=False, num_devices=1)
    arrays, args = {}, []
    for name in _INS:
        a = np.ascontiguousarray(inputs[name])
        arrays[f"in_{name}"] = a
        args.append(nc.dram_tensor(f"in_{name}", a.shape, mybir.dt.from_np(a.dtype), kind="ExternalInput").ap())
    arrays["in_consts"] = shape_constants()
    args.append(nc.dram_tensor("in_consts", (P, CW), F32, kind="ExternalInput").ap())
    args.append(nc.dram_tensor("bias_lines", (H * P * TL,), F32, kind="Internal").ap())
    for i, shape in enumerate(_OUTS):
        args.append(nc.dram_tensor(f"out_{i}", shape, F32, kind="ExternalOutput").ap())
    build(nc, *args)
    r = run(nc, [arrays], core_ids=[0])
    return tuple(r.results[0][f"out_{i}"] for i in range(len(_OUTS)))
```

```python
from contextlib import ExitStack
import math

import numpy as np
import concourse.bass as bass
from concourse import mybir

F32 = mybir.dt.float32
U32 = mybir.dt.uint32
I32 = mybir.dt.int32
ALU = mybir.AluOpType
ACT = mybir.ActivationFunctionType
AX = mybir.AxisListType

P = 128
D = 1024
KD = D // P
SEQ = 512
NBLK = SEQ // P
DB = 8
NB = NBLK + 1
SMP = NBLK
ROWS = [P] * NBLK + [DB]
TOK = SEQ + DB
MEM = 256
NMEM = MEM // P
H = 4
HC = 2 * H
DH = 64
MDH = D // H
PAGES = 16
PAGE = 128
PAST = PAGES * PAGE
PPG = 4
GRP = PAGES // PPG
TPR = PAGE // 32
NBUCKET = 32
EPS = 1e-6
NEG = -1e30
LAM_INIT = 0.8 - 0.6 * math.exp(-0.0)
SCALE = DH ** -0.5
MSCALE = MDH ** -0.5
PH = 8
NSUB = 2 * PH
NK = 128
TOPK = 16
NSEL = PH * TOPK
NEXP = NK * NK
CHUNK = 8

TL = 640
PIECES = [("ident", 128), ("ones", 128), ("zeros", 128), ("decayT", H * P), ("kdec", H), ("gL", H), ("gam", H),
          ("sel", DB * P), ("mask8", DB * DB), ("hmask4", D), ("even", 1), ("odd", 1), ("dmask", DB * DB),
          ("part32", 1), ("iota16", TOPK),
          ("rot", NB * 256), ("qdec", H * P), ("hmask", 512), ("line", TL), ("past", 6 * P)]
CO = {}
_o = 0
for _n, _w in PIECES:
    CO[_n] = (_o, _w)
    _o += _w
CW = _o


def shape_constants():
    c = np.zeros((P, CW), np.float32)

    def put(name, value, rows=P):
        o, w = CO[name]
        c[:rows, o:o + w] = np.asarray(value, np.float32).reshape(-1, w)

    p = np.arange(P)
    put("ident", np.eye(P))
    put("ones", np.ones((P, P)))
    half = P // 2
    inv = (np.float32(1.0) / (np.float32(10000.0) ** (np.arange(half, dtype=np.float32) / np.float32(half)))).astype(np.float32)
    rot = np.zeros((P, NB, 4, half), np.float32)
    for b in range(NB):
        pos = np.float32(PAST) * np.ones(P, np.float32) if b == SMP else (b * P + p).astype(np.float32)
        ang = (pos[:, None] * inv[None, :]).astype(np.float32).astype(np.float64)
        rot[:, b, 0] = np.cos(ang) * P ** -0.5
        rot[:, b, 1] = np.sin(ang) * P ** -0.5
        rot[:, b, 2] = np.cos(ang)
        rot[:, b, 3] = np.sin(ang)
    put("rot", rot)
    lg = np.log(1.0 - 2.0 ** (-5.0 - np.arange(H)))
    dif = p[None, :] - p[:, None]
    dec = np.where(dif[:, None, :] >= 0, np.exp(np.maximum(dif, 0)[:, None, :] * lg[None, :, None]), 0.0)
    put("decayT", dec)
    put("qdec", np.broadcast_to(np.exp((p[None, :] + 1.0) * lg[:, None])[None], (P, H, P)))
    put("kdec", np.exp((P - 1.0 - p)[:, None] * lg[None, :]))
    put("gL", np.broadcast_to(np.exp(P * lg)[None], (P, H)))
    put("gam", np.broadcast_to(np.exp(lg)[None], (P, H)))
    sel = np.zeros((DB, DB, P))
    for b in range(DB):
        sel[b, b] = 1.0
    put("sel", sel, DB)
    put("mask8", np.broadcast_to(np.eye(DB)[None], (P, DB, DB)))
    dm = np.zeros((DB, DB, DB))
    for b in range(DB):
        dm[b, b] = 1.0
    put("dmask", dm, DB)
    hc = np.arange(HC)
    put("hmask", hc[:, None] // 2 == np.arange(512)[None, :] // P, HC)
    put("hmask4", np.arange(H)[:, None] == np.arange(D)[None, :] // MDH, H)

    def bucket(n):
        n = np.maximum(n, 0)
        me = NBUCKET // 2
        nf = np.maximum(n, 1).astype(np.float32)
        large = me + (np.log(nf / np.float32(me)) / np.float32(math.log(128 / me)) * np.float32(NBUCKET - me)).astype(np.int32)
        return np.where(n < me, n, np.minimum(large, NBUCKET - 1))

    rel = SEQ - 1 - np.arange(TL)
    line = np.zeros((NBUCKET + 1, TL))
    for m in range(TL):
        line[bucket(rel[m:m + 1])[0] if rel[m] >= 0 else NBUCKET, m] = 1.0
    put("line", line, NBUCKET + 1)
    past = np.zeros((NBUCKET, 6, P))
    for j in range(TPR):
        pos = ((GRP - 1) * PPG + p // 32) * PAGE + (p % 32) * TPR + j
        past[bucket(PAST - pos), j, p] = 1.0
    past[NBUCKET - 1, 4] = 1.0
    past[0, 5] = 1.0
    put("past", past, NBUCKET)
    put("even", hc % 2 == 0, HC)
    put("odd", hc % 2 == 1, HC)
    put("part32", p % 32)
    put("iota16", np.broadcast_to(np.arange(TOPK)[None], (P, TOPK)))
    return c


LAYOUT = [("const", CW), ("misc", 1104), ("dvs", 1024), ("xtm", 8 * 256), ("xt", 8 * 520), ("w", 2 * 4096), ("r1", 5120), ("r2", 7680),
          ("r3", 2560), ("ring", 3 * 2048), ("s", 1104), ("toe", 2048), ("g", 1024), ("t", 4096)]
BASE = {}
_o = 0
for _n, _w in LAYOUT:
    BASE[_n] = _o
    _o += _w
SBW = _o
KEYS_AHEAD = 16
RING = 3
PSUM_JOB = 4

GROUPS = ([0], list(range(1, NB)))
WTILES = ([("w_in", 512 * c, k) for c, k in ((4, "dq"), (5, "dk"), (6, "dv"))]
          + [("w_mk", 512 * i, "mem") for i in range(2)] + [("w_mv", 512 * i, "mem") for i in range(2)]
          + [("w_in", 512 * c, k) for c, k in ((3, "rg"), (0, "rq"), (1, "rk"), (2, "rv"))]
          + [(name, 512 * i, kind + str(g)) for g in range(2)
             for name, kind, n in (("w_out", "mix", 2), ("w_mq", "mq", 2), ("w_mo", "mo", 2), ("w_pq", "pq", 4))
             for i in range(n)])
JOBS = [(t, u) for t, (_, _, k) in enumerate(WTILES) if k[0:2] != "pq"
        for u in (range(NMEM) if k == "mem" else GROUPS[int(k[-1])] if k[-1] in "01" else range(NB))]
BY_DVE = ("rq", "rk", "mix0", "mo0", "mix1", "mo1")


def job_kind(j):
    return WTILES[JOBS[j][0]][2]


def first_job(kind):
    return next(j for j in range(len(JOBS)) if job_kind(j) == kind)


def taken_by(j):
    dve = job_kind(j) in BY_DVE
    return dve, sum((job_kind(i) in BY_DVE) == dve for i in range(j + 1))


TILES = ([("k", b, g) for b in range(DB) for g in range(GRP)] + [("st", b, 0) for b in range(DB)]
         + [("v", b, g) for b in range(DB) for g in range(GRP)])
TILE_BY_DVE = ("k",)
MTILES = [(kind, b) for kind in ("mk", "mv") for b in range(DB)]


def first_tile(kind):
    return next(t for t, w in enumerate(WTILES) if w[2] == kind)


def tile_no(kind, b, g=0):
    return TILES.index((kind, b, g))


def tile_used(n):
    dve = TILES[n][0] in TILE_BY_DVE
    return dve, sum((TILES[i][0] in TILE_BY_DVE) == dve for i in range(n + 1))


SEMS = """smp_scores_taken head_steps head_gate mtile_in0 mtile_in1 ident_loaded sq_saved const_loaded small_loaded
        mem_loaded x_loaded gains_loaded w_loaded0 w_loaded1 tile_in0 tile_in1 tile_in2 tile_used_dve tile_used_pe
        ss_cleared sumsq_done inv_done rstd_done xn_ready turned xt_done job_ready job_taken_dve job_taken_act vstep
        astep mem_stored0 mem_stored1 mem_stored2 mem_stored3 new_kv_stored lam_sums lam_exp lam_ready line_cols
        line_ps line_row line_stored toe_loaded past_ps past_ready kvidx_ready rows_turned rowsT_done scores_ready
        sc_biased nmax_ready exp_done w_ready wmat_turned wT_ready av_done dif_taken srow_saved qb_ready s_scored
        colmax_ready colmax_turned maxdiag_ready maxbc_ready sarg_ready sexp_done esum_ready z_ready coef_ready
        pv_done om_ready dif_row_ready rqd_ready ret_scores ret_sc_ready ret_out ret_state ret_rows rqm_ready
        kexp_ready outer_ready ns_ready ns_stored0 ns_stored1 ns_stored2 state_stored hsq_ready hrstd_done mix_ready
        x_again done_stored final_ready mkr_loaded mkr_turned mkT_done mv_loaded cs_ready cmax_ready cexp_done
        ce_turned ceT_ready co_ready co_taken cqb_ready cs_scored ccolmax_ready ccolmax_turned cmaxdiag_ready
        cmaxbc_ready csexp_done cesum_ready cz_ready ccoef_ready cpv_done com_ready crow_ready sk_loaded sk_turned
        skT_done rqp_ready rqp_taken rs_ready rs_taken sel_ready sidx_turned xb_ready gelu_done weight_ready
        diag_ready y_ready u_in0 u_in1 u_in2 u_in3 u_in4 u_in5 u_in6 u_in7 v_in0 v_in1 v_in2 v_in3 v_in4 v_in5 v_in6
        v_in7 u_used v_used idx_copied smp_w select_steps""".split()


def build(nc, x_prompt, x_sample, mem_prompt, cache_diff_k, cache_diff_v, page_table, state_ret, cache_mem_k,
          cache_mem_v, g_mix, w_in, w_out, lam_q1, lam_k1, lam_q2, lam_k2, rel_bias, g_cross, g_mem, w_mq, w_mk,
          w_mv, w_mo, g_ffn, w_pq, sub_keys, peer_u, peer_v, g_final, consts, line_dram,
          y_prompt, y_sample, new_k_p, new_v_p, state_p, mk_p, mv_p, new_k_s, new_v_s, state_s):
    weights = {"w_mk": w_mk, "w_mv": w_mv, "w_in": w_in, "w_out": w_out, "w_mq": w_mq, "w_mo": w_mo, "w_pq": w_pq}
    with ExitStack() as ctx:
        A = ctx.enter_context(nc.sbuf_tensor("arena", [P, SBW], F32))
        PS = ctx.enter_context(nc.psum_tensor("ps", [P, 8, 512], F32))
        s = {n: ctx.enter_context(nc.semaphore(n)) for n in SEMS}

        def at(region, off, n):
            return A[:, BASE[region] + off:BASE[region] + off + n]

        def const(name):
            return at("const", CO[name][0], CO[name][1])

        small_used = [0]

        def small(n):
            small_used[0] += n
            assert small_used[0] <= 1104
            return at("misc", small_used[0] - n, n)

        ident, ones, zeros = const("ident"), const("ones"), const("zeros")
        rot = const("rot").rearrange("p (b t d) -> p b t d", b=NB, t=4)
        sel = const("sel").rearrange("p (b m) -> p b m", b=DB)
        mask8 = const("mask8").rearrange("p (b j) -> p b j", b=DB)
        dmask = const("dmask").rearrange("p (b j) -> p b j", b=DB)

        XTM = at("xtm", 0, 8 * 256).rearrange("p (k t) -> p k t", k=KD)
        XT = at("xt", 0, 8 * 520).rearrange("p (k t) -> p k t", k=KD)
        W = [at("w", 4096 * i, 4096).rearrange("p (k n) -> p k n", k=KD) for i in range(2)]
        G = at("g", 0, 1024)
        GM = at("t", 0, 1024)
        XN = [at("t", 2048 + 1024 * i, 1024) for i in range(2)]
        X0 = at("r1", 0, 7 * 1024).rearrange("p (u d) -> p u d", u=7)
        DQT = at("r1", 0, H * TOK).rearrange("p (h t) -> p h t", h=H)
        DKT = at("r1", 2560, H * TOK).rearrange("p (h t) -> p h t", h=H)
        HR = at("r1", 0, NB * D).rearrange("p (b d) -> p b d", b=NB)
        DV = at("r2", 0, 2560).rearrange("p (b d) -> p b d", b=NB)
        RK = at("r2", 2560, 2560).rearrange("p (b d) -> p b d", b=NB)
        RG = at("r2", 5120, 2560).rearrange("p (b d) -> p b d", b=NB)
        QR = at("r2", 0, NB * D).rearrange("p (b d) -> p b d", b=NB)
        DIF = at("r3", 0, 2560).rearrange("p (b d) -> p b d", b=NB)
        MSTAGE = [at("r2", 2560 + 512 * i, 512) for i in range(4)]
        SLOT = [at("ring", 2048 * i, 2048) for i in range(RING)]
        S = at("s", 0, 1024)
        TOE = at("toe", 0, 2048).rearrange("p (h c) -> p h c", h=H)
        DVS = at("dvs", 0, 512)
        SRQ, SRK = at("g", 0, 512), at("g", 512, 512)
        SC = [at("t", 1024 * i, 1024).rearrange("p (c n) -> p c n", c=2) for i in range(2)]
        WM = [at("t", 2048 + 512 * i, 512) for i in range(2)]
        WT = [at("t", 3072 + 512 * i, 512) for i in range(2)]
        RQD, RKD = at("t", 0, 512), at("t", 512, 512)
        RSC = at("t", 1024, 512)
        STATE = at("t", 1536, 512)
        ROT_A, ROT_B = at("t", 2048, 512), at("t", 2560, 512)
        KEXP = [at("t", 2048 + 512 * i, 512) for i in range(2)]
        RQM = at("t", 3072, H * DB * DB).rearrange("p (h b j) -> p h b j", h=H, b=DB)
        OM = [at("t", 3072 + 512 * i, 512) for i in range(2)]
        SQ = [at("t", 2048 * i, 2048) for i in range(2)]

        ss = [small(8) for _ in range(7)]
        rstd = [small(8) for _ in range(7)]
        lamv = small(256)
        lsum, lexp, nlam = small(2), small(2), small(1)
        tab = small(H)
        pt_f, kv_idx = small(32), small(32)
        nmx, zsum = small(4), small(4)
        bias_s = small(24).rearrange("p (j h) -> p j h", j=6)
        sself, sself_e = small(HC), small(DB * HC).rearrange("p (b c) -> p b c", b=DB)
        sself_m = small(DB * HC).rearrange("p (b c) -> p b c", b=DB)
        colmax, mcol = small(64), small(1)
        esum = small(DB * HC).rearrange("p (b c) -> p b c", b=DB)
        rz, coef = small(DB), small(1)
        cl = small(DB * DB).rearrange("p (b j) -> p b j", b=DB)
        hss = small(NB * 8).rearrange("p (b h) -> p b h", b=NB)
        mdiag = small(64)
        TABB = at("t", 1024, 512).rearrange("p (h m) -> p h m", h=H)
        PTAB = at("t", 1536, DB * PAGES)
        LROW = at("ring", 0, H * TL).rearrange("p (h c) -> p h c", h=H)
        BFULL = at("t", 1536, 128).rearrange("p (x c) -> p x c", x=16)

        k_rows = cache_diff_k.rearrange("l g (r t) h c d -> (l g r) (t h c d)", t=TPR)
        v_rows = cache_diff_v.rearrange("l g (r t) h d -> (l g r) (t h d)", t=TPR)
        mk_rows = cache_mem_k.rearrange("l b (p t) h d -> (l b) p (t h d)", t=NMEM)
        mv_rows = cache_mem_v.rearrange("l b (p t) h d -> (l b) p (t h d)", t=NMEM)
        mem_out = {"w_mk": mk_p.rearrange("l b (u p) h d -> (l b u) p (h d)", p=P),
                   "w_mv": mv_p.rearrange("l b (u p) h d -> (l b u) p (h d)", p=P)}
        kp_out = new_k_p.rearrange("l b (u p) h c d -> (l b u) p (h c d)", p=P)
        vp_out = new_v_p.rearrange("l b (u p) h d -> (l b u) p (h d)", p=P)
        ks_out = new_k_s.rearrange("l b t h c d -> (l b t) (h c d)")
        vs_out = new_v_s.rearrange("l b t h d -> (l b t) (h d)")
        yp = y_prompt.rearrange("b (u p) d -> (b u) p d", p=P)
        line_rows = line_dram[0:H * P * TL].rearrange("(h p c) -> p h c", h=H, p=P)

        TURN = 7
        N_MIX = TURN
        N_EV = {}
        n = TURN + NB
        for g, blocks in enumerate(GROUPS):
            for name in ("cross", "q", "o", "ffn"):
                for b in blocks:
                    N_EV[name, b] = n
                    n += 1

        def turn_banks(n):
            return PS[:, 2 * (n % 2):2 * (n % 2) + 2, :].rearrange("p a c -> p (a c)")

        mem_jobs = [j for j in range(len(JOBS)) if job_kind(j) == "mem"]
        extra_jobs = [j for j in range(len(JOBS)) if job_kind(j) in ("mem", "rg")]

        def w_arrived(eng, t):
            eng.wait_ge((s["w_loaded0"], s["w_loaded1"])[t % 2], 16 * (t // 2 + 1))

        tile_in = (s["tile_in0"], s["tile_in1"], s["tile_in2"])
        mem_stored = (s["mem_stored0"], s["mem_stored1"], s["mem_stored2"], s["mem_stored3"])
        ns_stored = (s["ns_stored0"], s["ns_stored1"], s["ns_stored2"])

        def tile_arrived(eng, n):
            eng.wait_ge(tile_in[n % RING], 16 * (n // RING + 1))

        NSTORES = 2 * NB

        MKR = at("t", 0, 2048).rearrange("p (m d) -> p m d", m=NMEM)
        MKT = at("ring", 2048, 2048).rearrange("p (k m) -> p k m", k=KD)
        MV = at("r3", 0, 2048).rearrange("p (m d) -> p m d", m=NMEM)
        CE = [at("t", 1024 * i, 1024).rearrange("p (h m) -> p h m", h=H) for i in range(2)]
        CET = [at("t", 2048 + 1024 * i, 1024) for i in range(2)]
        COM = [at("t", 1024 * i, 1024) for i in range(2)]
        CS = at("s", 0, DB * NMEM * H)
        CS4 = CS.rearrange("p (b j h) -> p b j h", b=DB, j=NMEM)
        cneg, csum = small(2 * H), small(2 * H)
        ccol, cesum = at("s", 128, DB * H), at("s", 160, DB * H)
        cmd = at("s", 192, DB * H)
        cmx = at("s", 224, 1)
        crz = at("s", 232, DB)
        ccl = at("s", 240, DB * DB).rearrange("p (b j) -> p b j", b=DB)
        SKR = at("t", 0, 2048).rearrange("p (x d) -> p x d", x=NSUB)
        SKT = at("toe", 0, 2048).rearrange("p (x k) -> p x k", x=NSUB)
        QPT = [at("t", 2048 + TOK * i, TOK) for i in range(2)]
        WORK = at("t", 3200, NB * NK).rearrange("p (b k) -> p b k", b=NB)
        SSC = at("ring", 0, NSUB * NK)
        SWORK = [at("t", 3200 + NK * i, NK) for i in range(4)]
        JUNK = at("ring", 0, 1024)
        TV = at("r2", 5120, NB * NSUB * TOPK).rearrange("p (b x k) -> p b x k", b=NB, x=NSUB)
        TI = at("r2", 6400, NB * NSUB * TOPK).rearrange("p (b x k) -> p b x k", b=NB, x=NSUB)
        CAND, CAND2 = at("t", 0, 256), at("t", 256, 256)
        HOT = at("t", 512, 512)
        BV, BI = at("t", 1024, TOPK), at("t", 1040, TOPK)
        AF, CF, AU, CU = (at("t", 1056 + TOPK * i, TOPK) for i in range(4))
        TIF, GAC = at("t", 1120, 2 * TOPK), at("t", 1152, 2 * TOPK)
        bsum, bmax = at("t", 1184, PH), at("t", 1192, PH)
        SELECT_LINKS = 12
        IDX = at("const", CW - NB * NSEL, NB * NSEL).rearrange("p (b k) -> p b k", b=NB)
        GATE = at("s", 320, NB * NSEL).rearrange("p (b k) -> p b k", b=NB)
        sidx_row = at("t", 3968, NSEL)
        SIDX, SGATE = at("t", 1200, DB), at("t", 1208, DB)
        sdot, sgl = at("t", 1216, DB), at("t", 1224, DB)
        SWM = at("t", 1232, DB * DB).rearrange("p (b j) -> p b j", b=DB)
        GH, GE, gsum, rgate = at("t", 1344, TOPK), at("t", 1360, TOPK), at("t", 1376, 1), at("t", 1377, 1)
        dots, gl, WCH = small(CHUNK), small(CHUNK), small(CHUNK)
        ICH = [small(CHUNK) for _ in range(2)]
        VSLOT = ([at("const", CO["rot"][0] + 1024 * i, 1024) for i in range(3)] + [at("xtm", 1024 * i, 1024) for i in range(2)]
                 + [at("dvs", 0, 1024)] + [at("ring", 4096 + 1024 * i, 1024) for i in range(2)])
        WSLOT = [at("w", 1024 * i, 1024) for i in range(CHUNK)]
        DIAG = [at("t", 2048 + 128 * i, 128) for i in range(CHUNK)]
        uv_in = ((s["u_in0"], s["u_in1"], s["u_in2"], s["u_in3"], s["u_in4"], s["u_in5"], s["u_in6"], s["u_in7"]),
                 (s["v_in0"], s["v_in1"], s["v_in2"], s["v_in3"], s["v_in4"], s["v_in5"], s["v_in6"], s["v_in7"]))
        NCH = NSEL // CHUNK

        mtile_in = (s["mtile_in0"], s["mtile_in1"])

        def mtile_arrived(eng, n):
            eng.wait_ge(mtile_in[n % 2], 16 * (n // 2 + 1))


        PLACES = ([(("mix", i), n) for i, n in enumerate((0, 1, 0, 1, 0, 1, 1, 0))] + [(("turned keys", 0), 1)]
                  + [(("mq", i), n) for i, n in enumerate((1, 0, 1, 0, 1, 0, 1, 1))]
                  + [(("cross", b), 1) for b in GROUPS[1]]
                  + [(("mk", b), int(b == 5)) for b in range(DB)] + [(("mv", b), b % 2) for b in range(DB)]
                  + [(("mo", i), n) for i, n in enumerate((1, 1, 0, 1, 1, 0, 1, 1))]
                  + [(("ffn", 0), 1), (("ffn", 1), 1)]
                  + [(("router", x), int(x in (1, 4, 7, 9, 11))) for x in range(NSUB)])
        HALF_STEPS = 2 * NCH

        def half_steps_at(place):
            before = sum(n for i, (p, n) in enumerate(PLACES) if i < [q for q, _ in PLACES].index(place))
            return range(before, before + dict(PLACES)[place])

        assert sum(n for _, n in PLACES) == HALF_STEPS

        block = ctx.enter_context(nc.Block())

        @block.sync
        def _(sp):
            m = mem_prompt.rearrange("b (u p) d -> p (b u) d", p=P)
            sp.dma_start(X0[:, 0:NMEM, :], m).then_inc(s["mem_loaded"], 16)
            sp.dma_start(X0[:, NMEM:NMEM + NBLK, :], x_prompt.rearrange("b (u p) d -> p (b u) d", p=P)).then_inc(s["x_loaded"], 16)
            sp.dma_start(X0[0:DB, NMEM + SMP, :], x_sample.rearrange("b t d -> (b t) d")).then_inc(s["x_loaded"], 16)
            sp.dma_start(at("const", 0, 3 * P), consts[:, 0:3 * P]).then_inc(s["ident_loaded"], 16)
            sp.dma_start(GM, g_mem[0].partition_broadcast(P)).then_inc(s["mem_loaded"], 16)
            sp.dma_start(G, g_mix[0].partition_broadcast(P)).then_inc(s["gains_loaded"], 16)
            for i, v in enumerate((lam_q1, lam_k1, lam_q2, lam_k2)):
                sp.dma_start(lamv[:, 64 * i:64 * i + 64], v[0].partition_broadcast(P)).then_inc(s["small_loaded"], 16)
            sp.dma_start(tab[0:NBUCKET, :], rel_bias).then_inc(s["small_loaded"], 16)
            sp.dma_start(PTAB.bitcast(I32), page_table.rearrange("b g -> (b g)").partition_broadcast(P)
                         ).then_inc(s["small_loaded"], 16)
            for t, (name, c0, kind) in enumerate(WTILES):
                if t == 1:
                    sp.dma_start(at("const", 3 * P, CW - 3 * P), consts[:, 3 * P:CW]).then_inc(s["const_loaded"], 16)
                if kind == "mq0" and c0 == 0:
                    sp.wait_ge(s["hsq_ready"], 1)
                    sp.wait_ge(s["state_stored"], 16)
                    sp.dma_start(HR[:, 0:NBLK, :], x_prompt.rearrange("b (u p) d -> p (b u) d", p=P)).then_inc(s["x_again"], 16)
                    sp.dma_start(HR[0:DB, SMP, :], x_sample.rearrange("b t d -> (b t) d")).then_inc(s["x_again"], 16)
                    sp.dma_start(G, g_cross[0].partition_broadcast(P)).then_inc(s["gains_loaded"], 16)
                    for i in range(4):
                        sp.wait_ge(mem_stored[i], 32)
                    sp.dma_start(MKR, mk_p.rearrange("l b (u p) h d -> p (l b u) (h d)", p=P)).then_inc(s["mkr_loaded"], 16)
                    sp.wait_ge(s["turned"], N_MIX + NB)
                    sp.dma_start(MV, mv_p.rearrange("l b (u p) h d -> p (l b u) (h d)", p=P)).then_inc(s["mv_loaded"], 16)
                if kind == "mq1" and c0 == 0:
                    sp.wait_ge(s["xn_ready"], TURN + 2)
                    sp.dma_start(G, g_cross[0].partition_broadcast(P)).then_inc(s["gains_loaded"], 16)
                if kind in ("mo0", "mo1") and c0 == 0:
                    sp.wait_ge(s["xn_ready"], TURN + (1 if kind == "mo0" else 2 + len(GROUPS[1])))
                    sp.dma_start(G, g_ffn[0].partition_broadcast(P)).then_inc(s["gains_loaded"], 16)
                if kind == "pq1" and c0 == 0:
                    for n, (mkind, b) in enumerate(MTILES):
                        if n >= 2:
                            before, bb = MTILES[n - 2]
                            sp.wait_ge(*((s["tile_used_dve"], DB * GRP + bb + 1) if before == "mk" else (s["cpv_done"], bb + 1)))
                        elif n == 1:
                            sp.wait_ge(s["cs_ready"], NBLK)
                        else:
                            sp.wait_ge(s["tile_used_pe"], DB * (GRP + 1))
                        sp.dma_start(SLOT[n % 2], (mk_rows if mkind == "mk" else mv_rows)[b]).then_inc(mtile_in[n % 2], 16)
                if kind == "pq0" and c0 == 0:
                    sp.wait_ge(s["co_taken"], 1)
                    sp.dma_start(SKR, sub_keys[0].rearrange("h c k d -> k (h c) d")).then_inc(s["sk_loaded"], 16)
                if t >= 2:
                    before = WTILES[t - 2][2]
                    if before[0:2] == "pq":
                        sp.wait_ge(s["rqp_ready"], NSUB * int(before[2]) + 4 * (t - 1 - first_tile(before)))
                    else:
                        sp.wait_ge(s["job_ready"], max(j for j in range(len(JOBS)) if JOBS[j][0] <= t - 2) + 1)
                w = weights[name][0].rearrange("(k p) n -> p k n", p=P)
                sp.dma_start(W[t % 2], w[:, :, c0:c0 + 512]).then_inc((s["w_loaded0"], s["w_loaded1"])[t % 2], 16)

            sp.wait_ge(s["xn_ready"], TURN + 2 * NB)
            sp.dma_start(G, g_final.partition_broadcast(P)).then_inc(s["gains_loaded"], 16)
            for b in range(NB):
                sp.wait_ge(s["final_ready"], b + 1)
                if b == SMP:
                    sp.dma_start(y_sample.rearrange("b t d -> (b t) d"), QR[0:DB, b, :]).then_inc(s["done_stored"], 16)
                else:
                    sp.dma_start(yp[b], QR[:, b, :]).then_inc(s["done_stored"], 16)
            sp.wait_ge(s["done_stored"], 16 * NB)

        @block.gpsimd
        def _(pool):
            pool.wait_ge(s["kvidx_ready"], 1)
            for n, (kind, b, g) in enumerate(TILES):
                if n >= RING:
                    dve, c = tile_used(n - RING)
                    pool.wait_ge(s["tile_used_dve"] if dve else s["tile_used_pe"], c)
                    if TILES[n - RING][0] == "st":
                        prior = [m for m in range(n - RING + 1) if TILES[m][0] == "st" and m % RING == n % RING]
                        pool.wait_ge(ns_stored[n % RING], 16 * len(prior))
                else:
                    pool.wait_ge(s["line_stored"], 16)
                if kind in ("k", "v"):
                    pool.indirect_dma_start(SLOT[n % RING], None, k_rows if kind == "k" else v_rows,
                                            bass.IndirectOffsetOnAxis(kv_idx[:, b * GRP + g:b * GRP + g + 1].bitcast(U32), 0)
                                            ).then_inc(tile_in[n % RING], 16)
                else:
                    pool.dma_start(SLOT[n % RING][:, 0:512].rearrange("p (h e) -> p h e", h=H),
                                   state_ret[0, b].rearrange("h d e -> d h e")).then_inc(tile_in[n % RING], 16)

            def gather(slot, table, idx):
                return pool.indirect_dma_start(slot, None, table[0], bass.IndirectOffsetOnAxis(idx.bitcast(U32), 0))

            for blk in range(NBLK):
                if blk != 1:
                    pool.wait_ge(s["sel_ready"], max(blk, 1))
                uslot = WSLOT if blk else VSLOT
                with pool.Fori(0, NCH // 2) as c2:
                    if blk == 1:
                        pool.wait_ge(s["head_steps"], c2 * SELECT_LINKS + SELECT_LINKS)
                        pool.nop(nofuse=True)
                    for half in range(2):
                        pool.tensor_copy(ICH[half].bitcast(U32), IDX[:, blk, bass.ds(c2 * (2 * CHUNK) + half * CHUNK, CHUNK)].bitcast(U32)
                                         ).then_inc(s["idx_copied"], 1)
                        pool.wait_ge(s["idx_copied"], c2 * 2 + (NCH * blk + half + 1))
                        done = CHUNK * (NCH * blk + half)
                        for k in range(CHUNK):
                            pool.wait_ge(s["u_used"] if blk else s["v_used"], c2 * (2 * CHUNK) + (done + k + 1))
                            pool.nop(nofuse=True)
                            gather(uslot[k], peer_u, ICH[half][:, k:k + 1]).then_inc(uv_in[0][k], 16)
                        for k in range(CHUNK):
                            if blk:
                                pool.wait_ge(s["v_used"], c2 * (2 * CHUNK) + (done + k + 1))
                            else:
                                pool.wait_ge(s["u_used"], c2 * (2 * CHUNK) + (done + CHUNK + k + 1))
                            pool.nop(nofuse=True)
                            gather(VSLOT[k], peer_v, ICH[half][:, k:k + 1]).then_inc(uv_in[1][k], 16)
            pool.wait_ge(s["sel_ready"], NB)
            for b in range(DB):
                pool.wait_ge(s["u_used"], CHUNK * NCH * NBLK + b + 1)
                gather(WSLOT[b], peer_u, SIDX[:, b:b + 1]).then_inc(uv_in[0][b], 16)
            for b in range(DB):
                pool.wait_ge(s["v_used"], CHUNK * NCH * NBLK + b + 1)
                gather(VSLOT[b], peer_v, SIDX[:, b:b + 1]).then_inc(uv_in[1][b], 16)

        @block.scalar
        def _(act):
            steps = [0]

            def link(ins):
                steps[0] += 1
                ins.then_inc(s["astep"], 1)
                act.wait_ge(s["astep"], steps[0])

            def sumsq(stage, rows_of, junk):
                if stage == 0:
                    act.wait_ge(s["ss_cleared"], 1)
                last = None
                for u, r, src in rows_of:
                    last = act.activation(junk[0:r, :], src, ACT.Square, accum_out=ss[stage][0:r, u:u + 1])
                    if u < rows_of[-1][0]:
                        link(last)
                last.then_inc(s["sumsq_done"], 1)
                act.wait_ge(s["inv_done"], stage + 1)
                act.activation(rstd[stage], rstd[stage], ACT.Sqrt).then_inc(s["rstd_done"], 1)

            def xt_copy(n, dst, r):
                act.wait_ge(s["turned"], n + 1)
                act.copy(dst, turn_banks(n).rearrange("p (k t) -> p k t", k=KD)[:, :, 0:r]).then_inc(s["xt_done"], 1)

            def xt_block(n, b):
                xt_copy(n, XT[:, :, P * b:P * b + ROWS[b]], ROWS[b])

            def job_rows(j):
                return P if job_kind(j) == "mem" else ROWS[JOBS[j][1]]

            def take(j, dst):
                act.wait_ge(s["job_ready"], j + 1)
                kind = job_kind(j)
                act.activation(dst, PS[0:job_rows(j), PSUM_JOB + j % 2, :], ACT.Silu if kind == "rg" else ACT.Copy
                               ).then_inc(s["job_taken_act"], 1)

            act.wait_ge(s["mem_loaded"], 32)
            act.wait_ge(s["x_loaded"], 32)
            sumsq(0, [(u, P, X0[:, u, :]) for u in range(6)] + [(6, DB, X0[0:DB, 6, :])],
                  PS[:, 0:2, :].rearrange("p a c -> p (a c)"))
            for u in range(NMEM):
                xt_copy(u, XTM[:, :, P * u:P * u + P], P)
            for b in range(NB):
                xt_block(NMEM + b, b)
            for h in range(H):
                act.wait_ge(s["line_ps"], h + 1)
                act.copy(LROW[:, h, 0:512], PS[:, 6, :]).then_inc(s["line_cols"], 1)
                act.copy(LROW[:, h, 512:TL], PS[:, 7, 0:TL - 512]).then_inc(s["line_row"], 1)
            act.wait_ge(s["line_row"], H)
            act.wait_ge(s["line_cols"], H)
            act.dma_start(line_rows, LROW).then_inc(s["line_stored"], 16)
            act.wait_ge(s["line_stored"], 16)
            for h in range(H):
                o = h * P * TL + P - 1
                act.dma_start(TOE[:, h, :], line_dram[o:o + P * (TL - 1)].rearrange("(p c) -> p c", p=P)[:, 0:512]
                              ).then_inc(s["toe_loaded"], 16)
            act.wait_ge(s["lam_sums"], 1)
            act.activation(lexp, lsum, ACT.Exp).then_inc(s["lam_exp"], 1)

            def take_extra(j):
                t, u = JOBS[j]
                if job_kind(j) == "rg":
                    take(j, RG[0:ROWS[u], u, :])
                    return
                name, c0, _ = WTILES[t]
                i = j - mem_jobs[0]
                if i >= 4:
                    act.wait_ge(mem_stored[i % 4], 16 * (i // 4))
                take(j, MSTAGE[i % 4])
                taken(j)
                act.dma_start(mem_out[name][u][:, c0:c0 + 512], MSTAGE[i % 4]).then_inc(mem_stored[i % 4], 16)

            def taken(j):
                act.wait_ge(s["job_taken_act"], taken_by(j)[1])

            for b in range(NB):
                take(first_job("dq") + b, RK[0:ROWS[b], b, :])
            for kind, dst, outp, outs in (("dk", RG, kp_out, ks_out), ("dv", DV, vp_out, vs_out)):
                for b in range(NB):
                    j = first_job(kind) + b
                    take(j, dst[0:ROWS[b], b, :])
                    taken(j)
                    act.dma_start(outs if b == SMP else outp[b], dst[0:ROWS[b], b, :]).then_inc(s["new_kv_stored"], 16)

            act.wait_ge(s["new_kv_stored"], 16 * NSTORES)
            act.wait_ge(s["srow_saved"], 1)
            for st in range(NBLK * H + 1):
                if st < NBLK * H:
                    n = P * (st // H + 1)
                    act.wait_ge(s["nmax_ready"], st + 1)
                    for c in range(2):
                        last = act.activation(SC[st % 2][:, c, 0:n], SC[st % 2][:, c, 0:n], ACT.Exp,
                                              bias=nmx[:, 2 * (st % 2) + c:2 * (st % 2) + c + 1],
                                              accum_out=zsum[:, 2 * (st % 2) + c:2 * (st % 2) + c + 1])
                    last.then_inc(s["exp_done"], 1)
                if st < len(extra_jobs):
                    take_extra(extra_jobs[st])
                if st >= 1:
                    q = st - 1
                    n = P * (q // H + 1)
                    act.wait_ge(s["wmat_turned"], q + 1)
                    if q >= 2:
                        act.wait_ge(s["av_done"], q - 1)
                    act.copy(WT[q % 2][:, 0:n], PS[:, 6, 0:n]).then_inc(s["wT_ready"], 1)
                    if q % H == H - 1:
                        act.wait_ge(s["av_done"], q + 1)
                        act.copy(DIF[:, q // H, :], PS[:, 7, :]).then_inc(s["dif_taken"], 1)

            act.wait_ge(s["rowsT_done"], 3 * NB)
            for b in range(NB):
                take(first_job("rv") + b, DV[0:ROWS[b], b, :])

            act.wait_ge(s["s_scored"], 1)
            act.activation(S, S, ACT.Exp).then_inc(s["sexp_done"], 1)
            act.wait_ge(s["sarg_ready"], 1)
            act.activation(sself_e[0:DB], sself_e[0:DB], ACT.Exp).then_inc(s["sexp_done"], 1)

            for b in range(DB):
                n = tile_no("st", b)
                act.wait_ge(s["ns_ready"], b + 1)
                act.dma_start(state_s[0, b].rearrange("h d e -> d h e"),
                              SLOT[n % RING][:, 0:512].rearrange("p (h e) -> p h e", h=H)).then_inc(ns_stored[n % RING], 16)
            act.wait_ge(s["ret_state"], NBLK)
            act.dma_start(state_p[0, 0].rearrange("h d e -> d h e"), STATE.rearrange("p (h e) -> p h e", h=H)
                          ).then_inc(s["state_stored"], 16)
            for n, (b0, b1) in enumerate(((0, NBLK), (SMP, NB))):
                act.wait_ge(s["hsq_ready"], n + 1)
                act.activation(hss[:, b0:b1, :], hss[:, b0:b1, :], ACT.Sqrt).then_inc(s["hrstd_done"], 1)
                for b in range(b0, b1):
                    xt_block(N_MIX + b, b)
            junk = PS[:, 6:8, :].rearrange("p a c -> p (a c)")

            def h_rows(blocks):
                return [(b, ROWS[b], HR[0:ROWS[b], b, :]) for b in blocks]

            def peer_half_steps(g, place):
                for n in half_steps_at(place) if g else ():
                    if n % 2:
                        act.wait_ge(s["u_used"], CHUNK * (n // 2 + 2))
                        act.activation(gl, dots, ACT.Gelu).then_inc(s["gelu_done"], 1)

            def keep_sample_scores(x):
                act.wait_ge(s["rs_ready"], NSUB + x + 1)
                act.copy(SSC[0:DB, NK * x:NK * x + NK], PS[0:DB, 2 * (x % 2) + 1, 0:NK]).then_inc(s["smp_scores_taken"], 1)

            def gate_exp(b):
                act.wait_ge(s["sarg_ready"], 2 + b + (PH - 1 if b > 1 else 0))
                act.activation(GATE[0:ROWS[b], b, :], GATE[0:ROWS[b], b, :], ACT.Exp).then_inc(s["sexp_done"], 1)

            for g, blocks in enumerate(GROUPS):
                prompt = [b for b in blocks if b != SMP]
                for i in range(2 * len(blocks)):
                    peer_half_steps(g, ("mix", i))
                act.wait_ge(s["job_taken_dve"], taken_by(first_job(f"mq{g}") - 1)[1])
                sumsq(1 + 2 * g, h_rows(blocks), junk)
                peer_half_steps(g, ("turned keys", 0))
                for b in blocks:
                    xt_block(N_EV["cross", b], b)
                for i, j in enumerate(j for j in range(len(JOBS)) if job_kind(j) == f"mq{g}"):
                    t, b = JOBS[j]
                    c0 = WTILES[t][1]
                    take(j, QR[0:ROWS[b], b, c0:c0 + 512])
                    peer_half_steps(g, ("mq", i))
                for b in blocks:
                    xt_block(N_EV["q", b], b)

                for st in prompt + [prompt[-1] + 1]:
                    if st in prompt:
                        act.wait_ge(s["cmax_ready"], st + 1)
                        if st >= 2:
                            act.wait_ge(s["ce_turned"], st - 1)
                        for h in range(H):
                            z = H * (st % 2) + h
                            last = act.activation(CE[st % 2][:, h, :], PS[:, 2 * (st % 2) + h // 2, MEM * (h % 2):MEM * (h % 2) + MEM],
                                                  ACT.Exp, bias=cneg[:, z:z + 1], scale=MSCALE, accum_out=csum[:, z:z + 1])
                        last.then_inc(s["cexp_done"], 1)
                    if st > prompt[0]:
                        q = st - 1
                        act.wait_ge(s["ce_turned"], q + 1)
                        if q >= 2:
                            act.wait_ge(s["co_ready"], q - 1)
                        act.copy(CET[q % 2], PS[:, 4:6, :].rearrange("p a c -> p (a c)")).then_inc(s["ceT_ready"], 1)
                    peer_half_steps(g, ("cross", st))
                if g:
                    for b in range(DB):
                        peer_half_steps(g, ("mk", b))
                    act.wait_ge(s["cs_scored"], 1)
                    act.activation(CS, CS, ACT.Exp, scale=MSCALE).then_inc(s["csexp_done"], 1)
                    for b in range(DB):
                        peer_half_steps(g, ("mv", b))
                for b in blocks:
                    xt_block(N_EV["o", b], b)
                for i in range(2 * len(blocks)):
                    peer_half_steps(g, ("mo", i))
                act.wait_ge(s["job_taken_dve"], taken_by(max(j for j in range(len(JOBS)) if job_kind(j) == f"mo{g}"))[1])
                sumsq(2 + 2 * g, h_rows(blocks), junk)
                for b in blocks:
                    xt_block(N_EV["ffn", b], b)
                peer_half_steps(g, ("ffn", 0))
                peer_half_steps(g, ("ffn", 1))

                tokens = sum(ROWS[b] for b in blocks)
                for x in range(NSUB):
                    act.wait_ge(s["rqp_ready"], NSUB * g + x + 1)
                    if NSUB * g + x >= 2:
                        act.wait_ge(s["rs_ready"], NSUB * g + x - 1)
                    act.copy(QPT[x % 2][:, 0:tokens], PS[:, 4 + x % 2, 0:tokens]).then_inc(s["rqp_taken"], 1)
                    if g and x:
                        keep_sample_scores(x - 1)
                    peer_half_steps(g, ("router", x))
                if g:
                    keep_sample_scores(NSUB - 1)
                else:
                    gate_exp(0)

            def chunk(blk, c):
                act.wait_ge(s["u_used"], c * CHUNK + CHUNK * (NCH * blk + 2))
                act.activation(gl, dots, ACT.Gelu).then_inc(s["gelu_done"], 1)
                act.wait_ge(s["weight_ready"], c + (NCH * blk + 1))
                for k in range(CHUNK):
                    act.wait_ge(s["v_used"], c * CHUNK + (CHUNK * NCH * blk + k + 1))
                    act.activation(DIAG[k], ident, ACT.Copy, scale=WCH[:, k:k + 1]).then_inc(s["diag_ready"], 1)

            with act.Fori(0, PH) as h:
                act.wait_ge(s["sarg_ready"], h + 3)
                act.activation(GE, GH, ACT.Exp, accum_out=gsum).then_inc(s["sexp_done"], 1)
                for half in range(2):
                    chunk(1, h * 2 + half)
            gate_exp(2)
            for blk in range(2, NBLK):
                with act.Fori(0, NCH) as c:
                    chunk(blk, c)
                gate_exp(blk + 1)
            act.wait_ge(s["y_ready"], NBLK - 2)
            sumsq(5, h_rows(range(NBLK - 1)), JUNK)
            act.wait_ge(s["u_used"], CHUNK * (NCH * NBLK + 2))
            act.activation(sgl, sdot, ACT.Gelu).then_inc(s["gelu_done"], 1)
            act.wait_ge(s["y_ready"], NB - 1)
            sumsq(6, h_rows((NBLK - 1, SMP)), JUNK)

        @block.vector
        def _(dve):
            steps = [0]

            def link(ins):
                steps[0] += 1
                ins.then_inc(s["vstep"], 1)
                dve.wait_ge(s["vstep"], steps[0])

            def tt(out, a, b, op):
                return dve.tensor_tensor(out, a, b, op)

            def invert(stage):
                dve.wait_ge(s["sumsq_done"], stage + 1)
                link(dve.tensor_scalar(rstd[stage], ss[stage], 1.0 / D, EPS, ALU.mult, ALU.add))
                dve.reciprocal(rstd[stage], rstd[stage]).then_inc(s["inv_done"], 1)
                dve.wait_ge(s["rstd_done"], stage + 1)

            def normed(stage, u, r, src, gain, dst):
                return dve.scalar_tensor_tensor(out=dst[0:r, :], in0=src, scalar=rstd[stage][0:r, u:u + 1],
                                                in1=gain[0:r, :], op0=ALU.mult, op1=ALU.mult)

            for x in ss:
                dve.memset(x, 1.0)
            dve.memset(hss[:, :, :], 1.0).then_inc(s["ss_cleared"], 1)
            dve.wait_ge(s["ss_cleared"], 1)
            invert(0)
            dve.wait_ge(s["gains_loaded"], 16)
            for u in range(7):
                if u >= 2:
                    dve.wait_ge(s["turned"], u - 1)
                r = DB if u == 6 else P
                normed(0, u, r, X0[0:r, u, :], GM if u < NMEM else G, XN[u % 2]).then_inc(s["xn_ready"], 1)
            dve.wait_ge(s["const_loaded"], 16)
            dve.wait_ge(s["small_loaded"], 16 * 6)
            for q in range(PPG):
                last = dve.tensor_copy(pt_f[32 * q:32 * q + 32, :],
                                       PTAB[32 * q:32 * q + 32, :].bitcast(I32).rearrange("p (x q) -> p x q", q=PPG)[:, :, q])
            link(last)
            link(dve.tensor_scalar(pt_f, pt_f, 32.0, const("part32"), ALU.mult, ALU.add))
            dve.tensor_copy(kv_idx.bitcast(U32), pt_f).then_inc(s["kvidx_ready"], 1)
            link(dve.memset(tab[NBUCKET:NBUCKET + 1, :], NEG))
            dve.tensor_copy(TABB[0:NBUCKET + 1], tab[0:NBUCKET + 1, :].unsqueeze(2).broadcast_to([NBUCKET + 1, H, P])
                            ).then_inc(s["past_ready"], 1)
            lv = lamv.rearrange("p (a c d) -> p a c d", a=2, c=2)
            link(tt(lv[:, :, 0, :], lv[:, :, 0, :], lv[:, :, 1, :], ALU.mult))
            dve.tensor_reduce(lsum, lv[:, :, 0, :], AX.X, ALU.add).then_inc(s["lam_sums"], 1)
            dve.wait_ge(s["lam_exp"], 1)
            dve.scalar_tensor_tensor(out=nlam, in0=lexp[:, 1:2], scalar=-LAM_INIT, in1=lexp[:, 0:1], op0=ALU.add,
                                     op1=ALU.subtract).then_inc(s["lam_ready"], 1)
            dve.wait_ge(s["lam_ready"], 1)
            dve.wait_ge(s["past_ps"], 1)
            dve.tensor_copy(bias_s, PS[:, 7, 0:24].rearrange("p (j h) -> p j h", j=6)).then_inc(s["past_ready"], 1)
            dve.wait_ge(s["past_ready"], 2)

            def rows_t(e, dst):
                b = e % NB
                r = ROWS[b]
                dve.wait_ge(s["rows_turned"], e + 1)
                dve.tensor_copy(dst[:, :, P * b:P * b + r],
                                PS[:, e % 4, :].rearrange("p (h t) -> p h t", h=H)[:, :, 0:r]).then_inc(s["rowsT_done"], 1)

            def key_tile(b, g):
                n = tile_no("k", b, g)
                tile_arrived(dve, n)
                dve.wait_ge(s["qb_ready"], b + 1)
                t = SLOT[n % RING].rearrange("p (j x) -> p j x", j=TPR)
                link(tt(t, t, PS[:, 6 + b % 2, :].unsqueeze(1).broadcast_to([P, TPR, 512]), ALU.mult))
                dve.tensor_reduce(S[:, 128 * b + 32 * g:128 * b + 32 * g + 32],
                                  SLOT[n % RING].rearrange("p (x d) -> p x d", d=DH), AX.X, ALU.add).then_inc(s["tile_used_dve"], 1)

            keys = [(b, g) for b in range(DB) for g in range(GRP)]
            dve.wait_ge(s["job_taken_act"], taken_by(first_job("dq") + SMP)[1])
            dve.tensor_copy(SRQ[0:DB, :], RK[0:DB, SMP, :]).then_inc(s["sq_saved"], 1)
            for e in range(NB):
                rows_t(e, DQT)
            for k in keys[0:KEYS_AHEAD]:
                key_tile(*k)
            for e in range(NB, 2 * NB):
                rows_t(e, DKT)
            dve.wait_ge(s["job_taken_act"], taken_by(first_job("dv") + SMP)[1])
            dve.tensor_copy(SRK[0:DB, :], RG[0:DB, SMP, :])
            dve.tensor_copy(DVS[0:DB, :], DV[0:DB, SMP, :]).then_inc(s["srow_saved"], 1)
            dve.wait_ge(s["srow_saved"], 1)

            dve.wait_ge(s["toe_loaded"], 16 * H)
            for st in range(NBLK * H + 1):
                if st < NBLK * H:
                    i, h = st // H, st % H
                    n = P * (i + 1)
                    z = slice(2 * (st % 2), 2 * (st % 2) + 2)
                    dve.wait_ge(s["scores_ready"], st + 1)
                    b0 = 2 * (st % 2)
                    dve.scalar_tensor_tensor(out=SC[st % 2][:, :, 0:n], in0=PS[:, b0:b0 + 2, 0:n], scalar=SCALE,
                                             in1=TOE[:, h, 512 - n:512].unsqueeze(1).broadcast_to([P, 2, n]),
                                             op0=ALU.mult, op1=ALU.add).then_inc(s["sc_biased"], 1)
                    dve.wait_ge(s["sc_biased"], st + 1)
                    dve.tensor_reduce(nmx[:, z], SC[st % 2][:, :, 0:n], AX.X, ALU.max, negate=True).then_inc(s["nmax_ready"], 1)
                if st >= 1:
                    q = st - 1
                    n = P * (q // H + 1)
                    z = 2 * (q % 2)
                    dve.wait_ge(s["exp_done"], q + 1)
                    link(dve.reciprocal(zsum[:, z:z + 2], zsum[:, z:z + 2]))
                    link(tt(zsum[:, z + 1:z + 2], zsum[:, z + 1:z + 2], nlam, ALU.mult))
                    if q >= 2:
                        dve.wait_ge(s["wmat_turned"], q - 1)
                    link(dve.tensor_scalar(WM[q % 2][:, 0:n], SC[q % 2][:, 0, 0:n], zsum[:, z:z + 1], None, ALU.mult))
                    dve.scalar_tensor_tensor(out=WM[q % 2][:, 0:n], in0=SC[q % 2][:, 1, 0:n], scalar=zsum[:, z + 1:z + 2],
                                             in1=WM[q % 2][:, 0:n], op0=ALU.mult, op1=ALU.add).then_inc(s["w_ready"], 1)

            def rotary(j, dst, tq):
                b = JOBS[j][1]
                r = ROWS[b]
                dve.wait_ge(s["job_ready"], j + 1)
                src = PS[0:r, PSUM_JOB + j % 2, :].rearrange("p (x d) -> p x d", d=64)
                cos = rot[0:r, b, tq, :].unsqueeze(1).broadcast_to([r, 2 * H, 64])
                sin = rot[0:r, b, tq + 1, :].unsqueeze(1).broadcast_to([r, 2 * H, 64])
                a = ROT_A[0:r, :].rearrange("p (x d) -> p x d", d=64)
                c = ROT_B[0:r, :].rearrange("p (x d) -> p x d", d=64)
                tt(a, src, cos, ALU.mult)
                tt(c, src, sin, ALU.mult).then_inc(s["job_taken_dve"], 1)
                dve.wait_ge(s["job_taken_dve"], taken_by(j)[1])
                a4 = ROT_A[0:r, :].rearrange("p (h c d) -> p h c d", h=H, c=2)
                c4 = ROT_B[0:r, :].rearrange("p (h c d) -> p h c d", h=H, c=2)
                d4 = dst[0:r, b, :].rearrange("p (h c d) -> p h c d", h=H, c=2)
                tt(d4[:, :, 0, :], a4[:, :, 0, :], c4[:, :, 1, :], ALU.subtract)
                tt(d4[:, :, 1, :], a4[:, :, 1, :], c4[:, :, 0, :], ALU.add).then_inc(s["ret_rows"], 1)

            dve.wait_ge(s["new_kv_stored"], 16 * NSTORES)
            done = KEYS_AHEAD
            for kind, dst, tq, tdst, e0 in (("rq", DV, 0, DQT, 2 * NB), ("rk", RK, 2, DKT, 3 * NB)):
                if kind == "rk":
                    for i in range(4):
                        dve.wait_ge(mem_stored[i], 32)
                dve.wait_ge(s["av_done"], NBLK * H)
                for b in range(NB):
                    rotary(first_job(kind) + b, dst, tq)
                    key_tile(*keys[done])
                    done += 1
                for b in range(NB):
                    rows_t(e0 + b, tdst)
            for k in keys[done:]:
                key_tile(*k)

            b5 = BFULL[:, :, :].rearrange("p (g j) (h c) -> p g j h c", j=TPR, h=H)
            for g in range(GRP):
                for j in range(TPR):
                    src = bias_s[:, j if g == GRP - 1 else 4, :].unsqueeze(2).broadcast_to([P, H, 2])
                    last = dve.tensor_copy(b5[:, g, j], src)
            link(last)
            S3 = S.rearrange("p (b x) -> p b x", b=DB)
            S4 = S.rearrange("p (b x c) -> p b x c", b=DB, c=HC)
            link(dve.scalar_tensor_tensor(out=S3, in0=S3, scalar=SCALE,
                                          in1=BFULL.rearrange("p x c -> p (x c)").unsqueeze(1).broadcast_to([P, DB, 128]),
                                          op0=ALU.mult, op1=ALU.add))
            link(dve.tensor_reduce(colmax.rearrange("p (b c) -> p b c", b=DB), S4.rearrange("p b x c -> p b c x"),
                                   AX.X, ALU.max))
            link(tt(ROT_A[0:DB, :], SRQ[0:DB, :], SRK[0:DB, :], ALU.mult))
            link(dve.tensor_reduce(sself[0:DB, :], ROT_A[0:DB, :].rearrange("p (x d) -> p x d", d=DH), AX.X, ALU.add))
            link(dve.scalar_tensor_tensor(out=sself[0:DB, :].rearrange("p (h c) -> p h c", h=H),
                                          in0=sself[0:DB, :].rearrange("p (h c) -> p h c", h=H), scalar=SCALE,
                                          in1=bias_s[0:DB, 5, :].unsqueeze(2).broadcast_to([DB, H, 2]),
                                          op0=ALU.mult, op1=ALU.add))
            link(tt(sself_e[0:DB], sself[0:DB, :].unsqueeze(1).broadcast_to([DB, DB, HC]), dmask[0:DB], ALU.mult))
            link(dve.tensor_scalar(sself_m[0:DB], dmask[0:DB], 1.0, -NEG, ALU.subtract, ALU.mult))
            link(tt(sself_m[0:DB], sself_m[0:DB], sself_e[0:DB], ALU.add))
            tt(colmax[0:DB, :].rearrange("p (b c) -> p b c", b=DB), colmax[0:DB, :].rearrange("p (b c) -> p b c", b=DB),
               sself_m[0:DB], ALU.max).then_inc(s["colmax_ready"], 1)
            dve.wait_ge(s["colmax_turned"], 1)
            link(dve.tensor_reduce(mcol[0:64, :], PS[0:64, 0, 0:P], AX.X, ALU.max))
            dve.tensor_scalar(mdiag[0:64, :], ident[0:64, 0:64], mcol[0:64, :], None, ALU.mult).then_inc(s["maxdiag_ready"], 1)
            dve.wait_ge(s["maxbc_ready"], 1)
            mbc = PS[:, 1, 0:64].rearrange("p (b c) -> p b c", b=DB)
            tt(S4, S4, mbc.unsqueeze(2).broadcast_to([P, DB, 16, HC]), ALU.subtract).then_inc(s["s_scored"], 1)
            link(tt(sself_e[0:DB], sself_e[0:DB], mbc[0:DB], ALU.subtract))
            tt(sself_e[0:DB], sself_e[0:DB], dmask[0:DB], ALU.mult).then_inc(s["sarg_ready"], 1)
            dve.wait_ge(s["sexp_done"], 2)
            tt(sself_e[0:DB], sself_e[0:DB], dmask[0:DB], ALU.mult)
            dve.tensor_reduce(esum, S4.rearrange("p b x c -> p b c x"), AX.X, ALU.add).then_inc(s["esum_ready"], 1)
            dve.wait_ge(s["z_ready"], 1)
            link(dve.reciprocal(rz[0:HC, :], PS[0:HC, 0, 0:DB]))
            link(dve.scalar_tensor_tensor(out=coef[0:HC, :], in0=const("odd")[0:HC, :], scalar=nlam[0:HC, :],
                                          in1=const("even")[0:HC, :], op0=ALU.mult, op1=ALU.add))
            link(dve.tensor_scalar(rz[0:HC, :], rz[0:HC, :], coef[0:HC, :], None, ALU.mult))
            tt(cl[0:HC], mask8[0:HC], rz[0:HC, :].unsqueeze(2).broadcast_to([HC, DB, DB]), ALU.mult).then_inc(s["coef_ready"], 1)

            dve.wait_ge(s["rowsT_done"], 20)
            for h in range(H):
                last = tt(RQM[:, h], mask8, DQT[:, h, SEQ:TOK].unsqueeze(2).broadcast_to([P, DB, DB]), ALU.mult)
            last.then_inc(s["rqm_ready"], 1)
            gam4 = const("gam").unsqueeze(2).broadcast_to([P, H, P])

            def one_key(b):
                if b >= 2:
                    dve.wait_ge(s["outer_ready"], b - 1)
                dve.tensor_scalar(KEXP[b % 2][0:DB, :], RK[0:DB, SMP, :], dmask[0:DB, b, 0:1], None, ALU.mult
                                  ).then_inc(s["kexp_ready"], 1)

            one_key(0)
            for b in range(DB):
                n = tile_no("st", b)
                if b < DB - 1:
                    one_key(b + 1)
                tile_arrived(dve, n)
                st = SLOT[n % RING][:, 0:512]
                link(tt(st.rearrange("p (h e) -> p h e", h=H), st.rearrange("p (h e) -> p h e", h=H), gam4, ALU.mult))
                dve.wait_ge(s["outer_ready"], b + 1)
                tt(st, st, PS[:, 2 + b % 2, :], ALU.add).then_inc(s["ns_ready"], 1)
            dve.wait_ge(s["tile_used_pe"], DB)
            dve.tensor_copy(RK[0:DB, SMP, :], PS[0:DB, 7, :]).then_inc(s["ret_rows"], 1)

            gl4 = const("gL").unsqueeze(2).broadcast_to([P, H, P])
            for i in range(NBLK):
                if i:
                    dve.wait_ge(s["ret_out"], i)
                tt(RQD.rearrange("p (h t) -> p h t", h=H), DQT[:, :, P * i:P * i + P],
                   const("qdec").rearrange("p (h t) -> p h t", h=H), ALU.mult)
                tt(RKD.rearrange("p (h d) -> p h d", h=H), RK[:, i, :].rearrange("p (h d) -> p h d", h=H),
                   const("kdec").unsqueeze(2).broadcast_to([P, H, P]), ALU.mult).then_inc(s["rqd_ready"], 1)
                dve.wait_ge(s["ret_scores"], i + 1)
                tt(RSC, PS[:, 0, :], const("decayT"), ALU.mult).then_inc(s["ret_sc_ready"], 1)
                dve.wait_ge(s["rqd_ready"], i + 1)
                dve.wait_ge(s["ret_out"], i + 1)
                dve.tensor_copy(RK[:, i, :], PS[:, 2, :])
                if i == 0:
                    dve.tensor_copy(STATE, PS[:, 3, :]).then_inc(s["ret_state"], 1)
                else:
                    link(tt(STATE.rearrange("p (h e) -> p h e", h=H), STATE.rearrange("p (h e) -> p h e", h=H), gl4, ALU.mult))
                    tt(STATE, STATE, PS[:, 3, :], ALU.add).then_inc(s["ret_state"], 1)
                dve.wait_ge(s["ret_state"], i + 1)

            def head_norm(b0, b1, squares):
                r, w = ROWS[b0], 512 * (b1 - b0)
                for sq, src in zip(squares, (RK, DIF)):
                    last = tt(sq[0:r, 0:w].rearrange("p (b d) -> p b d", b=b1 - b0), src[0:r, b0:b1, :], src[0:r, b0:b1, :], ALU.mult)
                link(last)
                for i, sq in enumerate(squares):
                    last = dve.tensor_reduce(hss[0:r, b0:b1, H * i:H * i + H],
                                             sq[0:r, 0:w].rearrange("p (b h d) -> p b h d", b=b1 - b0, h=H), AX.X, ALU.add)
                link(last)
                part = hss[:, b0:b1, :]
                link(dve.tensor_scalar(part, part, 1.0 / P, EPS, ALU.mult, ALU.add))
                dve.reciprocal(part, part).then_inc(s["hsq_ready"], 1)
                dve.wait_ge(s["hrstd_done"], 1 + (b0 == SMP))
                link(dve.tensor_scalar(hss[:, b0:b1, H:2 * H], hss[:, b0:b1, H:2 * H], 1.0 - LAM_INIT, None, ALU.mult))
                for b in range(b0, b1):
                    def heads(x):
                        return x[0:r, b, :].rearrange("p (h d) -> p h d", h=H)

                    link(tt(heads(RK), heads(RK), hss[0:r, b, 0:H].unsqueeze(2).broadcast_to([r, H, P]), ALU.mult))
                    tt(RK[0:r, b, :], RK[0:r, b, :], RG[0:r, b, :], ALU.mult)
                    tt(heads(DIF), heads(DIF), hss[0:r, b, H:2 * H].unsqueeze(2).broadcast_to([r, H, P]), ALU.mult
                       ).then_inc(s["mix_ready"], 1)

            dve.wait_ge(s["state_stored"], 16)
            head_norm(0, NBLK, SQ)

            for b in range(DB):
                dve.wait_ge(s["pv_done"], b + 1)
                if b == 0:
                    dve.wait_ge(s["tile_used_pe"], DB)
                if b >= 2:
                    dve.wait_ge(s["dif_row_ready"], b - 1)
                tt(OM[b % 2][0:HC, :], PS[0:HC, 4 + b % 2, :], const("hmask")[0:HC, :], ALU.mult).then_inc(s["om_ready"], 1)
            dve.wait_ge(s["dif_row_ready"], DB)
            link(dve.tensor_copy(DIF[0:DB, SMP, :], PS[0:DB, 6, :]))
            head_norm(SMP, NB, (at("t", 2048, 512), at("t", 2560, 512)))

            def residual(kind, g):
                for i, j in enumerate(j for j in range(len(JOBS)) if job_kind(j) == kind + str(g)):
                    t, b = JOBS[j]
                    c0, r = WTILES[t][1], ROWS[b]
                    dve.wait_ge(s["job_ready"], j + 1)
                    tt(HR[0:r, b, c0:c0 + 512], HR[0:r, b, c0:c0 + 512], PS[0:r, PSUM_JOB + j % 2, :], ALU.add
                       ).then_inc(s["job_taken_dve"], 1)
                    peer_half_steps(g, (kind, i))

            def peer_half_steps(g, place):
                for n in half_steps_at(place) if g else ():
                    c = n // 2
                    if n % 2 == 0:
                        for k in range(CHUNK):
                            dve.wait_ge(uv_in[0][k], 16 * (c + 1))
                            dve.tensor_tensor_reduce(VSLOT[k], VSLOT[k], QR[:, 0, :], 1.0, 0.0, ALU.mult, ALU.add,
                                                     dots[:, k:k + 1]).then_inc(s["u_used"], 1)
                    else:
                        dve.wait_ge(s["gelu_done"], c + 1)
                        tt(WCH, gl, GATE[:, 0, CHUNK * c:CHUNK * c + CHUNK], ALU.mult).then_inc(s["weight_ready"], 1)
                        dve.wait_ge(s["weight_ready"], c + 1)
                        for k in range(CHUNK):
                            dve.wait_ge(uv_in[1][k], 16 * (c + 1))
                            dve.wait_ge(s["v_used"], CHUNK * (c + 1) + k)
                            dve.scalar_tensor_tensor(out=HR[:, 0, :], in0=VSLOT[k], scalar=WCH[:, k:k + 1], in1=HR[:, 0, :],
                                                     op0=ALU.mult, op1=ALU.add).then_inc(s["v_used"], 1)

            def top16(step, v, i, src, work):
                if step == 0:
                    return dve.max(v[:, 0:8], src), True
                if step == 1:
                    return dve.max_index(i[:, 0:8], v[:, 0:8], src), False
                if step == 2:
                    return dve.match_replace(work, v[:, 0:8], src, NEG), True
                if step == 3:
                    return dve.max(v[:, 8:16], work), True
                return dve.max_index(i[:, 8:16], v[:, 8:16], work), False

            def sample_top16(xs):
                for x0 in range(xs[0], xs[-1] + 1, 4):
                    for step in range(5):
                        for x in range(x0, x0 + 4):
                            last, read = top16(step, TV[0:DB, SMP, x, :], TI[0:DB, SMP, x, :].bitcast(U32),
                                               SSC[0:DB, NK * x:NK * x + NK], SWORK[x % 4][0:DB, :])
                        if read or step == 4:
                            link(last)

            TVF = TV.rearrange("p b x k -> p b (x k)")
            TIFB = TI.rearrange("p b x k -> p b (x k)")

            def select_head(order, b, h):
                r, k = ROWS[b], [0]

                def slink(ins, alone=False):
                    k[0] += 1
                    steps, before = (s["head_steps"], 0) if order == 1 else (s["select_steps"], order - (order > 1))
                    ins.then_inc(steps, 1)
                    dve.wait_ge(steps, h * SELECT_LINKS + (PH * SELECT_LINKS * before + k[0]))
                    if alone:
                        dve.nop(nofuse=True)

                v1, v2 = TVF[0:r, b, bass.ds(h * 32, TOPK)], TVF[0:r, b, bass.ds(h * 32 + TOPK, TOPK)]
                cand, work = CAND[0:r], CAND2[0:r]
                slink(tt(cand.rearrange("p (a c) -> p a c", a=TOPK), v1.unsqueeze(2).broadcast_to([r, TOPK, TOPK]),
                         v2.unsqueeze(1).broadcast_to([r, TOPK, TOPK]), ALU.add), alone=True)
                bv, bi = BV[0:r], BI[0:r].bitcast(U32)
                slink(dve.max(bv[:, 0:8], cand), alone=True)
                dve.max_index(bi[:, 0:8], bv[:, 0:8], cand)
                slink(dve.match_replace(work, bv[:, 0:8], cand, NEG), alone=True)
                slink(dve.max(bv[:, 8:16], work), alone=True)
                dve.tensor_copy(TIF[0:r], TIFB[0:r, b, bass.ds(h * 32, 2 * TOPK)].bitcast(U32))
                slink(dve.max_index(bi[:, 8:16], bv[:, 8:16], work))
                dve.tensor_copy(GATE[0:r, b, bass.ds(h * TOPK, TOPK)], bv)
                dve.tensor_scalar(AU[0:r].bitcast(U32), bi, 4, None, ALU.logical_shift_right)
                slink(dve.tensor_scalar(CU[0:r].bitcast(U32), bi, TOPK - 1, None, ALU.bitwise_and))
                dve.tensor_copy(AF[0:r], AU[0:r].bitcast(U32))
                slink(dve.tensor_copy(CF[0:r], CU[0:r].bitcast(U32)))
                hots = (HOT[0:r, 0:256].rearrange("p (k a) -> p k a", a=TOPK), HOT[0:r, 256:512].rearrange("p (k a) -> p k a", a=TOPK))
                iota = const("iota16")[0:r].unsqueeze(1).broadcast_to([r, TOPK, TOPK])
                for hot, pos in zip(hots, (AF, CF)):
                    last = tt(hot, pos[0:r].unsqueeze(2).broadcast_to([r, TOPK, TOPK]), iota, ALU.is_equal)
                slink(last)
                for half, hot in enumerate(hots):
                    last = tt(hot, hot, TIF[0:r, TOPK * half:TOPK * half + TOPK].unsqueeze(1).broadcast_to([r, TOPK, TOPK]), ALU.mult)
                slink(last)
                slink(dve.tensor_reduce(GAC[0:r], HOT[0:r, 0:512].rearrange("p (n a) -> p n a", a=TOPK), AX.X, ALU.add))
                slink(dve.scalar_tensor_tensor(out=GAC[0:r, 0:TOPK], in0=GAC[0:r, 0:TOPK], scalar=float(NK),
                                               in1=GAC[0:r, TOPK:2 * TOPK], op0=ALU.mult, op1=ALU.add))
                if b == SMP:
                    dve.tensor_copy(sidx_row[0:r, bass.ds(h * TOPK, TOPK)], GAC[0:r, 0:TOPK])
                slink(dve.tensor_copy(IDX[0:r, b, bass.ds(h * TOPK, TOPK)].bitcast(U32), GAC[0:r, 0:TOPK]))
                assert k[0] == SELECT_LINKS

            def gates(order, b):
                r = ROWS[b]
                gate3 = GATE[0:r, b, :].rearrange("p (h k) -> p h k", h=PH)
                link(dve.tensor_copy(bmax[0:r], gate3[:, :, 0]))
                tt(gate3, gate3, bmax[0:r].unsqueeze(2).broadcast_to([r, PH, TOPK]), ALU.subtract).then_inc(s["sarg_ready"], 1)
                dve.wait_ge(s["sexp_done"], 3 + order + (PH - 1 if order > 1 else 0))
                link(dve.tensor_reduce(bsum[0:r], gate3, AX.X, ALU.add))
                link(dve.reciprocal(bsum[0:r], bsum[0:r]))
                tt(gate3, gate3, bsum[0:r].unsqueeze(2).broadcast_to([r, PH, TOPK]), ALU.mult).then_inc(s["sel_ready"], 1)

            dve.wait_ge(s["x_again"], 32)
            for g, blocks in enumerate(GROUPS):
                prompt = [b for b in blocks if b != SMP]
                residual("mix", g)
                if g == 0:
                    for e in range(4):
                        dve.wait_ge(s["mkr_turned"], e + 1)
                        dve.tensor_copy(MKT[:, 2 * e:2 * e + 2, :].rearrange("p k m -> p (k m)"), PS[:, e, :]).then_inc(s["mkT_done"], 1)
                invert(1 + 2 * g)
                peer_half_steps(g, ("turned keys", 0))
                dve.wait_ge(s["gains_loaded"], 16 * (2 + 2 * g))
                for i, b in enumerate(blocks):
                    if i >= 2:
                        dve.wait_ge(s["turned"], N_EV["cross", b] - 1)
                    normed(1 + 2 * g, b, ROWS[b], HR[0:ROWS[b], b, :], G, XN[i % 2]).then_inc(s["xn_ready"], 1)
                for i in range(2 * len(blocks)):
                    peer_half_steps(g, ("mq", i))

                for st in prompt + [prompt[-1] + 1]:
                    if st in prompt:
                        z = slice(H * (st % 2), H * (st % 2) + H)
                        dve.wait_ge(s["cs_ready"], st + 1)
                        link(dve.tensor_reduce(cneg[:, z], PS[:, 2 * (st % 2):2 * (st % 2) + 2, :].rearrange("p a (c m) -> p (a c) m", c=2),
                                               AX.X, ALU.max, negate=True))
                        dve.tensor_scalar(cneg[:, z], cneg[:, z], MSCALE, None, ALU.mult).then_inc(s["cmax_ready"], 1)
                    if st > prompt[0]:
                        q = st - 1
                        z = slice(H * (q % 2), H * (q % 2) + H)
                        dve.wait_ge(s["co_ready"], q + 1)
                        link(dve.reciprocal(csum[:, z], csum[:, z]))
                        tt(QR[:, q, :].rearrange("p (h d) -> p h d", h=H),
                           PS[:, 6:8, :].rearrange("p a (c d) -> p (a c) d", c=2),
                           csum[:, z].unsqueeze(2).broadcast_to([P, H, MDH]), ALU.mult).then_inc(s["co_taken"], 1)
                    peer_half_steps(g, ("cross", st))

                if g:
                    for b in range(DB):
                        mtile_arrived(dve, b)
                        dve.wait_ge(s["cqb_ready"], b + 1)
                        t = SLOT[b % 2].rearrange("p (j x) -> p j x", j=NMEM)
                        q = PS[:, 2 * (b % 2):2 * (b % 2) + 2, :].rearrange("p a c -> p (a c)")
                        link(tt(t, t, q.unsqueeze(1).broadcast_to([P, NMEM, D]), ALU.mult))
                        dve.tensor_reduce(CS4[:, b], SLOT[b % 2].rearrange("p (j h d) -> p j h d", j=NMEM, h=H), AX.X, ALU.add
                                          ).then_inc(s["tile_used_dve"], 1)
                        peer_half_steps(g, ("mk", b))
                    dve.wait_ge(s["tile_used_dve"], DB * GRP + DB)
                    dve.tensor_reduce(ccol.rearrange("p (b h) -> p b h", b=DB), CS4.rearrange("p b j h -> p b h j"), AX.X, ALU.max
                                      ).then_inc(s["ccolmax_ready"], 1)
                    dve.wait_ge(s["ccolmax_turned"], 1)
                    link(dve.tensor_reduce(cmx[0:32, :], PS[0:32, 4, 0:P], AX.X, ALU.max))
                    dve.tensor_scalar(cmd[0:32, :], ident[0:32, 0:32], cmx[0:32, :], None, ALU.mult).then_inc(s["cmaxdiag_ready"], 1)
                    dve.wait_ge(s["cmaxbc_ready"], 1)
                    tt(CS4, CS4, PS[:, 5, 0:32].rearrange("p (b h) -> p b h", b=DB).unsqueeze(2).broadcast_to([P, DB, NMEM, H]),
                       ALU.subtract).then_inc(s["cs_scored"], 1)
                    dve.wait_ge(s["csexp_done"], 1)
                    dve.tensor_reduce(cesum.rearrange("p (b h) -> p b h", b=DB), CS4.rearrange("p b j h -> p b h j"), AX.X, ALU.add
                                      ).then_inc(s["cesum_ready"], 1)
                    dve.wait_ge(s["cz_ready"], 1)
                    link(dve.reciprocal(crz[0:H, :], PS[0:H, 4, 0:DB]))
                    tt(ccl[0:H], mask8[0:H], crz[0:H, :].unsqueeze(2).broadcast_to([H, DB, DB]), ALU.mult).then_inc(s["ccoef_ready"], 1)
                    for b in range(DB):
                        dve.wait_ge(s["cpv_done"], b + 1)
                        if b >= 2:
                            dve.wait_ge(s["crow_ready"], b - 1)
                        tt(COM[b % 2][0:H, :], PS[0:H, 2 * (b % 2):2 * (b % 2) + 2, :].rearrange("p a c -> p (a c)"),
                           const("hmask4")[0:H, :], ALU.mult).then_inc(s["com_ready"], 1)
                        peer_half_steps(g, ("mv", b))
                    dve.wait_ge(s["crow_ready"], DB)
                    dve.tensor_copy(QR[0:DB, SMP, :], PS[0:DB, 6:8, :].rearrange("p a c -> p (a c)")).then_inc(s["crow_ready"], 1)
                residual("mo", g)
                invert(2 + 2 * g)
                dve.wait_ge(s["gains_loaded"], 16 * (3 + 2 * g))
                dve.wait_ge(s["turned"], N_EV["ffn", blocks[0]])
                for b in blocks:
                    normed(2 + 2 * g, b, ROWS[b], HR[0:ROWS[b], b, :], G, QR[:, b, :]).then_inc(s["xn_ready"], 1)
                peer_half_steps(g, ("ffn", 0))
                if g == 0:
                    for e in range(4):
                        dve.wait_ge(s["sk_turned"], e + 1)
                        dve.tensor_copy(SKT[:, 4 * e:4 * e + 4, :].rearrange("p x k -> p (x k)"), PS[:, e, :]).then_inc(s["skT_done"], 1)
                peer_half_steps(g, ("ffn", 1))

                for x in range(NSUB):
                    dve.wait_ge(s["rs_ready"], NSUB * g + x + 1)
                    for step in range(5):
                        for b in prompt:
                            last, read = top16(step, TV[:, b, x, :], TI[:, b, x, :].bitcast(U32),
                                               PS[:, 2 * (x % 2), NK * b:NK * b + NK], WORK[:, b, :])
                        if step == 4:
                            last.then_inc(s["rs_taken"], 1)
                        elif read:
                            link(last)
                    if g == 0 and x % 2:
                        dve.wait_ge(s["rs_taken"], x + 1)
                        select_head(0, 0, x // 2)
                    peer_half_steps(g, ("router", x))
                if g:
                    dve.wait_ge(s["rs_taken"], 2 * NSUB)
                    select_head(1, 1, 0)
                else:
                    gates(0, 0)
                if g == 0:
                    dve.memset(mcol[0:1, :], 0.0).then_inc(s["u_used"], CHUNK)
                    dve.memset(coef[0:1, :], 0.0).then_inc(s["v_used"], CHUNK)

            def add_expert_rows(b):
                banks = 6 if b == SMP else 2 * (b % 2)
                r = ROWS[b]
                dve.wait_ge(s["v_used"], CHUNK * (NCH * min(b + 1, NBLK) + 1 + (b == SMP)))
                tt(HR[0:r, b, :], HR[0:r, b, :], PS[0:r, banks:banks + 2, :].rearrange("p a c -> p (a c)"), ALU.add
                   ).then_inc(s["y_ready"], 1)

            def dot_products(blk, c, h2):
                for k in range(CHUNK):
                    dve.wait_ge(uv_in[0][k], h2 * 32 + 16 * (NCH * blk + c + 1))
                    dve.tensor_tensor_reduce(WSLOT[k], WSLOT[k], QR[:, blk, :], 1.0, 0.0, ALU.mult, ALU.add,
                                             dots[:, k:k + 1]).then_inc(s["u_used"], 1)

            def weights_wanted(blk, c, h2):
                dve.wait_ge(s["gelu_done"], h2 * 2 + (NCH * blk + c + 1))
                dve.wait_ge(s["v_used"], h2 * (2 * CHUNK) + CHUNK * (NCH * blk + c + 1))

            def head_of_block_1(h, last=False):
                top = GATE[:, 1, bass.ds(h * TOPK, 1)].broadcast_to([P, TOPK])
                tt(GH, GATE[:, 1, bass.ds(h * TOPK, TOPK)], top, ALU.subtract).then_inc(s["sarg_ready"], 1)
                dot_products(1, 0, h)
                dve.wait_ge(s["sexp_done"], h + 4)
                dve.nop(nofuse=True)
                dve.reciprocal(rgate, gsum).then_inc(s["head_gate"], 1)
                dve.wait_ge(s["head_gate"], h + 1)
                dve.nop(nofuse=True)
                for half in range(2):
                    if half:
                        dot_products(1, 1, h)
                    weights_wanted(1, half, h)
                    dve.scalar_tensor_tensor(out=WCH, in0=GE[:, CHUNK * half:CHUNK * half + CHUNK], scalar=rgate, in1=gl,
                                             op0=ALU.mult, op1=ALU.mult).then_inc(s["weight_ready"], 1)
                    if half == 0 and not last:
                        select_head(1, 1, h + 1)
                select_head(2, 2, h)

            with dve.Fori(0, PH - 1) as h:
                head_of_block_1(h)
            head_of_block_1(PH - 1, last=True)
            gates(2, 2)
            dve.wait_ge(s["smp_scores_taken"], NSUB)
            for blk in range(2, NBLK):
                if blk == 2:
                    sample_top16(range(0, NSUB // 2))
                else:
                    sample_top16(range(NSUB // 2, NSUB))
                with dve.Fori(0, PH) as h:
                    for half in range(NCH // PH):
                        dot_products(blk, half, h)
                        weights_wanted(blk, half, h)
                        tt(WCH, gl, GATE[:, blk, bass.ds(h * (2 * CHUNK) + half * CHUNK, CHUNK)], ALU.mult).then_inc(s["weight_ready"], 1)
                    select_head(blk + 1, blk + 1, h)
                gates(blk + 1, blk + 1)
                add_expert_rows(blk - 1)

            def final_norm(stage, blocks):
                invert(stage)
                dve.wait_ge(s["gains_loaded"], 96)
                for b in blocks:
                    normed(stage, b, ROWS[b], HR[0:ROWS[b], b, :], G, QR[:, b, :]).then_inc(s["final_ready"], 1)

            final_norm(5, range(NBLK - 1))

            dve.wait_ge(s["sidx_turned"], 1)
            dve.tensor_copy(SIDX.bitcast(U32), PS[:, 4, 0:DB])
            dve.tensor_copy(SGATE, PS[:, 4, P:P + DB]).then_inc(s["sel_ready"], 1)
            dve.wait_ge(s["sel_ready"], NB)
            for b in range(DB):
                dve.wait_ge(uv_in[0][b], 16 * (NCH * NBLK + 1))
                dve.wait_ge(s["xb_ready"], b + 1)
                x = PS[:, 4 + 2 * (b % 2):6 + 2 * (b % 2), :].rearrange("p a c -> p (a c)")
                dve.tensor_tensor_reduce(WSLOT[b], WSLOT[b], x, 1.0, 0.0, ALU.mult, ALU.add, sdot[:, b:b + 1]).then_inc(s["u_used"], 1)
            add_expert_rows(NBLK - 1)
            dve.wait_ge(s["gelu_done"], NCH * NBLK + 1)
            link(tt(sgl, sgl, SGATE, ALU.mult))
            tt(SWM, mask8, sgl.unsqueeze(2).broadcast_to([P, DB, DB]), ALU.mult).then_inc(s["smp_w"], 1)
            add_expert_rows(SMP)

            final_norm(6, (NBLK - 1, SMP))


        @block.tensor
        def _(pe):
            def turn(n, chunks, r):
                if n >= 2:
                    pe.wait_ge(s["xt_done"], n - 1)
                tb = turn_banks(n)
                for k, c in enumerate(chunks):
                    last = pe.transpose(tb[:, P * k:P * k + r], c, ident[0:r, 0:r])
                last.then_inc(s["turned"], 1)

            def pieces(row, r):
                return [row[0:r, P * k:P * k + P] for k in range(row.shape[-1] // P)]

            pe.wait_ge(s["ident_loaded"], 16)
            for n in range(TURN):
                pe.wait_ge(s["xn_ready"], n + 1)
                r = DB if n == 6 else P
                turn(n, pieces(XN[n % 2], r), r)
            pe.wait_ge(s["const_loaded"], 16)
            pe.wait_ge(s["past_ready"], 1)
            for h in range(H):
                if h:
                    pe.wait_ge(s["line_row"], h)
                    pe.wait_ge(s["line_cols"], h)
                pe.matmul(PS[:, 6, :], TABB[0:NBUCKET + 1, h, :], const("line")[0:NBUCKET + 1, 0:512], start=True, stop=True)
                pe.matmul(PS[:, 7, 0:TL - 512], TABB[0:NBUCKET + 1, h, :], const("line")[0:NBUCKET + 1, 512:TL],
                          start=True, stop=True).then_inc(s["line_ps"], 1)
            pe.wait_ge(s["line_row"], H)
            for j in range(6):
                last = pe.matmul(PS[:, 7, 4 * j:4 * j + 4], const("past")[0:NBUCKET, P * j:P * j + P], tab[0:NBUCKET, :],
                                 start=True, stop=True)
            last.then_inc(s["past_ps"], 1)
            pe.wait_ge(s["xt_done"], TURN)

            def job(j):
                t, u = JOBS[j]
                r = P if job_kind(j) == "mem" else ROWS[u]
                xt = XTM if job_kind(j) == "mem" else XT
                w_arrived(pe, t)
                if j >= 2:
                    dve, c = taken_by(j - 2)
                    pe.wait_ge(s["job_taken_dve"] if dve else s["job_taken_act"], c)
                for k in range(KD):
                    last = pe.matmul(PS[0:r, PSUM_JOB + j % 2, :], xt[:, k, P * u:P * u + r], W[t % 2][:, k, :],
                                     start=(k == 0), stop=(k == KD - 1))
                last.then_inc(s["job_ready"], 1)

            def jobs(kind, between=None):
                done = [j for j in range(len(JOBS)) if job_kind(j) == kind]
                for j in done:
                    job(j)
                    if between:
                        between(j - done[0])

            def rows_turn(e, row, b, ready, count):
                r = ROWS[b]
                pe.wait_ge(ready, count)
                if e >= 4:
                    pe.wait_ge(s["rowsT_done"], e - 3)
                for h in range(H):
                    last = pe.transpose(PS[:, e % 4, P * h:P * h + r], row[0:r, P * h:P * h + P], ident[0:r, 0:r])
                last.then_inc(s["rows_turned"], 1)

            def query_bc(b):
                if b >= 2:
                    pe.wait_ge(s["tile_used_dve"], GRP * (b - 1))
                pe.matmul(PS[:, 6 + b % 2, :], sel[0:DB, b, :], SRQ[0:DB, :], start=True, stop=True).then_inc(s["qb_ready"], 1)

            jobs("dq")
            pe.wait_ge(s["past_ready"], 2)
            pe.wait_ge(s["sq_saved"], 1)
            query_bc(0)
            query_bc(1)
            for b in range(NB):
                rows_turn(b, RK[:, b, :], b, s["job_taken_act"], taken_by(first_job("dq") + b)[1])
            jobs("dk", lambda i: query_bc(2) if i == 3 else None)
            jobs("dv", lambda i: query_bc(3) if i == 1 else None)
            for b in range(NB):
                rows_turn(NB + b, RG[:, b, :], b, s["job_taken_act"], taken_by(first_job("dk") + b)[1])

            pe.wait_ge(s["rowsT_done"], 2 * NB)
            pe.wait_ge(s["job_taken_act"], taken_by(first_job("dv") + SMP)[1])
            pe.wait_ge(s["past_ready"], 2)
            for st in range(NBLK * H + 1):
                if st < NBLK * H:
                    i, h = st // H, st % H
                    n = P * (i + 1)
                    if st >= 2:
                        pe.wait_ge(s["sc_biased"], st - 1)
                    for c in range(2):
                        last = pe.matmul(PS[:, 2 * (st % 2) + c, 0:n], DQT[DH * c:DH * c + DH, h, P * i:P * i + P],
                                         DKT[DH * c:DH * c + DH, h, 0:n], start=True, stop=True)
                    last.then_inc(s["scores_ready"], 1)
                if st < len(extra_jobs):
                    j = extra_jobs[st]
                    job(j)
                if st >= 1:
                    q = st - 1
                    i, h = q // H, q % H
                    pe.wait_ge(s["w_ready"], q + 1)
                    if q >= 1:
                        pe.wait_ge(s["wT_ready"], q)
                    for k in range(i + 1):
                        last = pe.transpose(PS[:, 6, P * k:P * k + P], WM[q % 2][:, P * k:P * k + P], ident)
                    last.then_inc(s["wmat_turned"], 1)
                    if h == 0 and i >= 1:
                        pe.wait_ge(s["dif_taken"], i)
                    pe.wait_ge(s["wT_ready"], q + 1)
                    for k in range(i + 1):
                        last = pe.matmul(PS[:, 7, P * h:P * h + P], WT[q % 2][:, P * k:P * k + P], DV[:, k, P * h:P * h + P],
                                         start=(k == 0), stop=(k == i))
                    last.then_inc(s["av_done"], 1)
            pe.wait_ge(s["dif_taken"], NBLK)
            pe.wait_ge(s["srow_saved"], 1)

            query_bc(4)
            query_bc(5)
            jobs("rq")
            for b in range(NB):
                rows_turn(2 * NB + b, DV[:, b, :], b, s["ret_rows"], b + 1)
            query_bc(6)
            jobs("rk")
            for b in range(NB):
                rows_turn(3 * NB + b, RK[:, b, :], b, s["ret_rows"], NB + b + 1)
            jobs("rv", lambda i: query_bc(7) if i == 2 else None)

            pe.wait_ge(s["rowsT_done"], 20)
            pe.wait_ge(s["colmax_ready"], 1)
            pe.transpose(PS[0:64, 0, 0:P], colmax, ident).then_inc(s["colmax_turned"], 1)
            pe.wait_ge(s["maxdiag_ready"], 1)
            pe.matmul(PS[:, 1, 0:64], ones[0:64, :], mdiag[0:64, :], start=True, stop=True).then_inc(s["maxbc_ready"], 1)
            pe.wait_ge(s["esum_ready"], 1)
            for b in range(DB):
                pe.matmul(PS[0:HC, 0, b:b + 1], esum[:, b, :], ones[:, 0:1], start=True, stop=False)
                last = pe.matmul(PS[0:HC, 0, b:b + 1], sself_e[0:DB, b, :], ones[0:DB, 0:1], start=False, stop=True)
            last.then_inc(s["z_ready"], 1)

            pe.wait_ge(s["tile_used_dve"], GRP * DB)
            pe.wait_ge(s["job_taken_act"], taken_by(first_job("rv") + SMP)[1])
            pe.wait_ge(s["rqm_ready"], 1)
            pe.matmul(PS[0:DB, 7, :], zeros[:, 0:DB], const("decayT"), start=True, stop=False, skip_group_check=True)

            def outer(b):
                pe.wait_ge(s["kexp_ready"], b + 1)
                if b >= 2:
                    pe.wait_ge(s["ns_ready"], b - 1)
                for h in range(H):
                    last = pe.matmul(PS[:, 2 + b % 2, P * h:P * h + P], KEXP[b % 2][0:DB, P * h:P * h + P],
                                     DV[0:DB, SMP, P * h:P * h + P], start=True, stop=True)
                last.then_inc(s["outer_ready"], 1)

            outer(0)
            for b in range(DB):
                if b < DB - 1:
                    outer(b + 1)
                pe.wait_ge(s["ns_ready"], b + 1)
                n = tile_no("st", b)
                for h in range(H):
                    last = pe.matmul(PS[0:DB, 7, P * h:P * h + P], RQM[:, h, b, :], SLOT[n % RING][:, P * h:P * h + P],
                                     start=False, stop=(b == DB - 1 and h == H - 1), skip_group_check=True)
                last.then_inc(s["tile_used_pe"], 1)

            pe.wait_ge(s["coef_ready"], 1)
            pe.wait_ge(s["ns_ready"], DB)
            for i in range(NBLK):
                if i:
                    pe.wait_ge(s["ret_sc_ready"], i)
                for h in range(H):
                    last = pe.matmul(PS[:, 0, P * h:P * h + P], DKT[:, h, P * i:P * i + P], DQT[:, h, P * i:P * i + P],
                                     start=True, stop=True)
                last.then_inc(s["ret_scores"], 1)
                pe.wait_ge(s["rqd_ready"], i + 1)
                pe.wait_ge(s["ret_sc_ready"], i + 1)
                if i:
                    pe.wait_ge(s["ret_state"], i)
                for h in range(H):
                    pe.matmul(PS[:, 2, P * h:P * h + P], RSC[:, P * h:P * h + P], DV[:, i, P * h:P * h + P],
                              start=True, stop=(i == 0))
                    if i:
                        pe.matmul(PS[:, 2, P * h:P * h + P], RQD[:, P * h:P * h + P], STATE[:, P * h:P * h + P],
                                  start=False, stop=True)
                    last = pe.matmul(PS[:, 3, P * h:P * h + P], RKD[:, P * h:P * h + P], DV[:, i, P * h:P * h + P],
                                     start=True, stop=True)
                last.then_inc(s["ret_out"], 1)

            pe.matmul(PS[0:DB, 6, :], zeros[:, 0:DB], const("decayT"), start=True, stop=False, skip_group_check=True)

            def weigh(b):
                pe.wait_ge(s["om_ready"], b + 1)
                pe.matmul(PS[0:DB, 6, :], cl[0:HC, b, :], OM[b % 2][0:HC, :], start=False, stop=(b == DB - 1),
                          skip_group_check=True).then_inc(s["dif_row_ready"], 1)

            def mixed_turn(b):
                pe.wait_ge(s["mix_ready"], b + 1)
                turn(N_MIX + b, pieces(RK[:, b, :], ROWS[b]) + pieces(DIF[:, b, :], ROWS[b]), ROWS[b])

            for b in range(DB):
                if b >= 2:
                    pe.wait_ge(s["om_ready"], b - 1)
                for g in range(GRP):
                    n = tile_no("v", b, g)
                    tile_arrived(pe, n)
                    for j in range(TPR):
                        c0 = 128 * b + 32 * g + 8 * j
                        last = pe.matmul(PS[0:HC, 4 + b % 2, :], S[:, c0:c0 + HC], SLOT[n % RING][:, 512 * j:512 * j + 512],
                                         start=(g == 0 and j == 0), stop=False)
                    last.then_inc(s["tile_used_pe"], 1)
                pe.matmul(PS[0:HC, 4 + b % 2, :], sself_e[0:DB, b, :], DVS[0:DB, :], start=False, stop=True
                          ).then_inc(s["pv_done"], 1)
                if b >= 1:
                    weigh(b - 1)
                if b >= DB - NBLK:
                    mixed_turn(b - DB + NBLK)
            weigh(DB - 1)

            def xt_ready(n):
                pe.wait_ge(s["xt_done"], n)

            xt_ready(N_MIX + 1)
            for g, blocks in enumerate(GROUPS):
                prompt = [b for b in blocks if b != SMP]
                jobs(f"mix{g}")
                if g == 0:
                    mixed_turn(SMP)
                    xt_ready(N_MIX + NB)
                    pe.wait_ge(s["mkr_loaded"], 16)
                    for e in range(4):
                        for k in range(2):
                            for m in range(NMEM):
                                last = pe.transpose(PS[:, e, MEM * k + P * m:MEM * k + P * m + P],
                                                    MKR[:, m, P * (2 * e + k):P * (2 * e + k) + P], ident)
                        last.then_inc(s["mkr_turned"], 1)
                    pe.wait_ge(s["mkT_done"], 4)

                for i, b in enumerate(blocks):
                    pe.wait_ge(s["xn_ready"], TURN + (2 if g else 0) + i + 1)
                    turn(N_EV["cross", b], pieces(XN[i % 2], ROWS[b]), ROWS[b])
                xt_ready(N_EV["cross", blocks[-1]] + 1)
                jobs(f"mq{g}")
                for i, b in enumerate(blocks):
                    pe.wait_ge(s["job_taken_act"], taken_by(first_job(f"mq{g}") + len(blocks) + i)[1])
                    turn(N_EV["q", b], pieces(QR[:, b, :], ROWS[b]), ROWS[b])
                xt_ready(N_EV["q", blocks[-1]] + 1)

                pe.wait_ge(s["mv_loaded"], 16)
                for st in prompt + [prompt[-1] + 1]:
                    if st in prompt:
                        if st >= 2:
                            pe.wait_ge(s["cexp_done"], st - 1)
                        for h in range(H):
                            for k in range(2):
                                last = pe.matmul(PS[:, 2 * (st % 2) + h // 2, MEM * (h % 2):MEM * (h % 2) + MEM],
                                                 XT[:, 2 * h + k, P * st:P * st + P], MKT[:, 2 * h + k, :],
                                                 start=(k == 0), stop=(k == 1))
                        last.then_inc(s["cs_ready"], 1)
                    if st > prompt[0]:
                        q = st - 1
                        pe.wait_ge(s["cexp_done"], q + 1)
                        if q >= 1:
                            pe.wait_ge(s["ceT_ready"], q)
                        for h in range(H):
                            for m in range(NMEM):
                                x = NMEM * h + m
                                last = pe.transpose(PS[:, 4 + x // 4, P * (x % 4):P * (x % 4) + P], CE[q % 2][:, h, P * m:P * m + P], ident)
                        last.then_inc(s["ce_turned"], 1)
                        pe.wait_ge(s["ceT_ready"], q + 1)
                        if q >= 1:
                            pe.wait_ge(s["co_taken"], q)
                        for h in range(H):
                            for m in range(NMEM):
                                x = P * (NMEM * h + m)
                                last = pe.matmul(PS[:, 6 + h // 2, MDH * (h % 2):MDH * (h % 2) + MDH], CET[q % 2][:, x:x + P],
                                                 MV[:, m, MDH * h:MDH * h + MDH], start=(m == 0), stop=(m == NMEM - 1))
                        last.then_inc(s["co_ready"], 1)

                if g:
                    for b in range(DB):
                        if b >= 2:
                            pe.wait_ge(s["tile_used_dve"], DB * GRP + b - 1)
                        for i in range(2):
                            last = pe.matmul(PS[:, 2 * (b % 2) + i, :], sel[0:DB, b, :], QR[0:DB, SMP, 512 * i:512 * i + 512],
                                             start=True, stop=True)
                        last.then_inc(s["cqb_ready"], 1)
                    pe.wait_ge(s["ccolmax_ready"], 1)
                    pe.transpose(PS[0:32, 4, 0:P], ccol, ident).then_inc(s["ccolmax_turned"], 1)
                    pe.wait_ge(s["cmaxdiag_ready"], 1)
                    pe.matmul(PS[:, 5, 0:32], ones[0:32, :], cmd[0:32, :], start=True, stop=True).then_inc(s["cmaxbc_ready"], 1)
                    pe.wait_ge(s["cesum_ready"], 1)
                    for b in range(DB):
                        last = pe.matmul(PS[0:H, 4, b:b + 1], cesum[:, H * b:H * b + H], ones[:, 0:1], start=True, stop=True)
                    last.then_inc(s["cz_ready"], 1)
                    pe.wait_ge(s["co_taken"], NBLK)
                    pe.wait_ge(s["ccoef_ready"], 1)
                    for i in range(2):
                        pe.matmul(PS[0:DB, 6 + i, :], zeros[:, 0:DB], const("decayT"), start=True, stop=False, skip_group_check=True)

                    def cweigh(b):
                        pe.wait_ge(s["com_ready"], b + 1)
                        for i in range(2):
                            last = pe.matmul(PS[0:DB, 6 + i, :], ccl[0:H, b, :], COM[b % 2][0:H, 512 * i:512 * i + 512],
                                             start=False, stop=(b == DB - 1), skip_group_check=True)
                        last.then_inc(s["crow_ready"], 1)

                    for b in range(DB):
                        if b >= 2:
                            pe.wait_ge(s["com_ready"], b - 1)
                        mtile_arrived(pe, DB + b)
                        for i in range(2):
                            for j in range(NMEM):
                                last = pe.matmul(PS[0:H, 2 * (b % 2) + i, :], CS4[:, b, j, :],
                                                 SLOT[b % 2][:, D * j + 512 * i:D * j + 512 * i + 512], start=(j == 0), stop=(j == 1))
                        last.then_inc(s["cpv_done"], 1)
                        if b >= 1:
                            cweigh(b - 1)
                    cweigh(DB - 1)
                for b in blocks:
                    if b < NBLK:
                        pe.wait_ge(s["co_taken"], b + 1)
                    else:
                        pe.wait_ge(s["crow_ready"], DB + 1)
                    turn(N_EV["o", b], pieces(QR[:, b, :], ROWS[b]), ROWS[b])
                xt_ready(N_EV["o", blocks[-1]] + 1)
                jobs(f"mo{g}")

                for i, b in enumerate(blocks):
                    pe.wait_ge(s["xn_ready"], TURN + (2 + len(blocks) if g else 1) + i + 1)
                    turn(N_EV["ffn", b], pieces(QR[:, b, :], ROWS[b]), ROWS[b])
                xt_ready(N_EV["ffn", blocks[-1]] + 1)
                if g == 0:
                    pe.wait_ge(s["sk_loaded"], 16)
                    for e in range(4):
                        for k in range(4):
                            last = pe.transpose(PS[:, e, P * k:P * k + P], SKR[:, 4 * e + k, :], ident)
                        last.then_inc(s["sk_turned"], 1)
                    pe.wait_ge(s["skT_done"], 4)

                tokens, first = sum(ROWS[b] for b in blocks), P * blocks[0]

                def router_scores(x):
                    pe.wait_ge(s["rqp_taken"], NSUB * g + x + 1)
                    if NSUB * g + x >= 2:
                        pe.wait_ge(s["rs_taken"], NSUB * g + x - 1)
                    if g and x >= 2:
                        pe.wait_ge(s["smp_scores_taken"], x - 1)
                    for b in blocks:
                        r = ROWS[b]
                        last = pe.matmul(PS[0:r, 2 * (x % 2) + (b == SMP), (0 if b == SMP else NK * b):(NK if b == SMP else NK * b + NK)],
                                         QPT[x % 2][:, P * b - first:P * b - first + r], SKT[:, x, :], start=True, stop=True)
                    last.then_inc(s["rs_ready"], 1)

                for x in range(NSUB):
                    t = first_tile(f"pq{g}") + x // 4
                    w_arrived(pe, t)
                    if x >= 2:
                        pe.wait_ge(s["rqp_taken"], NSUB * g + x - 1)
                    for k in range(KD):
                        last = pe.matmul(PS[:, 4 + x % 2, 0:tokens], W[t % 2][:, k, P * (x % 4):P * (x % 4) + P],
                                         XT[:, k, first:first + tokens], start=(k == 0), stop=(k == KD - 1))
                    last.then_inc(s["rqp_ready"], 1)
                    if x >= 1:
                        router_scores(x - 1)
                router_scores(NSUB - 1)

            def open_group(bank, r):
                for i in range(2):
                    last = pe.matmul(PS[0:r, bank + i, :], zeros[:, 0:r], const("decayT"), start=True, stop=False, skip_group_check=True)
                return last

            for blk in range(1, NBLK):
                bank = 2 * (blk % 2)
                if blk > 2:
                    pe.wait_ge(s["y_ready"], blk - 2)
                else:
                    pe.wait_ge(s["rs_taken"], 2 * NSUB)
                    pe.wait_ge(s["smp_scores_taken"], NSUB)
                open_group(bank, P)
                with pe.Fori(0, NCH) as c:
                    for k in range(CHUNK):
                        pe.wait_ge(uv_in[1][k], c * 16 + 16 * (NCH * blk + 1))
                        pe.wait_ge(s["diag_ready"], c * CHUNK + (CHUNK * NCH * (blk - 1) + k + 1))
                        for i in range(2):
                            last = pe.matmul(PS[:, bank + i, :], DIAG[k], VSLOT[k][:, 512 * i:512 * i + 512], start=False,
                                             stop=False, skip_group_check=True)
                        last.then_inc(s["v_used"], 1)

            pe.wait_ge(s["sel_ready"], NB - 1)
            pe.transpose(PS[:, 4, 0:DB], sidx_row[0:DB, :], ident[0:DB, 0:DB])
            pe.transpose(PS[:, 4, P:P + DB], GATE[0:DB, SMP, :], ident[0:DB, 0:DB]).then_inc(s["sidx_turned"], 1)
            pe.wait_ge(s["sel_ready"], NB)
            for b in range(DB):
                if b >= 2:
                    pe.wait_ge(s["u_used"], CHUNK * (NCH * NBLK + 1) + b - 1)
                for i in range(2):
                    last = pe.matmul(PS[:, 4 + 2 * (b % 2) + i, :], sel[0:DB, b, :], QR[0:DB, SMP, 512 * i:512 * i + 512],
                                     start=True, stop=True)
                last.then_inc(s["xb_ready"], 1)
            pe.wait_ge(s["u_used"], CHUNK * (NCH * NBLK + 2))
            open_group(6, DB)
            pe.wait_ge(s["smp_w"], 1)
            for b in range(DB):
                pe.wait_ge(uv_in[1][b], 16 * (NCH * NBLK + 1))
                for i in range(2):
                    last = pe.matmul(PS[0:DB, 6 + i, :], SWM[:, b, :], VSLOT[b][:, 512 * i:512 * i + 512], start=False,
                                     stop=(b == DB - 1), skip_group_check=True)
                last.then_inc(s["v_used"], 1)


_INS = ["x_prompt", "x_sample", "mem_prompt", "cache_diff_k", "cache_diff_v", "page_table", "state_ret", "cache_mem_k",
        "cache_mem_v", "g_mix", "w_in", "w_out", "lam_q1", "lam_k1", "lam_q2", "lam_k2", "rel_bias", "g_cross", "g_mem",
        "w_mq", "w_mk", "w_mv", "w_mo", "g_ffn", "w_pq", "sub_keys", "peer_u", "peer_v", "g_final"]
_OUTS = [(1, SEQ, D), (DB, 1, D), (1, 1, SEQ, H, 2, DH), (1, 1, SEQ, H, 2 * DH), (1, 1, H, P, P), (1, 1, MEM, H, MDH),
         (1, 1, MEM, H, MDH), (1, DB, 1, H, 2, DH), (1, DB, 1, H, 2 * DH), (1, DB, H, P, P)]


def kernel(**inputs):
    import concourse.bacc as bacc
    from concourse.bass_utils import run_bass_kernel_spmd as run

    nc = bacc.Bacc("TRN2", target_bir_lowering=False, num_devices=1)
    arrays, args = {}, []
    for name in _INS:
        a = np.ascontiguousarray(inputs[name])
        arrays[f"in_{name}"] = a
        args.append(nc.dram_tensor(f"in_{name}", a.shape, mybir.dt.from_np(a.dtype), kind="ExternalInput").ap())
    arrays["in_consts"] = shape_constants()
    args.append(nc.dram_tensor("in_consts", (P, CW), F32, kind="ExternalInput").ap())
    args.append(nc.dram_tensor("bias_lines", (H * P * TL,), F32, kind="Internal").ap())
    for i, shape in enumerate(_OUTS):
        args.append(nc.dram_tensor(f"out_{i}", shape, F32, kind="ExternalOutput").ap())
    build(nc, *args)
    r = run(nc, [arrays], core_ids=[0])
    return tuple(r.results[0][f"out_{i}"] for i in range(len(_OUTS)))
```
